# Optimizing a Trainium2 kernel written in Bass

```python
import jax, jax.numpy as jnp
from jax import lax
import numpy as np

D_MODEL = 2048
BATCH = 1
SEQ = 512
DEPTH = 1

RET_HEADS = 4
RET_DK = 256
RET_DV = 256
RET_WIDTH = RET_HEADS * RET_DV
GDN_HEADS = 8
GDN_DK = 128
GDN_DV = 128
GDN_WIDTH = GDN_HEADS * GDN_DV
D_MIX = RET_WIDTH + GDN_WIDTH
CONV_K = 4
GDN_CONV_CH = 2 * GDN_HEADS * GDN_DK + GDN_WIDTH
RET_CHUNK = 128
GDN_CHUNK = 64
ROPE_BASE = 10000.0
EPS = 1e-6
IN_SIZES = (RET_HEADS * RET_DK, RET_HEADS * RET_DK, RET_WIDTH, RET_WIDTH,
            GDN_HEADS * GDN_DK, GDN_HEADS * GDN_DK, GDN_WIDTH, GDN_WIDTH,
            GDN_HEADS, GDN_HEADS)
D_IN = sum(IN_SIZES)

kernel_name = 'hymba_retention_gated_deltanet_block'

def _split_points():
    pts, acc = [], 0
    for s in IN_SIZES[:-1]:
        acc += s
        pts.append(acc)
    return pts

def rms_norm(x, w=None):
    xf = x.astype(jnp.float32)
    y = xf * lax.rsqrt(jnp.mean(xf * xf, axis=-1, keepdims=True) + EPS)
    if w is not None:
        y = y * w.astype(jnp.float32)
    return y

def rotary(t, positions):
    d = t.shape[-1]
    inv_freq = 1.0 / (ROPE_BASE ** (jnp.arange(0, d, 2, dtype=jnp.float32) / d))
    ang = positions.astype(jnp.float32)[..., None] * inv_freq
    cos = jnp.cos(ang)[:, :, None, :]
    sin = jnp.sin(ang)[:, :, None, :]
    t1, t2 = t[..., : d // 2], t[..., d // 2:]
    return jnp.concatenate([t1 * cos - t2 * sin, t1 * sin + t2 * cos], axis=-1)

def causal_dwconv(x, w):
    k = w.shape[0]
    return lax.conv_general_dilated(
        x, w[:, None, :], window_strides=(1,), padding=[(k - 1, 0)],
        dimension_numbers=('NWC', 'WIO', 'NWC'), feature_group_count=x.shape[-1])

def multiscale_retention(q, k, v, positions):
    b, s, h, dk = q.shape
    dv = v.shape[-1]
    c = RET_CHUNK
    n = s // c
    q = rotary(q, positions)
    k = rotary(k, positions) * (dk ** -0.5)
    log_gamma = jnp.log1p(-jnp.exp2(-5.0 - jnp.arange(h, dtype=jnp.float32)))
    i = jnp.arange(c, dtype=jnp.float32)
    rel = i[:, None] - i[None, :]
    intra_decay = jnp.where(rel >= 0, jnp.exp(log_gamma[:, None, None] * jnp.maximum(rel, 0.0)), 0.0)
    q_decay = jnp.exp(log_gamma[None, :] * (i[:, None] + 1.0))
    k_decay = jnp.exp(log_gamma[None, :] * (c - 1.0 - i[:, None]))
    chunk_decay = jnp.exp(log_gamma * c)
    qc = q.reshape(b, n, c, h, dk)
    kc = k.reshape(b, n, c, h, dk)
    vc = v.reshape(b, n, c, h, dv)
    scores = jnp.einsum('bnihd,bnjhd->bnhij', qc, kc) * intra_decay
    o_intra = jnp.einsum('bnhij,bnjhe->bnihe', scores, vc)
    kv = jnp.einsum('bnjhd,bnjhe->nbhde', kc * k_decay[:, :, None], vc)

    def step(state, kv_n):
        return state * chunk_decay[None, :, None, None] + kv_n, state

    _, state_prev = lax.scan(step, jnp.zeros((b, h, dk, dv), jnp.float32), kv)
    o_inter = jnp.einsum('bnihd,nbhde->bnihe', qc * q_decay[:, :, None], state_prev)
    return (o_intra + o_inter).reshape(b, s, h, dv)

def chunk_gated_delta_rule(q, k, v, beta, g):
    b, s, h, dk = q.shape
    dv = v.shape[-1]
    c = GDN_CHUNK
    n = s // c
    q = q * (dk ** -0.5)

    def chunks(t):
        return t.reshape(b, n, c, h, -1).transpose(0, 3, 1, 2, 4)

    qc, kc, vc = chunks(q), chunks(k), chunks(v)
    bc = beta.reshape(b, n, c, h).transpose(0, 3, 1, 2)
    gc = jnp.cumsum(g.reshape(b, n, c, h).transpose(0, 3, 1, 2), axis=-1)
    causal = jnp.tril(jnp.ones((c, c), dtype=bool))
    strict = jnp.tril(jnp.ones((c, c), dtype=bool), -1)
    diff = gc[..., :, None] - gc[..., None, :]
    decay = jnp.where(causal, jnp.exp(jnp.where(causal, diff, 0.0)), 0.0)
    kb = kc * bc[..., None]
    lower = jnp.where(strict, jnp.einsum('bhnid,bhnjd->bhnij', kb, kc) * decay, 0.0)
    rhs = jnp.concatenate([vc * bc[..., None], kb * jnp.exp(gc)[..., None]], axis=-1)
    sol = lax.linalg.triangular_solve(lower, rhs, left_side=True, lower=True, unit_diagonal=True)
    u, w = sol[..., :dv], sol[..., dv:]
    attn = jnp.einsum('bhnid,bhnjd->bhnij', qc, kc) * decay
    q_g = qc * jnp.exp(gc)[..., None]
    g_last = gc[..., -1]
    k_tail = kc * jnp.exp(g_last[..., None] - gc)[..., None]
    xs = (jnp.moveaxis(u, 2, 0), jnp.moveaxis(w, 2, 0), jnp.moveaxis(attn, 2, 0),
          jnp.moveaxis(q_g, 2, 0), jnp.moveaxis(k_tail, 2, 0), jnp.moveaxis(g_last, 2, 0))

    def step(state, inp):
        u_n, w_n, attn_n, qg_n, kt_n, gl_n = inp
        v_new = u_n - jnp.einsum('bhcd,bhde->bhce', w_n, state)
        o_n = jnp.einsum('bhcd,bhde->bhce', qg_n, state) + jnp.einsum('bhij,bhje->bhie', attn_n, v_new)
        state = state * jnp.exp(gl_n)[..., None, None] + jnp.einsum('bhcd,bhce->bhde', kt_n, v_new)
        return state, o_n

    _, o = lax.scan(step, jnp.zeros((b, h, dk, dv), jnp.float32), xs)
    return o.transpose(1, 0, 3, 2, 4).reshape(b, s, h, dv)

def hybrid_layer(h, positions, norm_w, w_in, conv_w, a_log, dt_bias, gdn_norm_w, w_out):
    b, s, _ = h.shape
    xn = rms_norm(h, norm_w).astype(h.dtype)
    proj = (xn @ w_in).astype(jnp.float32)
    rq, rk, rv, rg, gq, gk, gv, gg, gb, ga = jnp.split(proj, _split_points(), axis=-1)

    o_ret = multiscale_retention(rq.reshape(b, s, RET_HEADS, RET_DK), rk.reshape(b, s, RET_HEADS, RET_DK),
                                 rv.reshape(b, s, RET_HEADS, RET_DV), positions)
    o_ret = rms_norm(o_ret).reshape(b, s, RET_WIDTH) * jax.nn.silu(rg)

    qkv = jax.nn.silu(causal_dwconv(jnp.concatenate([gq, gk, gv], axis=-1), conv_w.astype(jnp.float32)))
    cq, ck, cv = jnp.split(qkv, [GDN_HEADS * GDN_DK, 2 * GDN_HEADS * GDN_DK], axis=-1)
    cq = rms_norm(cq.reshape(b, s, GDN_HEADS, GDN_DK)) * (GDN_DK ** -0.5)
    ck = rms_norm(ck.reshape(b, s, GDN_HEADS, GDN_DK)) * (GDN_DK ** -0.5)
    beta = jax.nn.sigmoid(gb)
    g = -jnp.exp(a_log.astype(jnp.float32)) * jax.nn.softplus(ga + dt_bias.astype(jnp.float32))
    o_gdn = chunk_gated_delta_rule(cq, ck, cv.reshape(b, s, GDN_HEADS, GDN_DV), beta, g)
    o_gdn = (rms_norm(o_gdn, gdn_norm_w) * jax.nn.silu(gg.reshape(b, s, GDN_HEADS, GDN_DV))).reshape(b, s, GDN_WIDTH)

    mix = jnp.concatenate([o_ret, o_gdn], axis=-1).astype(h.dtype)
    return h + mix @ w_out

def setup_inputs(seed: int = 0) -> dict:
    key = jax.random.key(seed)
    ks = jax.random.split(key, 10)
    x = jax.random.normal(ks[0], (BATCH, SEQ, D_MODEL), jnp.float32)
    offset = jax.random.randint(ks[1], (BATCH, 1), 0, SEQ, dtype=jnp.int32)
    positions = jnp.arange(SEQ, dtype=jnp.int32)[None, :] + offset
    norm_w = 1.0 + 0.02 * jax.random.normal(ks[2], (DEPTH, D_MODEL), jnp.float32)
    w_in = jax.random.normal(ks[3], (DEPTH, D_MODEL, D_IN), jnp.float32) * (D_MODEL ** -0.5)
    conv_w = jax.random.normal(ks[4], (DEPTH, CONV_K, GDN_CONV_CH), jnp.float32) * (CONV_K ** -0.5)
    a_log = jnp.log(jax.random.uniform(ks[5], (DEPTH, GDN_HEADS), jnp.float32, 1.0, 16.0))
    dt = jnp.exp(jax.random.uniform(ks[6], (DEPTH, GDN_HEADS), jnp.float32, np.log(1e-3), np.log(1e-1)))
    dt_bias = dt + jnp.log(-jnp.expm1(-dt))
    gdn_norm_w = 1.0 + 0.02 * jax.random.normal(ks[7], (DEPTH, GDN_DV), jnp.float32)
    w_out = jax.random.normal(ks[8], (DEPTH, D_MIX, D_MODEL), jnp.float32) * (D_MIX ** -0.5)
    final_norm_w = 1.0 + 0.02 * jax.random.normal(ks[9], (D_MODEL,), jnp.float32)
    return {'x': x, 'positions': positions, 'norm_w': norm_w, 'w_in': w_in, 'conv_w': conv_w,
            'a_log': a_log, 'dt_bias': dt_bias, 'gdn_norm_w': gdn_norm_w, 'w_out': w_out,
            'final_norm_w': final_norm_w}

def reference(x, positions, norm_w, w_in, conv_w, a_log, dt_bias, gdn_norm_w, w_out, final_norm_w):
    h = x
    for layer in range(DEPTH):
        h = hybrid_layer(h, positions, norm_w[layer], w_in[layer], conv_w[layer], a_log[layer],
                         dt_bias[layer], gdn_norm_w[layer], w_out[layer])
    return rms_norm(h, final_norm_w).astype(x.dtype)


_drawn_inputs = setup_inputs


def setup_inputs(seed=0):
    import zlib

    import numpy as np

    out = dict(_drawn_inputs(seed))
    spreads = {}
    factors = {'norm_w': 2.901, 'gdn_norm_w': 7.745, 'final_norm_w': 2.785}
    for name, (base, spread) in spreads.items():
        noise = np.random.default_rng([zlib.crc32(name.encode()), seed]).standard_normal(out[name].shape)
        drawn = base * np.exp(spread * noise) if base else spread * noise
        out[name] = __import__('jax').numpy.asarray(drawn.astype(out[name].dtype))
    for name, factor in factors.items():
        out[name] = (out[name] * factor).astype(out[name].dtype)
    return out
```

```python
import math
from contextlib import ExitStack

import numpy as np
import concourse.bass as bass
from concourse import mybir

F32 = mybir.dt.float32
F32R = mybir.dt.float32r
I32 = mybir.dt.int32
ALU = mybir.AluOpType
ACT = mybir.ActivationFunctionType
AX = mybir.AxisListType

P = 128
SEQ = 512
D = 2048
KT = D // P
NT = SEQ // P
GH, RH = 8, 4
RDK = 256
GROUP = 1024
GDN_COL = 4 * GROUP
GATE_COL = 8 * GROUP
EPS = 1e-6
PIECE = 512
UNIT_MM = 3 * KT
N_GDN_UNITS = 4 * GH
N_RET_UNITS = 8 * RH
OUT_U = N_GDN_UNITS + N_RET_UNITS
LEVELS = 7
NP = 20

(W_KTOK, W_QTOK, W_QGTOK, W_VTOK, W_KT, W_QT, W_QGT, W_Y0, W_Y1, W_X, W_XT, W_T1, W_KBG, W_KTAIL,
 W_VN, W_S, W_GATE) = range(17)

DVE_GDN_LINKS = 14
DVE_RET_LINKS = 2


class Links:

    def __init__(self, eng, sem, base=0):
        self.eng, self.sem, self.base, self.n = eng, sem, base, 0

    def __call__(self, instruction):
        instruction.then_inc(self.sem, 1)
        self.n += 1
        self.eng.wait_ge(self.sem, self.base + self.n)


def build(nc, x, positions, norm_w, w_in, conv_w, a_log, dt_bias, gdn_norm_w, w_out, final_norm_w,
          consts, decays, out):
    with ExitStack() as ctx:
        def sb(name, shape, dt=F32):
            return ctx.enter_context(nc.sbuf_tensor(name, shape, dt))

        def sem(name):
            return ctx.enter_context(nc.semaphore(name))

        act_hi = sb("act_hi", [P, KT, SEQ], F32R)
        act_lo = sb("act_lo", [P, KT, SEQ], F32R)
        w_raw = sb("w_raw", [P, 2, KT * P])
        w_hi = sb("w_hi", [P, 2, KT * P], F32R)
        w_lo = sb("w_lo", [P, 2, KT * P], F32R)
        mix = sb("mix", [P, KT, SEQ])
        work1 = sb("work1", [P, 6, SEQ])
        work2 = sb("work2", [P, 17, SEQ])
        cst = sb("cst", [P, P + P + LEVELS * P + 1])
        ones = sb("ones", [P, P])
        rope_cos = sb("rope_cos", [P, SEQ])
        rope_sin = sb("rope_sin", [P, SEQ])
        rows = sb("rows", [P, P])
        cols = sb("cols", [P, P])
        wg_hi = sb("wg_hi", [P, KT, 16], F32R)
        wg_lo = sb("wg_lo", [P, KT, 16], F32R)
        head_par = sb("head_par", [P, GH, NP])
        par = sb("par", [P, NP])
        conv_par = sb("conv_par", [P, 4, 3])
        g_log = sb("g_log", [P, GH, NT])
        g_cum = sb("g_cum", [P, GH, NT])
        small = sb("small", [P, 6, GH * NT])
        a_row = sb("a_row", [P, GH])
        dt_row = sb("dt_row", [P, GH])
        stat = sb("stat", [P, 4, 16])
        half = sb("half", [P, 16])
        ps = ctx.enter_context(nc.psum_tensor("ps", [P, 8, SEQ], F32))

        ident = cst[:, 0:P]
        causal = cst[:, P:2 * P]
        inv_freq = cst[:, 2 * P + LEVELS * P:]

        def level_mask(n):
            return cst[:, (2 + n) * P:(3 + n) * P]

        def tiles(ap):
            return ap.rearrange("p (t c) -> p t c", t=NT)

        def bank(b):
            return ps[:, b, :]

        def over_free(col, n=P):
            return col.unsqueeze(2).to_broadcast([P, col.shape[1], n])

        def over_tiles(mat, n=NT):
            return mat.unsqueeze(1).to_broadcast([P, n, mat.shape[1]])

        wk = lambda i: work2[:, i, :]
        conv = work1
        half_cols = half[:, 0:8]
        x_tok = mix[:, :, :].rearrange("p (t a) c -> p t (a c)", t=NT)
        ktok, qtok, qgtok, vtok = wk(W_KTOK), wk(W_QTOK), wk(W_QGTOK), wk(W_VTOK)
        kT, qT, qgT = wk(W_KT), wk(W_QT), wk(W_QGT)
        lower_t, attn_t, w_t = wk(W_QTOK), wk(W_QGTOK), wk(W_QTOK)
        ys = [wk(W_Y0), wk(W_Y1)]
        inv, inv_t, t1, o_n = wk(W_X), wk(W_XT), wk(W_T1), wk(W_T1)
        kbg, ktail, vnew = wk(W_KBG), wk(W_KTAIL), wk(W_VN)
        state = [wk(W_S)[:, i * P:(i + 1) * P] for i in range(3)]
        gate = wk(W_GATE)
        q_rot, k_rot, rot_tmp = work1[:, 0:2, :], work1[:, 2:4, :], work1[:, 4:6, :]
        v_feat = work2[:, 0:2, :]
        rv_tok = work2[:, 2:4, :].rearrange("p a c -> p (a c)").rearrange("p (j d) -> p j d", j=NT)
        rgate = work2[:, 4:6, :]
        s_off = [0, 512, 896, 1152]
        s_all = work2[:, 6:9, :].rearrange("p a c -> p (a c)")
        ro_n = work2[:, 9:11, :].rearrange("p a c -> p (a c)").rearrange("p (j d) -> p j d", j=NT)
        ro_sq = work2[:, 11:13, :]
        h_tok = work2[:, 0:16, :].rearrange("p a c -> p (a c)").rearrange("p (t n) -> p t n", t=NT)
        fin_w = work1[:, 0:4, :].rearrange("p a c -> p (a c)")

        w_in_k = w_in.rearrange("(k p) c -> p k c", p=P)
        w_out_k = w_out.rearrange("(k p) c -> p k c", p=P)
        x_rows = x.rearrange("(t p) c -> p t c", p=P)
        out_rows = out.rearrange("(t p) c -> p t c", p=P)

        s_x = [sem(f"x_loaded{t}") for t in range(NT)]
        s_xres = [sem(f"x_again_loaded{n}") for n in range(4)]
        s_w = [sem(f"w_loaded{i}") for i in range(2)]
        s_cst, s_rows, s_wg, s_pos, s_arow, s_dec, s_fin = (
            sem(n) for n in ("cst_loaded", "rows_loaded", "wg_loaded", "pos_loaded", "a_dt_loaded",
                             "decays_loaded", "final_w_loaded"))
        s_out = sem("out_stored")
        hi_ready, lo_ready, proj_done = sem("w_hi_ready"), sem("w_lo_ready"), sem("unit_projected")
        memsets, cols_mm, cols_ready = sem("memsets"), sem("cols_turned"), sem("cols_ready")
        x_sq, x_ms, x_rstd, x_scaled = sem("x_squared"), sem("x_mean"), sem("x_rstd"), sem("x_scaled")
        xt_mm, xhi_ready, xlo_ready = sem("x_turned"), sem("x_hi_ready"), sem("x_lo_ready")
        wg_hi_ready, wg_lo_ready, gates_mm = sem("wg_hi"), sem("wg_lo"), sem("gates_projected")
        p_dve, p_act, p_mm, p_ready = sem("par_dve"), sem("par_act"), sem("cumsum_mm"), sem("par_ready")
        ug_ready, g_mm, dif_ready, dif_exp, decay_ready = (
            sem(n) for n in ("ug_ready", "decay_mm", "decay_log_ready", "decay_exp", "decay_ready"))
        dt_added = sem("dt_added")
        rope_arg, rope_ready = sem("rope_arg"), sem("rope_ready")
        dve_link = sem("dve_link")
        dve_link_gdn, dve_link_ret = sem("dve_link_gdn"), sem("dve_link_ret")
        par_ready, conv_par_ready = sem("head_par_ready"), sem("conv_par_ready")
        tap_done, conv_done, silu_done, gate_done = (
            sem(n) for n in ("tap_done", "conv_done", "silu_done", "gate_done"))
        tr_in, qk_sq, v_ready, ss_ready, r_ready, rqg_ready, tok_ready = (
            sem(n) for n in ("tr_in", "qk_squared", "v_ready", "ss_ready", "r_ready", "rqg_ready",
                             "tok_ready"))
        kk_ready, tr_back, t_ready, kk_mm, low_ready = (
            sem(n) for n in ("k_scaled_ready", "tr_back", "t_ready", "kk_mm", "lower_ready"))
        y_ready, inv_first, t1_mm, t1_ready, lvl_mm, lvl_ready = (
            sem(n) for n in ("y_ready", "inv_first", "t1_mm", "t1_ready", "level_mm", "level_ready"))
        uw_mm, w_ready, u_ready = sem("uw_mm"), sem("w_ready"), sem("u_ready")
        ws_mm, vn_ready, ktv_mm, st_ready, o_mm = (
            sem(n) for n in ("ws_mm", "vnew_ready", "ktv_mm", "state_ready", "o_mm"))
        o_sq, o_ms, o_rstd, on_ready, otr_mm, mix_done = (
            sem(n) for n in ("o_squared", "o_mean", "o_rstd", "o_normed", "o_turned", "mix_done"))
        rot_read, rot_done, rs_mm, rs_ready, vf_done, rgate_done, rvt_mm, rvt_ready = (
            sem(n) for n in ("rot_read", "rot_done", "ret_scores_mm", "ret_scores_ready", "v_feat_done",
                             "ret_gate_done", "ret_v_turned", "ret_v_ready"))
        ro_mm, ro_sqd, ro_ms, ro_rstd, ron_ready, rotr_mm, rmix_done = (
            sem(n) for n in ("ret_o_mm", "ret_o_squared", "ret_o_mean", "ret_o_rstd", "ret_o_normed",
                             "ret_o_turned", "ret_mix_done"))
        mhi_ready, mlo_ready, oproj_mm, h_ready, h_sq, h_ms, h_rstd, y_done = (
            sem(n) for n in ("mix_hi_ready", "mix_lo_ready", "out_projected", "h_ready", "h_squared",
                             "h_mean", "h_rstd", "y_done"))

        block = ctx.enter_context(nc.Block())

        @block.sync
        def _(sp):
            for t in range(NT):
                sp.dma_start(x_tok[:, t, :], x_rows[:, t, :]).then_inc(s_x[t], 16)

            def load_in(slot, col, wait):
                if wait is not None:
                    sp.wait_ge(lo_ready, wait)
                sp.dma_start(w_raw[:, slot, :].rearrange("p (k c) -> p k c", k=KT),
                             w_in_k[:, :, bass.ds(col, P)]).then_inc(s_w[slot], 16)

            for s in range(4):
                if s == 2:
                    sp.wait_ge(xt_mm, KT)
                    for r in range(RH):
                        sp.dma_start(mix[:, GH + 2 * r, :], decays[r, :, :]).then_inc(s_dec, 16)
                load_in(s % 2, GDN_COL + GROUP * s, None if s < 2 else 4 * s - 4)
            with sp.Fori(1, GH) as h:
                for s in range(4):
                    load_in(s % 2, GDN_COL + GROUP * s + h * P, 16 * h + 4 * s - 4)
            with sp.Fori(0, RH) as r:
                for i in range(8):
                    load_in(i % 2, GROUP * (i // 2) + P * (i % 2) + r * (2 * P),
                            32 * r + 4 * N_GDN_UNITS + 4 * i - 4)

            def load_out(n, kg, after=None):
                first = GH + 4 * kg if kg < 2 else 4 * (kg - 2)
                col = n * SEQ if after is None else after * SEQ + SEQ
                sp.wait_ge(lo_ready, 16 * n + 4 * OUT_U + 4 * kg - 4)
                sp.dma_start(w_raw[:, kg % 2, :].rearrange("p (k c) -> p k c", k=4),
                             w_out_k[:, first:first + 4, bass.ds(col, SEQ)]).then_inc(s_w[kg % 2], 16)

            for kg in range(4):
                load_out(0, kg)
            sp.wait_ge(rmix_done, 2 * RH + 1)
            for n in range(4):
                sp.dma_start(h_tok[:, :, n * SEQ:(n + 1) * SEQ],
                             x_rows[:, :, n * SEQ:(n + 1) * SEQ]).then_inc(s_xres[n], 16)
            sp.dma_start(fin_w, final_norm_w.partition_broadcast(P)).then_inc(s_fin, 16)
            with sp.Fori(0, 3) as before:
                for kg in range(4):
                    load_out(before + 1, kg, before)
            for t in range(NT):
                sp.wait_ge(y_done, t + 1)
                sp.dma_start(out_rows[:, t, :], h_tok[:, t, :]).then_inc(s_out, 16)
            sp.wait_ge(s_out, 16 * NT)

        @block.tensor
        def _(pe):
            mm = pe.matmul

            class Unit:

                def __init__(self, first, bank_free):
                    self.first, self.bank_free, self.m = first, bank_free, 0

                def fill(self, n):
                    for _ in range(n):
                        i, m = divmod(self.m, UNIT_MM)
                        kt, pas = divmod(m, 3)
                        slot = i % 2
                        if m == 0:
                            self.bank_free(i)
                        if m % 12 == 0:
                            pe.wait_ge(lo_ready, self.first * 4 + (4 * i + m // 12 + 1))
                        w = (w_hi, w_hi, w_lo)[pas][:, slot, kt * P:(kt + 1) * P]
                        a = (act_hi, act_lo, act_hi)[pas][:, kt, :]
                        op = mm(bank(slot), w, a, start=m == 0, stop=m == UNIT_MM - 1)
                        if m == UNIT_MM - 1:
                            op.then_inc(proj_done, 1)
                        self.m += 1

            pe.wait_ge(s_cst, 16)
            pe.wait_ge(s_rows, 48)
            pe.transpose(bank(7)[:, 0:113], rows[0:113, :], ident[0:113, 0:113]).then_inc(cols_mm, 1)

            pe.wait_ge(x_scaled, NT)

            def turn_x(kt):
                if kt >= 5:
                    pe.wait_ge(xlo_ready, kt - 4)
                for t in range(NT):
                    op = pe.transpose(tiles(bank(2 + kt % 5))[:, t, :], x_tok[:, t, kt * P:(kt + 1) * P],
                                      ident)
                op.then_inc(xt_mm, 1)

            head0 = Unit(0, lambda i: None)
            for kt in range(3):
                turn_x(kt)
            for kt in range(KT):
                if kt + 3 < KT:
                    turn_x(kt + 3)
                pe.wait_ge(xlo_ready, kt + 1)
                head0.fill(3)

            pe.wait_ge(wg_lo_ready, 1)
            for t in range(NT):
                for kt in range(KT):
                    for a, w in ((act_hi, wg_hi), (act_hi, wg_lo), (act_lo, wg_hi)):
                        first = kt == 0 and w is wg_hi and a is act_hi
                        op = mm(bank(2)[:, 16 * t:16 * t + 16], a[:, kt, t * P:(t + 1) * P], w[:, kt, :],
                                start=first, stop=kt == KT - 1 and a is act_lo)
            op.then_inc(gates_mm, 1)

            def head0_bank(i):
                if i >= 2:
                    pe.wait_ge(conv_done, i - 1)

            head0.bank_free = head0_bank
            head0.fill(UNIT_MM)
            pe.wait_ge(p_dve, 1)
            g_all = g_log[:, :, :].rearrange("p h t -> p (h t)")
            mm(bank(3)[:, 0:GH * NT], causal, g_all, start=True, stop=True)
            mm(bank(3)[:, GH * NT:2 * GH * NT], ones[:, :], g_all, start=True, stop=True).then_inc(p_mm, 1)
            for e in range(GH):
                pe.wait_ge(ug_ready, e + 1)
                if e >= 2:
                    pe.wait_ge(dif_ready, e - 1)
                mm(bank(4 + e % 2), ones[:, :], ys[e % 2], start=True, stop=True).then_inc(g_mm, 1)
                head0.fill(2 * UNIT_MM // GH)

            def gdn_head(h, unit, per):
                fill = unit.fill
                for s in range(3):
                    pe.wait_ge(silu_done, 3 * h + (s + 1))
                    for t in range(NT):
                        op = pe.transpose(tiles(bank(2 + s))[:, t, :], conv[:, s, t * P:(t + 1) * P], ident)
                    op.then_inc(tr_in, 1)
                fill(4 * per)
                for s, src in enumerate((ktok, qtok, qgtok)):
                    pe.wait_ge(tok_ready, 3 * h + (s + 1))
                    for t in range(NT):
                        op = pe.transpose(tiles(bank(5 + s))[:, t, :], tiles(src)[:, t, :], ident)
                    op.then_inc(tr_back, 1)
                fill(per)
                pe.wait_ge(t_ready, 3 * h + 2)
                for b, rhs in ((2, kT), (3, qT)):
                    for t in range(NT):
                        op = mm(tiles(bank(b))[:, t, :], tiles(kT)[:, t, :], tiles(rhs)[:, t, :],
                                start=True, stop=True)
                    op.then_inc(kk_mm, 1)
                fill(2 * per)
                for n in range(1, LEVELS):
                    pe.wait_ge(y_ready, 7 * h + (n + 1))
                    if n == 1:
                        pe.wait_ge(inv_first, h + 1)
                    else:
                        pe.wait_ge(lvl_ready, 7 * h + (n - 1 if n < 6 else 6))
                    for t in range(NT):
                        op = mm(tiles(bank(4))[:, t, :], tiles(ys[n % 2])[:, t, :], tiles(inv)[:, t, :],
                                start=True, stop=True)
                    op.then_inc(t1_mm, 1)
                    fill(per)
                    pe.wait_ge(t1_ready, 6 * h + n)
                    if n == 6:
                        pe.wait_ge(lvl_ready, 7 * h + 6)
                    if n < 6:
                        if n == 1:
                            pe.wait_ge(t_ready, 3 * h + 3)
                        for t in range(NT):
                            op = mm(tiles(bank(5))[:, t, :], tiles(inv_t)[:, t, :], tiles(t1)[:, t, :],
                                    start=True, stop=True)
                        op.then_inc(lvl_mm, 1)
                    if n >= 5:
                        for t in range(NT):
                            op = mm(tiles(bank(6))[:, t, :], tiles(t1)[:, t, :], tiles(inv_t)[:, t, :],
                                    start=True, stop=True)
                        op.then_inc(lvl_mm, 1)
                    fill(per)
                pe.wait_ge(lvl_ready, 7 * h + 7)
                pe.wait_ge(v_ready, h + 1)
                pe.wait_ge(kk_ready, 2 * h + 2)
                for t in range(NT):
                    op = mm(tiles(bank(2))[:, t, :], tiles(inv_t)[:, t, :], tiles(vtok)[:, t, :],
                            start=True, stop=True)
                op.then_inc(uw_mm, 1)
                for t in range(NT):
                    op = mm(tiles(bank(6))[:, t, :], tiles(kbg)[:, t, :], tiles(inv_t)[:, t, :],
                            start=True, stop=True)
                op.then_inc(uw_mm, 1)
                fill(per)
                for t in range(NT):
                    tt = slice(t * P, (t + 1) * P)
                    if t > 0:
                        pe.wait_ge(st_ready, 3 * h + t)
                        if t == 1:
                            pe.wait_ge(w_ready, h + 1)
                        mm(bank(4)[:, tt], w_t[:, tt], state[t - 1], start=True, stop=True).then_inc(ws_mm, 1)
                        mm(bank(7)[:, tt], qgT[:, tt], state[t - 1], start=True, stop=False)
                        fill(per)
                    pe.wait_ge(vn_ready, 4 * h + (t + 1))
                    if t < NT - 1:
                        mm(bank(5)[:, tt], ktail[:, tt], vnew[:, tt], start=True, stop=True).then_inc(ktv_mm, 1)
                    if t == 0:
                        pe.wait_ge(low_ready, 2 * h + 2)
                    op = mm(bank(7)[:, tt], attn_t[:, tt], vnew[:, tt], start=t == 0, stop=True)
                    if t == NT - 1:
                        op.then_inc(o_mm, 1)
                    fill(per)

            def gdn_body(h, unit):
                gdn_head(h, unit, 6)
                pe.wait_ge(on_ready, h + 1)
                for t in range(NT):
                    op = pe.transpose(tiles(bank(6))[:, t, :], tiles(o_n)[:, t, :], ident)
                op.then_inc(otr_mm, 1)
                unit.fill(4 * UNIT_MM - unit.m)

            def gdn_bank(h):
                def free(i):
                    if i == 1:
                        pe.wait_ge(gate_done, h + 1)
                    else:
                        pe.wait_ge(conv_done, 3 * h + (3, 0, 4, 5)[i])
                return free

            def ret_bank(r):
                def free(i):
                    if i < 2:
                        if isinstance(r, int) and r == 0:
                            pe.wait_ge(*((conv_done, 3 * GH), (gate_done, GH))[i])
                        else:
                            pe.wait_ge(rgate_done, 2 * r + (i - 1))
                    elif i < 6:
                        pe.wait_ge(rot_read, 4 * r + (i - 1))
                    else:
                        pe.wait_ge(vf_done, 2 * r + (i - 5))
                return free

            with pe.Fori(0, GH - 1) as h:
                gdn_body(h, Unit(4 * h + 4, gdn_bank(h)))
            gdn_body(GH - 1, Unit(N_GDN_UNITS, ret_bank(0)))

            def ret_scores(r, unit):
                for j in range(NT):
                    if j == 0:
                        pe.wait_ge(rot_done, 4 * r + 4)
                        pe.wait_ge(rmix_done, 2 * r + 1)
                    n = SEQ - j * P
                    for d in range(2):
                        op = mm(bank(4 + j)[:, 0:n], k_rot[:, d, j * P:(j + 1) * P], q_rot[:, d, j * P:],
                                start=d == 0, stop=d == 1)
                    op.then_inc(rs_mm, 1)
                    unit.fill(24)
                for d in range(2):
                    pe.wait_ge(vf_done, 2 * r + (d + 1))
                    if d == 0:
                        pe.wait_ge(rs_ready, 4 * r + 2)
                    for j in range(NT):
                        op = pe.transpose(bank(4 + j // 2)[:, (j % 2) * RDK + d * P:(j % 2) * RDK + (d + 1) * P],
                                          v_feat[:, d, j * P:(j + 1) * P], ident)
                op.then_inc(rvt_mm, 1)
                unit.fill(8 * UNIT_MM - unit.m)

            def ret_out(r, fill):
                pe.wait_ge(rs_ready, 4 * r + 4)
                pe.wait_ge(rvt_ready, 2 * r + 2)
                for i in range(NT):
                    for j in range(i + 1):
                        at = s_off[j] + (i - j) * P
                        op = mm(bank(6 + i // 2)[:, (i % 2) * RDK:(i % 2 + 1) * RDK], s_all[:, at:at + P],
                                rv_tok[:, j, :], start=j == 0, stop=j == i)
                    if i % 2:
                        op.then_inc(ro_mm, 1)
                    fill(6)
                fill(24)
                for d in range(2):
                    pe.wait_ge(ron_ready, 2 * r + 2)
                    for t in range(NT):
                        op = pe.transpose(tiles(bank(4 + d))[:, t, :], ro_n[:, t, d * P:(d + 1) * P], ident)
                    op.then_inc(rotr_mm, 1)

            pe.wait_ge(mix_done, GH + 1)
            with pe.Fori(0, RH - 1) as r:
                unit = Unit(8 * r + N_GDN_UNITS, ret_bank(r))
                unit.m = 4 * UNIT_MM
                ret_scores(r, unit)
                unit = Unit(8 * r + (N_GDN_UNITS + 8), ret_bank(r + 1))
                ret_out(r, unit.fill)
                unit.fill(4 * UNIT_MM - unit.m)
            last = RH - 1
            unit = Unit(8 * last + N_GDN_UNITS, ret_bank(last))
            unit.m = 4 * UNIT_MM
            ret_scores(last, unit)

            def out_mm(kg, kt, t, pas):
                a = (act_hi, act_lo, act_hi)[pas][:, 4 * kg + kt, t * P:(t + 1) * P]
                w = (w_hi, w_hi, w_lo)[pas][:, kg % 2, kt * SEQ:(kt + 1) * SEQ]
                return mm(bank(t), a, w, start=kg == 0 and kt == 0 and pas == 0,
                          stop=kg == 3 and kt == 3 and pas == 2)

            class Early:
                m = 0

                def fill(self, n):
                    for _ in range(n):
                        kg, m = divmod(self.m, UNIT_MM)
                        kt, rest = divmod(m, 12)
                        t, pas = divmod(rest, 3)
                        if self.m < 4 and self.m == 0:
                            pe.wait_ge(rgate_done, 2 * RH)
                        if rest == 0:
                            pe.wait_ge(lo_ready, 4 * OUT_U + 4 * kg + kt + 1)
                            pe.wait_ge(mlo_ready, 4 * kg + kt + 1)
                        op = out_mm(kg, kt, t, pas)
                        if m == UNIT_MM - 1:
                            op.then_inc(proj_done, 1)
                        self.m += 1

            early = Early()
            ret_out(last, early.fill)
            early.fill(3 * UNIT_MM - early.m)

            def last_group(n):
                pe.wait_ge(lo_ready, 16 * n + (4 * OUT_U + 16))
                for t in range(NT):
                    for kt in range(4):
                        for pas in range(3):
                            op = out_mm(3, kt, t, pas)
                    op.then_inc(oproj_mm, 1)

            pe.wait_ge(mlo_ready, 16)
            last_group(0)
            with pe.Fori(1, 4) as n:
                for kg in range(3):
                    for kt in range(4):
                        pe.wait_ge(lo_ready, 16 * n + (4 * OUT_U + 4 * kg + kt + 1))
                        for t in range(NT):
                            if kg == 0 and kt == 0:
                                pe.wait_ge(h_ready, 4 * n + (t - 3))
                            for pas in range(3):
                                op = out_mm(kg, kt, t, pas)
                    op.then_inc(proj_done, 1)
                last_group(n)

        @block.scalar
        def _(act):
            A = act.activation
            act.dma_start(cst[:, :], consts).then_inc(s_cst, 16)
            act.dma_start(rows[0:96, :], conv_w.rearrange("t (c p) -> (t c) p", p=P)).then_inc(s_rows, 16)
            act.dma_start(rows[96:112, :], norm_w.rearrange("(k p) -> k p", p=P)).then_inc(s_rows, 16)
            act.dma_start(rows[112:113, :], gdn_norm_w.rearrange("(a p) -> a p", a=1)).then_inc(s_rows, 16)
            act.dma_start(a_row[:, :], a_log.partition_broadcast(P)).then_inc(s_arow, 16)
            act.dma_start(dt_row[:, :], dt_bias.partition_broadcast(P)).then_inc(s_arow, 16)
            act.dma_start(work2[:, W_GATE, :].bitcast(I32), positions.partition_broadcast(P)).then_inc(s_pos, 16)
            wg_raw = work2[:, W_KBG, 0:KT * 16].rearrange("p (k c) -> p k c", k=KT)
            act.dma_start(wg_raw, w_in_k[:, :, GATE_COL:GATE_COL + 16]).then_inc(s_wg, 16)

            for t in range(NT):
                act.wait_ge(s_x[t], 16)
                if t > 0:
                    act.wait_ge(x_sq, t)
                A(work2[:, 0:2, :].rearrange("p a c -> p (a c)"), x_tok[:, t, 0:D // 2], ACT.Square,
                  accum_out=stat[:, 0, t:t + 1]).then_inc(x_sq, 1)

            def split_hi(u, pair, i, p):
                if p == 0:
                    act.wait_ge(s_w[i % 2], 16 * pair + 16 * (i // 2 + 1))
                    if not (isinstance(u, int) and u + i < 2):
                        act.wait_ge(proj_done, u + (i - 1))
                at = slice(p * PIECE, (p + 1) * PIECE)
                A(w_hi[:, i % 2, at], w_raw[:, i % 2, at], ACT.Copy).then_inc(hi_ready, 1)

            for p in range(4):
                split_hi(0, 0, 0, p)
            act.wait_ge(cols_ready, 1)
            for kt in range(KT):
                act.wait_ge(xt_mm, kt + 1)
                A(act_hi[:, kt, :], bank(2 + kt % 5), ACT.Copy,
                  scale=cols[:, 96 + kt:97 + kt]).then_inc(xhi_ready, 1)
                if kt % 4 == 3:
                    split_hi(0, 0, 1, kt // 4)
            act.wait_ge(s_wg, 16)
            A(wg_hi[:, :, :], wg_raw, ACT.Copy).then_inc(wg_hi_ready, 1)
            for p in range(4):
                split_hi(0, 0, 2, p)

            act.wait_ge(gates_mm, 1)
            gates = bank(2)[:, 0:16 * NT].rearrange("p (t c) -> p c t", c=16)
            sm = [small[:, i, :].rearrange("p (h t) -> p h t", h=GH) for i in range(6)]
            A(sm[0], gates[:, 0:8, :], ACT.Exp, scale=-1.0).then_inc(p_act, 1)
            act.wait_ge(dt_added, 1)
            A(sm[2], sm[1], ACT.Abs).then_inc(p_act, 1)
            act.wait_ge(p_act, 2)
            A(sm[2], sm[2], ACT.Exp, scale=-1.0).then_inc(p_act, 1)
            act.wait_ge(p_act, 3)
            A(sm[2], sm[2], ACT.Ln, bias=1.0).then_inc(p_act, 1)
            act.wait_ge(s_arow, 32)
            A(a_row[:, :], a_row[:, :], ACT.Exp).then_inc(p_act, 1)
            act.wait_ge(p_mm, 1)
            cum = bank(3)[:, 0:GH * NT].rearrange("p (h t) -> p h t", h=GH)
            tot = bank(3)[:, GH * NT:2 * GH * NT].rearrange("p (h t) -> p h t", h=GH)
            A(head_par[:, :, 8:12], cum, ACT.Exp).then_inc(p_act, 1)
            A(head_par[:, :, 16:20], tot, ACT.Exp).then_inc(p_act, 1)
            act.wait_ge(p_dve, 2)
            A(head_par[:, :, 12:16], sm[3], ACT.Exp).then_inc(p_ready, 1)

            def tap3(h_units, s):
                A(conv[:, s, :], bank(s % 2), ACT.Copy, scale=conv_par[:, 3, s:s + 1]).then_inc(tap_done, 1)

            def silu(s):
                A(conv[:, s, :], conv[:, s, :], ACT.Silu).then_inc(silu_done, 1)

            act.wait_ge(conv_par_ready, 1)
            for e in range(GH):
                act.wait_ge(dif_ready, e + 1)
                A(wk(W_X + e % 2), wk(W_X + e % 2), ACT.Exp).then_inc(dif_exp, 1)
                if e in (0, 3):
                    s = e // 3
                    act.wait_ge(proj_done, s + 1)
                    tap3(0, s)
                split_hi(0, 0, 3 + e // 4, e % 4)
            act.wait_ge(rope_arg, 2)
            A(rope_sin[:, :], rope_sin[:, :], ACT.Sin).then_inc(rope_ready, 1)
            A(rope_cos[:, :], rope_cos[:, :], ACT.Sin).then_inc(rope_ready, 1)
            for s in range(3):
                if s == 2:
                    act.wait_ge(proj_done, 3)
                    tap3(0, 2)
                act.wait_ge(conv_done, s + 1)
                silu(s)

            def gdn_body(h, unit0, pair, following):
                hi = lambda k: split_hi(unit0, pair, 1 + k // 4, k % 4)
                act.wait_ge(proj_done, 4 * h + 4)
                act.wait_ge(mix_done, h + 1)
                A(gate, bank(1), ACT.Silu).then_inc(gate_done, 1)
                hi(0)
                for s in range(2):
                    act.wait_ge(tr_in, 3 * h + (s + 1))
                    A(ys[s], bank(2 + s), ACT.Square).then_inc(qk_sq, 1)
                act.wait_ge(tr_in, 3 * h + 3)
                A(vtok, bank(4), ACT.Copy).then_inc(v_ready, 1)
                hi(1)
                hi(2)
                for s, dst in enumerate((kT, qT, qgT)):
                    act.wait_ge(tr_back, 3 * h + (s + 1))
                    A(dst, bank(5 + s), ACT.Copy).then_inc(t_ready, 1)
                hi(3)
                for n in range(1, LEVELS):
                    act.wait_ge(t1_mm, 6 * h + n)
                    A(t1, bank(4), ACT.Copy).then_inc(t1_ready, 1)
                    hi(3 + n)
                    if following == "gdn":
                        if n == 1:
                            act.wait_ge(proj_done, unit0 + 1)
                            act.wait_ge(conv_par_ready, h + 2)
                            tap3(0, 0)
                        if n == 3:
                            act.wait_ge(conv_done, 3 * h + 4)
                            silu(0)
                        if n == 5:
                            act.wait_ge(proj_done, unit0 + 2)
                            tap3(0, 1)
                act.wait_ge(uw_mm, 2 * h + 2)
                A(w_t, bank(6), ACT.Copy).then_inc(w_ready, 1)
                hi(10)
                if following == "gdn":
                    act.wait_ge(conv_done, 3 * h + 5)
                    silu(1)
                hi(11)
                hi(12)
                if following == "gdn":
                    act.wait_ge(proj_done, unit0 + 3)
                    tap3(0, 2)
                hi(13)
                hi(14)
                hi(15)
                act.wait_ge(o_mm, h + 1)
                A(ys[0], bank(7), ACT.Square).then_inc(o_sq, 1)
                if following == "gdn":
                    act.wait_ge(conv_done, 3 * h + 6)
                    silu(2)

            with act.Fori(0, GH - 1) as h:
                gdn_body(h, 4 * h + 4, 2 * h + 2, "gdn")
            gdn_body(GH - 1, N_GDN_UNITS, N_GDN_UNITS // 2, "ret")

            def ret_a(r, unit0, pair, n_pieces=16):
                hi = lambda k: split_hi(unit0, pair, 5 + k // 4, k % 4)
                for k in range(n_pieces):
                    hi(k)
                    if k == 5 or k == 9:
                        d = (k - 5) // 4
                        act.wait_ge(proj_done, unit0 + (5 + d))

                        A(v_feat[:, d, :], bank(d), ACT.Copy).then_inc(vf_done, 1)
                act.wait_ge(proj_done, unit0 + 7)
                A(rgate[:, 0, :], bank(0), ACT.Silu).then_inc(rgate_done, 1)
                act.wait_ge(rvt_mm, r + 1)
                for b in range(2):
                    A(work2[:, 2 + b, :], bank(4 + b), ACT.Copy).then_inc(rvt_ready, 1)
                act.wait_ge(proj_done, unit0 + 8)
                A(rgate[:, 1, :], bank(1), ACT.Silu).then_inc(rgate_done, 1)

            def ret_b(r, hi):
                for b in range(2):
                    act.wait_ge(ro_mm, 2 * r + (b + 1))
                    A(ro_sq[:, b, :], bank(6 + b), ACT.Square).then_inc(ro_sqd, 1)
                    hi(b)

            act.wait_ge(mix_done, GH + 1)
            with act.Fori(0, RH - 1) as r:
                ret_a(r, 8 * r + N_GDN_UNITS, 4 * r + N_GDN_UNITS // 2)
                hi = lambda k: split_hi(8 * r + (N_GDN_UNITS + 8), 4 * r + (N_GDN_UNITS // 2 + 4),
                                        1 + k // 4, k % 4)
                ret_b(r, hi)
                for k in range(2, 16):
                    hi(k)
            last = RH - 1
            ret_a(last, 8 * last + N_GDN_UNITS, 4 * last + N_GDN_UNITS // 2)

            def mix_hi(s):
                if s >= GH:
                    act.wait_ge(rmix_done, s - GH + 2)
                A(act_hi[:, s, :], mix[:, s, :], ACT.Copy).then_inc(mhi_ready, 1)

            for s in range(6):
                mix_hi(s)
            hi = lambda k: split_hi(OUT_U, OUT_U // 2, 1 + k // 4, k % 4)
            ret_b(last, hi)
            for s in range(6, 14):
                mix_hi(s)
                hi(s - 4)
            hi(10)
            hi(11)
            mix_hi(14)
            mix_hi(15)
            for k in range(12, 16):
                hi(k)

            def square_h(n, t):
                act.wait_ge(h_ready, 4 * n + (t + 1))
                if not (isinstance(n, int) and n + t == 0):
                    act.wait_ge(h_sq, 4 * n + t)
                A(work1[:, 4, :], h_tok[:, t, bass.ds(n * SEQ, SEQ)], ACT.Square,
                  accum_out=small[:, 0, bass.ds(4 * t + n, 1)]).then_inc(h_sq, 1)

            for t in range(NT):
                square_h(0, t)
            def hi_out(n, k):
                i, p = 1 + k // 4, k % 4
                if p == 0:
                    act.wait_ge(s_w[i % 2], 32 * n + (8 * OUT_U + 16 * (i // 2) + 16))
                    if i == 1:
                        act.wait_ge(oproj_mm, 4 * n)
                    else:
                        act.wait_ge(proj_done, 3 * n + (OUT_U + i - 1))
                at = slice(p * PIECE, (p + 1) * PIECE)
                A(w_hi[:, i % 2, at], w_raw[:, i % 2, at], ACT.Copy).then_inc(hi_ready, 1)

            with act.Fori(1, 3) as n:
                for k in range(16):
                    hi_out(n, k)
                for t in range(NT):
                    square_h(n, t)
            for k in range(12):
                hi_out(3, k)
            for t in range(NT):
                square_h(3, t)

        @block.vector
        def _(dve):
            TT, TS, STT = dve.tensor_tensor, dve.tensor_scalar, dve.scalar_tensor_tensor
            link = Links(dve, dve_link)
            dve.memset(ones[:, :], 1.0).then_inc(memsets, 1)
            dve.memset(half[:, :], -0.5).then_inc(memsets, 1)
            dve.memset(stat[:, 0, 14:15], 0.0).then_inc(mix_done, 1)
            dve.memset(stat[:, 0, 15:16], 0.0).then_inc(rmix_done, 1)

            def scale_x(t):
                dve.wait_ge(x_rstd, t + 1)
                TS(x_tok[:, t, :], x_tok[:, t, :], stat[:, 3, t:t + 1], math.sqrt(D), ALU.mult,
                   ALU.mult).then_inc(x_scaled, 1)

            for t in range(NT):
                dve.wait_ge(s_x[t], 16)
                link(dve.tensor_tensor_reduce(work2[:, 2:4, :].rearrange("p a c -> p (a c)"),
                                              x_tok[:, t, D // 2:], x_tok[:, t, D // 2:], 1.0, 0.0,
                                              ALU.mult, ALU.add, stat[:, 1, t:t + 1]))
                dve.wait_ge(x_sq, t + 1)
                TS(stat[:, 2, t:t + 1], stat[:, 0, t:t + 1], stat[:, 1, t:t + 1], D * EPS, ALU.add,
                   ALU.add).then_inc(x_ms, 1)
                if t == 0:
                    dve.wait_ge(cols_mm, 1)
                    dve.tensor_copy(cols[:, 0:113], bank(7)[:, 0:113]).then_inc(cols_ready, 1)
                else:
                    scale_x(t - 1)
            scale_x(NT - 1)

            def split_lo(u, i, p):
                dve.wait_ge(hi_ready, 4 * u + (4 * i + p + 1))
                at = slice(p * PIECE, (p + 1) * PIECE)
                TT(w_lo[:, i % 2, at], w_raw[:, i % 2, at], w_hi[:, i % 2, at].bitcast(F32),
                   ALU.subtract).then_inc(lo_ready, 1)

            for p in range(4):
                split_lo(0, 0, p)
            dve.wait_ge(cols_ready, 1)
            for kt in range(KT):
                dve.wait_ge(xhi_ready, kt + 1)
                STT(act_lo[:, kt, :], bank(2 + kt % 5), cols[:, 96 + kt:97 + kt],
                    act_hi[:, kt, :].bitcast(F32), ALU.mult, ALU.subtract).then_inc(xlo_ready, 1)
                if kt % 4 == 3:
                    split_lo(0, 1, kt // 4)
            wg_raw = work2[:, W_KBG, 0:KT * 16].rearrange("p (k c) -> p k c", k=KT)
            dve.wait_ge(wg_hi_ready, 1)
            TT(wg_lo[:, :, :], wg_raw, wg_hi[:, :, :].bitcast(F32), ALU.subtract).then_inc(wg_lo_ready, 1)
            for p in range(2):
                split_lo(0, 2, p)

            sm = [small[:, i, :].rearrange("p (h t) -> p h t", h=GH) for i in range(6)]
            gates = bank(2)[:, 0:16 * NT].rearrange("p (t c) -> p c t", c=16)
            dve.wait_ge(s_arow, 32)
            dve.wait_ge(p_act, 1)
            TT(sm[1], gates[:, 8:16, :], over_free(dt_row[:, :], NT), ALU.add).then_inc(dt_added, 1)
            link(TS(sm[0], sm[0], 1.0, None, ALU.add))
            link(dve.reciprocal(head_par[:, :, 0:4], sm[0]))
            TS(head_par[:, :, 4:8], head_par[:, :, 0:4], -1.0, None, ALU.mult).then_inc(p_ready, 1)
            dve.wait_ge(p_act, 5)
            link(STT(sm[4], sm[1], 0.0, sm[2], ALU.max, ALU.add))
            STT(g_log[:, :, :], sm[4], -1.0, over_free(a_row[:, :], NT), ALU.mult, ALU.mult).then_inc(p_dve, 1)
            dve.wait_ge(p_mm, 1)
            cum = bank(3)[:, 0:GH * NT].rearrange("p (h t) -> p h t", h=GH)
            tot = bank(3)[:, GH * NT:2 * GH * NT].rearrange("p (h t) -> p h t", h=GH)
            dve.wait_ge(p_act, 7)
            link(dve.tensor_copy(g_cum[:, :, :], cum))
            link(TT(sm[5], tot, g_cum[:, :, :], ALU.subtract))
            TS(sm[3], sm[5], 0.0, None, ALU.min).then_inc(p_dve, 1)

            def conv_weights(h):
                if not isinstance(h, int):
                    dve.wait_ge(conv_done, 3 * h)
                src = cols[:, 0:96].rearrange("p (t s c) -> p t s c", t=4, s=3)[:, :, :, bass.ds(h, 1)]
                dve.tensor_copy(conv_par[:, :, :].unsqueeze(3), src).then_inc(conv_par_ready, 1)

            def tap(h, s, j, link):
                back = 3 - j
                op = STT(conv[:, s, back:], bank(s % 2)[:, 0:SEQ - back], conv_par[:, j, s:s + 1],
                         conv[:, s, back:], ALU.mult, ALU.add)
                if j == 2:
                    op.then_inc(conv_done, 1)
                else:
                    link(op)

            conv_weights(0)
            split_lo(0, 2, 2)
            split_lo(0, 2, 3)

            def decay_in(e):
                if e >= 2:
                    dve.wait_ge(g_mm, e - 1)
                TT(tiles(ys[e % 2]), over_tiles(causal), over_free(g_log[:, e, :]),
                   ALU.mult).then_inc(ug_ready, 1)

            decay_in(0)
            for e in range(GH):
                if e + 1 < GH:
                    decay_in(e + 1)
                dve.wait_ge(g_mm, e + 1)
                if e >= 2:
                    dve.wait_ge(decay_ready, e - 1)
                dif = wk(W_X + e % 2)
                link(TT(tiles(dif), tiles(bank(4 + e % 2)), over_free(g_cum[:, e, :]), ALU.subtract))
                TS(dif, dif, 0.0, None, ALU.min).then_inc(dif_ready, 1)
                split_lo(0, 3 + e // 4, e % 4)
                if e in (0, 3):
                    s = e // 3
                    dve.wait_ge(tap_done, s + 1)
                    for j in range(3):
                        tap(0, s, j, link)

            magic = 1.5 * 2.0 ** 23
            c1, c2 = 6.28125, float(np.float32(2 * math.pi - 6.28125))
            c3 = float(np.float32(2 * math.pi - 6.28125 - c2))
            pos_f, turns, angle = wk(W_KTOK), wk(W_QTOK), wk(W_QGTOK)
            dve.wait_ge(s_pos, 16)
            link(dve.tensor_copy(pos_f, work2[:, W_GATE, :].bitcast(I32)))
            link(TS(angle, pos_f, inv_freq, None, ALU.mult))
            for dst, quarter in ((rope_sin, 0.0), (rope_cos, 0.25)):
                link(TS(turns, angle, 1.0 / (2 * math.pi), quarter, ALU.mult, ALU.add))
                link(TS(turns, turns, magic, None, ALU.add))
                link(TS(turns, turns, -magic, None, ALU.add))
                link(STT(dst[:, :], turns, -c1, angle, ALU.mult, ALU.add))
                link(STT(dst[:, :], turns, -c2, dst[:, :], ALU.mult, ALU.add))
                link(STT(dst[:, :], turns, -c3, dst[:, :], ALU.mult, ALU.add))
                link(TS(dst[:, :], dst[:, :], quarter * 2 * math.pi, 3.1415925, ALU.add, ALU.min))
                TS(dst[:, :], dst[:, :], -3.1415925, None, ALU.max).then_inc(rope_arg, 1)
            dve.wait_ge(tap_done, 3)
            for j in range(3):
                tap(0, 2, j, link)

            dve.wait_ge(p_ready, 2)
            dve.wait_ge(rope_ready, 2)

            def rot(r, i, first_wait):
                dst = (q_rot, k_rot)[i // 2]
                if i == 0:
                    first_wait()
                dve.wait_ge(proj_done, 8 * r + (N_GDN_UNITS + 1 + i))
                if i % 2 == 0:
                    a, b = dst[:, 0, :], dst[:, 1, :]
                else:
                    if i == 3:
                        dve.wait_ge(rot_done, 4 * r + 2)
                    elif not isinstance(r, int):
                        dve.wait_ge(rot_done, 4 * r)
                    a, b = rot_tmp[:, 1, :], rot_tmp[:, 0, :]
                TT(a, bank(i % 2), rope_cos[:, :], ALU.mult)
                TT(b, bank(i % 2), rope_sin[:, :], ALU.mult).then_inc(rot_read, 1)

            def gdn_body(h, unit0, following):
                glink = Links(dve, dve_link_gdn, DVE_GDN_LINKS * h)
                lo = lambda k: split_lo(unit0, 1 + k // 4, k % 4)
                dve.wait_ge(mix_done, h + 1)
                dve.tensor_copy(par[:, :].unsqueeze(1), head_par[:, bass.ds(h, 1), :]).then_inc(par_ready, 1)
                if following == "gdn":
                    conv_weights(h + 1)
                beta, nbeta, eg = par[:, 0:4], par[:, 4:8], par[:, 8:12]
                lo(0)
                for s in range(2):
                    dve.wait_ge(qk_sq, 2 * h + (s + 1))
                    glink(dve.tensor_reduce(stat[:, 0, 4 * s:4 * s + 4], tiles(ys[s]), AX.X, ALU.add))
                TS(stat[:, 1, 0:4], stat[:, 0, 0:4], P * EPS, float(P), ALU.add, ALU.mult).then_inc(ss_ready, 1)
                TS(stat[:, 1, 4:8], stat[:, 0, 4:8], P * EPS, None, ALU.add).then_inc(ss_ready, 1)
                lo(1)
                dve.wait_ge(r_ready, h + 1)
                dve.wait_ge(par_ready, h + 1)
                TT(stat[:, 3, 0:4], stat[:, 2, 0:4], eg, ALU.mult).then_inc(rqg_ready, 1)
                TT(tiles(ktok), tiles(bank(3)), over_free(stat[:, 2, 4:8]), ALU.mult).then_inc(tok_ready, 1)
                TT(tiles(qtok), tiles(bank(2)), over_free(stat[:, 2, 0:4]), ALU.mult).then_inc(tok_ready, 1)
                dve.wait_ge(rqg_ready, h + 1)
                TT(tiles(qgtok), tiles(bank(2)), over_free(stat[:, 3, 0:4]), ALU.mult).then_inc(tok_ready, 1)
                lo(2)
                lo(3)
                decay = mix[:, bass.ds(h, 1), :].rearrange("p a (t c) -> p (a t) c", t=NT)
                dve.wait_ge(decay_ready, GH)
                dve.wait_ge(kk_mm, 2 * h + 1)
                for t in range(NT):
                    op = STT(tiles(lower_t)[:, t, :], tiles(bank(2))[:, t, :], beta[:, t:t + 1],
                             decay[:, t, :], ALU.mult, ALU.mult)
                    op.then_inc(low_ready, 1) if t == NT - 1 else None
                dve.wait_ge(kk_mm, 2 * h + 2)
                TT(tiles(attn_t), tiles(bank(3)), decay, ALU.mult).then_inc(low_ready, 1)
                dve.wait_ge(y_ready, 7 * h + 1)
                glink(TT(tiles(inv_t), tiles(ys[0]), over_tiles(ident), ALU.add))
                dve.transpose(inv, inv_t).then_inc(inv_first, 1)
                for n in range(1, 7):
                    if n < 6:
                        dve.wait_ge(lvl_mm, 7 * h + n)
                        TT(inv, inv, bank(5), ALU.add).then_inc(lvl_ready, 1) if n == 5 else \
                            glink(TT(inv, inv, bank(5), ALU.add))
                    if n < 5:
                        dve.transpose(inv_t, inv).then_inc(lvl_ready, 1)
                    else:
                        dve.wait_ge(lvl_mm, 7 * h + (n + 1))
                        TT(inv_t, inv_t, bank(6), ALU.add).then_inc(lvl_ready, 1)
                    lo(3 + n)
                    if following == "gdn":
                        if n in (1, 2, 3):
                            if n == 1:
                                dve.wait_ge(tap_done, 3 * h + 4)
                            tap(0, 0, n - 1, glink)
                        if n == 6:
                            dve.wait_ge(tap_done, 3 * h + 5)
                            for j in range(3):
                                tap(0, 1, j, glink)
                    else:
                        if n == 2:
                            rot(0, 0, lambda: dve.wait_ge(tr_in, 3 * GH))
                        if n == 6:
                            rot(0, 1, None)
                dve.wait_ge(uw_mm, 2 * h + 1)
                TT(tiles(vnew), tiles(bank(2)), over_free(beta), ALU.mult).then_inc(vn_ready, 1)
                lo(10)
                for t in range(NT):
                    tt = slice(t * P, (t + 1) * P)
                    if t > 0:
                        dve.wait_ge(ws_mm, 3 * h + t)
                        STT(vnew[:, tt], bank(4)[:, tt], nbeta[:, t:t + 1], vnew[:, tt], ALU.mult,
                            ALU.add).then_inc(vn_ready, 1)
                    if t < NT - 1:
                        dve.wait_ge(ktv_mm, 3 * h + (t + 1))
                        if t == 0:
                            dve.tensor_copy(state[0], bank(5)[:, tt]).then_inc(st_ready, 1)
                        else:
                            dve.wait_ge(st_ready, 3 * h + t)
                            STT(state[t], state[t - 1], par[:, 16 + t:17 + t], bank(5)[:, tt], ALU.mult,
                                ALU.add).then_inc(st_ready, 1)
                    if t != 1:
                        lo((11, 0, 12, 13)[t])
                if following == "gdn":
                    dve.wait_ge(tap_done, 3 * h + 6)
                    for j in range(3):
                        tap(0, 2, j, glink)
                else:
                    rot(0, 2, None)
                dve.wait_ge(o_sq, h + 1)
                glink(dve.tensor_reduce(stat[:, 0, 8:12], tiles(ys[0]), AX.X, ALU.add))
                TS(stat[:, 1, 8:12], stat[:, 0, 8:12], 1.0 / P, EPS, ALU.mult, ALU.add).then_inc(o_ms, 1)
                lo(14)
                lo(15)
                dve.wait_ge(o_rstd, h + 1)
                TT(tiles(o_n), tiles(bank(7)), over_free(stat[:, 2, 8:12]), ALU.mult).then_inc(on_ready, 1)
                dve.wait_ge(otr_mm, h + 1)
                STT(mix[:, bass.ds(h, 1), :].rearrange("p a c -> p (a c)"), bank(6), cols[:, 112:113], gate,
                    ALU.mult, ALU.mult).then_inc(mix_done, 1)
                return glink.n

            with dve.Fori(0, GH - 1) as h:
                used = gdn_body(h, 4 * h + 4, "gdn")
            assert used == DVE_GDN_LINKS, used
            gdn_body(GH - 1, N_GDN_UNITS, "ret")

            def ret_a(r, unit0):
                lo = lambda k: split_lo(unit0, 5 + k // 4, k % 4)
                rot(r, 3, None)
                for k in range(16):
                    lo(k)
                    if k in (1, 3, 5, 7):
                        j = k // 2
                        n = SEQ - j * P
                        dve.wait_ge(rs_mm, 4 * r + (j + 1))
                        if j == 0:
                            dve.wait_ge(s_dec, 16 * RH)
                        table = mix[:, bass.ds(2 * r + GH, 1), 0:n].rearrange("p a c -> p (a c)")
                        TT(s_all[:, s_off[j]:s_off[j] + n], bank(4 + j)[:, 0:n], table,
                           ALU.mult).then_inc(rs_ready, 1)

            def ret_b(r, lo, following):
                rlink = Links(dve, dve_link_ret, DVE_RET_LINKS * r)
                sq = ro_sq.rearrange("p a c -> p (a c)").rearrange("p (j d) -> p j d", j=NT)
                for b in range(2):
                    dve.wait_ge(ro_sqd, 2 * r + (b + 1))
                    rlink(dve.tensor_reduce(stat[:, 0, 2 * b:2 * b + 2], sq[:, 2 * b:2 * b + 2, :], AX.X,
                                            ALU.add))
                    lo(b)
                TS(stat[:, 1, 0:4], stat[:, 0, 0:4], 1.0 / RDK, EPS, ALU.mult, ALU.add).then_inc(ro_ms, 1)
                lo(2)
                dve.wait_ge(ro_rstd, r + 1)
                for b in range(2):
                    TT(ro_n[:, 2 * b:2 * b + 2, :], bank(6 + b).rearrange("p (j d) -> p j d", j=2),
                       over_free(stat[:, 2, 2 * b:2 * b + 2], RDK), ALU.mult).then_inc(ron_ready, 1)
                lo(3)
                for d in range(2):
                    dve.wait_ge(rotr_mm, 2 * r + (d + 1))
                    dve.wait_ge(rgate_done, 2 * r + (d + 1))
                    TT(mix[:, bass.ds(2 * r + (GH + d), 1), :].rearrange("p a c -> p (a c)"), bank(4 + d),
                       rgate[:, d, :], ALU.mult).then_inc(rmix_done, 1)
                assert rlink.n == DVE_RET_LINKS

            with dve.Fori(0, RH - 1) as r:
                ret_a(r, 8 * r + N_GDN_UNITS)
                lo = lambda k: split_lo(8 * r + (N_GDN_UNITS + 8), 1 + k // 4, k % 4)
                ret_b(r, lo, "ret")
                for i in range(3):
                    for k in range(4):
                        lo(4 + 4 * i + k)
                    rot(r + 1, i, lambda: dve.wait_ge(rs_mm, 4 * r + 4))
            last = RH - 1
            ret_a(last, 8 * last + N_GDN_UNITS)

            def mix_lo(s):
                dve.wait_ge(mhi_ready, s + 1)
                if s == 0:
                    dve.wait_ge(proj_done, OUT_U)
                TT(act_lo[:, s, :], mix[:, s, :], act_hi[:, s, :].bitcast(F32),
                   ALU.subtract).then_inc(mlo_ready, 1)

            for s in range(6):
                mix_lo(s)
            lo = lambda k: split_lo(OUT_U, 1 + k // 4, k % 4)
            ret_b(last, lo, "out")
            for s in range(6, 14):
                mix_lo(s)
                if s < 14 and s - 2 < 12:
                    lo(s - 2)
            mix_lo(14)
            mix_lo(15)
            for k in range(12, 16):
                lo(k)

            def add_x(n, t):
                dve.wait_ge(oproj_mm, 4 * n + (t + 1))
                at = h_tok[:, t, bass.ds(n * SEQ, SEQ)]
                TT(at, at, bank(t), ALU.add).then_inc(h_ready, 1)

            dve.wait_ge(s_xres[0], 16)
            for t in range(NT):
                add_x(0, t)
            for n in range(1, 4):
                dve.wait_ge(s_xres[n], 16)
            with dve.Fori(1, 3) as n:
                for k in range(16):
                    split_lo(4 * n + OUT_U, 1 + k // 4, k % 4)
                for t in range(NT):
                    add_x(n, t)
            for k in range(12):
                split_lo(OUT_U + 12, 1 + k // 4, k % 4)
            dve.wait_ge(s_fin, 16)
            for t in range(NT):
                add_x(3, t)
                dve.wait_ge(h_sq, 12 + t + 1)
                link(dve.tensor_reduce(stat[:, 0, t:t + 1], small[:, 0, 4 * t:4 * t + 4], AX.X, ALU.add))
                TS(stat[:, 1, t:t + 1], stat[:, 0, t:t + 1], 1.0 / D, EPS, ALU.mult, ALU.add).then_inc(h_ms, 1)
                dve.wait_ge(h_rstd, t + 1)
                STT(h_tok[:, t, :], h_tok[:, t, :], stat[:, 2, t:t + 1], fin_w, ALU.mult,
                    ALU.mult).then_inc(y_done, 1)

        @block.gpsimd
        def _(pool):
            TT = pool.tensor_tensor
            for t in range(NT):
                pool.wait_ge(x_ms, t + 1)
                if t == 0:
                    pool.wait_ge(memsets, 2)
                TT(stat[:, 3, t:t + 1], stat[:, 2, t:t + 1], half[:, 0:1], ALU.pow).then_inc(x_rstd, 1)
            pool.wait_ge(xt_mm, KT)
            pool.wait_ge(s_cst, 16)
            for e in range(GH):
                pool.wait_ge(dif_exp, e + 1)
                TT(tiles(mix[:, e, :]), tiles(wk(W_X + e % 2)), over_tiles(causal),
                   ALU.mult).then_inc(decay_ready, 1)

            def rot_sum(r, i):
                dst = (q_rot, k_rot)[i]
                pool.wait_ge(rot_read, 4 * r + (2 * i + 2))
                TT(dst[:, 0, :], dst[:, 0, :], rot_tmp[:, 0, :], ALU.subtract).then_inc(rot_done, 1)
                TT(dst[:, 1, :], dst[:, 1, :], rot_tmp[:, 1, :], ALU.add).then_inc(rot_done, 1)

            def gdn_body(h, following):
                pool.wait_ge(ss_ready, 2 * h + 2)
                TT(stat[:, 2, 0:8], stat[:, 1, 0:8], half_cols, ALU.pow).then_inc(r_ready, 1)
                pool.wait_ge(tok_ready, 3 * h + 1)
                pool.wait_ge(par_ready, h + 1)
                pool.wait_ge(low_ready, 2 * h + 1)
                for n in range(2):
                    TT(tiles(ys[n]), tiles(lower_t), over_tiles(level_mask(n)), ALU.mult).then_inc(y_ready, 1)
                TT(tiles(kbg), tiles(ktok), over_free(par[:, 8:12]), ALU.mult).then_inc(kk_ready, 1)
                TT(tiles(ktail), tiles(ktok), over_free(par[:, 12:16]), ALU.mult).then_inc(kk_ready, 1)
                for n in range(2, LEVELS):
                    if n == 2:
                        pool.wait_ge(inv_first, h + 1)
                    else:
                        pool.wait_ge(t1_mm, 6 * h + (n - 2))
                    TT(tiles(ys[n % 2]), tiles(lower_t), over_tiles(level_mask(n)), ALU.mult).then_inc(y_ready, 1)
                if following == "ret":
                    rot_sum(0, 0)
                pool.wait_ge(o_ms, h + 1)
                TT(stat[:, 2, 8:12], stat[:, 1, 8:12], half[:, 0:4], ALU.pow).then_inc(o_rstd, 1)

            with pool.Fori(0, GH - 1) as h:
                gdn_body(h, "gdn")
            gdn_body(GH - 1, "ret")

            def ret_norm(r):
                pool.wait_ge(ro_ms, r + 1)
                TT(stat[:, 2, 0:4], stat[:, 1, 0:4], half[:, 0:4], ALU.pow).then_inc(ro_rstd, 1)

            with pool.Fori(0, RH - 1) as r:
                rot_sum(r, 1)
                ret_norm(r)
                rot_sum(r + 1, 0)
            rot_sum(RH - 1, 1)
            ret_norm(RH - 1)
            for t in range(NT):
                pool.wait_ge(h_ms, t + 1)
                TT(stat[:, 2, t:t + 1], stat[:, 1, t:t + 1], half[:, 0:1], ALU.pow).then_inc(h_rstd, 1)


def shape_constants():
    j, i = np.arange(P)[:, None], np.arange(P)[None, :]
    parts = [np.eye(P), (i >= j)]
    for n in range(LEVELS):
        parts.append(-1.0 * (((i >> n) & 1 == 1) & ((j >> n) == (i >> n) - 1)))
    freq = 1.0 / (np.float32(10000.0) ** (np.arange(0, RDK, 2, dtype=np.float32) / np.float32(RDK)))
    parts.append(freq[:, None])
    consts = np.concatenate([p.astype(np.float32) for p in parts], axis=1)
    gamma = 1.0 - 2.0 ** (-5.0 - np.arange(RH))
    rel = np.arange(SEQ)[None, :] - np.arange(P)[:, None]
    decays = np.where(rel >= 0, gamma[:, None, None] ** np.maximum(rel, 0), 0.0) * RDK ** -0.5
    return consts, decays.astype(np.float32)


def kernel(**inputs):
    import concourse.bacc as bacc
    from concourse.bass_utils import run_bass_kernel_spmd

    consts, decays = shape_constants()
    given = {name: np.asarray(a) for name, a in inputs.items()}
    arrays = {
        "x": given["x"][0], "positions": given["positions"][0], "norm_w": given["norm_w"][0],
        "w_in": given["w_in"][0], "conv_w": given["conv_w"][0], "a_log": given["a_log"][0],
        "dt_bias": given["dt_bias"][0], "gdn_norm_w": given["gdn_norm_w"][0],
        "w_out": given["w_out"][0], "final_norm_w": given["final_norm_w"],
        "consts": consts, "decays": decays,
    }
    arrays = {f"in_{name}": np.ascontiguousarray(a) for name, a in arrays.items()}
    nc = bacc.Bacc("TRN2", target_bir_lowering=False, num_devices=1)
    aps = [nc.dram_tensor(name, a.shape, mybir.dt.from_np(a.dtype), kind="ExternalInput").ap()
           for name, a in arrays.items()]
    y = nc.dram_tensor("y", (SEQ, D), F32, kind="ExternalOutput").ap()
    build(nc, *aps, y)
    result = run_bass_kernel_spmd(nc, [arrays], core_ids=[0])
    return result.results[0]["y"].reshape(1, SEQ, D)
```

```python
import math
from contextlib import ExitStack

import numpy as np
import concourse.bass as bass
from concourse import mybir

F32 = mybir.dt.float32
F32R = mybir.dt.float32r
I32 = mybir.dt.int32
ALU = mybir.AluOpType
ACT = mybir.ActivationFunctionType
AX = mybir.AxisListType

P = 128
SEQ = 512
D = 2048
KT = D // P
NT = SEQ // P
GH, RH = 8, 4
RDK = 256
GROUP = 1024
GDN_COL = 4 * GROUP
GATE_COL = 8 * GROUP
EPS = 1e-6
PIECE = 512
UNIT_MM = 3 * KT
N_GDN_UNITS = 4 * GH
N_RET_UNITS = 8 * RH
OUT_U = N_GDN_UNITS + N_RET_UNITS
LEVELS = 7
BLK = 32
NP = 20

(W_KTOK, W_QTOK, W_QGTOK, W_VTOK, W_KT, W_QT, W_QGT, W_Y0, W_Y1, W_X, W_XT, W_T1, W_KBG, W_KTAIL,
 W_VN, W_S, W_GATE) = range(17)

DVE_GDN_LINKS = 16
DVE_RET_LINKS = 2


class Links:

    def __init__(self, eng, sem, base=0):
        self.eng, self.sem, self.base, self.n = eng, sem, base, 0

    def __call__(self, instruction):
        instruction.then_inc(self.sem, 1)
        self.n += 1
        self.eng.wait_ge(self.sem, self.base + self.n)


def build(nc, x, positions, norm_w, w_in, conv_w, a_log, dt_bias, gdn_norm_w, w_out, final_norm_w,
          consts, decays, out):
    with ExitStack() as ctx:
        def sb(name, shape, dt=F32):
            return ctx.enter_context(nc.sbuf_tensor(name, shape, dt))

        def sem(name):
            return ctx.enter_context(nc.semaphore(name))

        act_hi = sb("act_hi", [P, KT, SEQ], F32R)
        act_lo = sb("act_lo", [P, KT, SEQ], F32R)
        w_raw = sb("w_raw", [P, 2, KT * P])
        w_hi = sb("w_hi", [P, 2, KT * P], F32R)
        w_lo = sb("w_lo", [P, 2, KT * P], F32R)
        mix = sb("mix", [P, KT, SEQ])
        work1 = sb("work1", [P, 6, SEQ])
        work2 = sb("work2", [P, 17, SEQ])
        cst = sb("cst", [P, (3 + LEVELS) * P + 1])
        inv_blocks = sb("inv_blocks", [P, NT * BLK])
        ones = sb("ones", [P, P])
        rope_cos = sb("rope_cos", [P, SEQ])
        rope_sin = sb("rope_sin", [P, SEQ])
        rows = sb("rows", [P, P])
        cols = sb("cols", [P, P])
        wg_hi = sb("wg_hi", [P, KT, 16], F32R)
        wg_lo = sb("wg_lo", [P, KT, 16], F32R)
        head_par = sb("head_par", [P, GH, NP])
        par = sb("par", [P, NP])
        conv_par = sb("conv_par", [P, 4, 3])
        g_log = sb("g_log", [P, GH, NT])
        g_cum = sb("g_cum", [P, GH, NT])
        small = sb("small", [P, 6, GH * NT])
        a_row = sb("a_row", [P, GH])
        dt_row = sb("dt_row", [P, GH])
        stat = sb("stat", [P, 4, 16])
        half = sb("half", [P, 16])
        ps = ctx.enter_context(nc.psum_tensor("ps", [P, 8, SEQ], F32))

        ident = cst[:, 0:P]
        causal = cst[:, P:2 * P]
        diag_mask = cst[:, (2 + LEVELS) * P:(3 + LEVELS) * P]
        inv_freq = cst[:, (3 + LEVELS) * P:]

        def level_mask(n):
            return cst[:, (2 + n) * P:(3 + n) * P]

        def tiles(ap):
            return ap.rearrange("p (t c) -> p t c", t=NT)

        def bank(b):
            return ps[:, b, :]

        def over_free(col, n=P):
            return col.unsqueeze(2).to_broadcast([P, col.shape[1], n])

        def over_tiles(mat, n=NT):
            return mat.unsqueeze(1).to_broadcast([P, n, mat.shape[1]])

        wk = lambda i: work2[:, i, :]
        conv = work1
        q_eps, k_norm2, k_norm = stat[:, 1, 0:4], stat[:, 1, 4:8], stat[:, 2, 4:8]
        beta_both = stat[:, 3, 8:16]
        beta_k, nbeta_k = beta_both[:, 0:4], beta_both[:, 4:8]
        x_tok = mix[:, :, :].rearrange("p (t a) c -> p t (a c)", t=NT)
        ktok, vtok, q_keep = wk(W_KTOK), wk(W_VTOK), wk(W_QT)
        lower_t, attn_t, w_t = wk(W_QTOK), wk(W_QGTOK), wk(W_KT)
        ys = [wk(W_Y0), wk(W_Y1)]
        inv, inv_t, t1, o_n = wk(W_X), wk(W_XT), wk(W_T1), wk(W_T1)
        kbg, ktail, vnew = wk(W_KBG), wk(W_KTAIL), wk(W_VN)
        inv_d = inv_blocks[:, :].rearrange("p (t c) -> p t c", t=NT)

        def diag(ap):
            return ap[:, 0:NT * BLK].rearrange("p (t c) -> p t c", t=NT)

        def on_diag(ap, q):
            return tiles(ap)[q * BLK:(q + 1) * BLK, :, q * BLK:(q + 1) * BLK]

        state = [wk(W_S)[:, i * P:(i + 1) * P] for i in range(3)]
        o_raw = wk(W_QGT)
        gate = wk(W_GATE)

        def from_state(t):
            return bank(2 + t % 2)[:, t * P:(t + 1) * P]

        def within(t):
            return bank(7 - t % 2)[:, t * P:(t + 1) * P]
        gates_f = wk(W_KTAIL)[0:16, :]
        q_rot, k_rot, rot_tmp = work1[:, 0:2, :], work1[:, 2:4, :], work1[:, 4:6, :]
        v_feat = work2[:, 0:2, :]
        rv_tok = work2[:, 2:4, :].rearrange("p a c -> p (a c)").rearrange("p (j d) -> p j d", j=NT)
        rgate = work2[:, 4:6, :]
        s_off = [0, 512, 896, 1152]
        s_all = work2[:, 6:9, :].rearrange("p a c -> p (a c)")
        ro_n = work2[:, 9:11, :].rearrange("p a c -> p (a c)").rearrange("p (j d) -> p j d", j=NT)
        ro_sq = work2[:, 11:13, :]
        h_tok = work2[:, 0:16, :].rearrange("p a c -> p (a c)").rearrange("p (t n) -> p t n", t=NT)
        fin_w = work1[:, 0:4, :].rearrange("p a c -> p (a c)")

        w_in_k = w_in.rearrange("(k p) c -> p k c", p=P)
        w_out_k = w_out.rearrange("(k p) c -> p k c", p=P)
        x_rows = x.rearrange("(t p) c -> p t c", p=P)
        out_rows = out.rearrange("(t p) c -> p t c", p=P)

        s_x = [sem(f"x_loaded{t}") for t in range(NT)]
        s_xres = [sem(f"x_again_loaded{n}") for n in range(4)]
        s_w = [sem(f"w_loaded{i}") for i in range(2)]
        s_ident = sem("ident_loaded")
        s_cst, s_rows, s_wg, s_pos, s_arow, s_dec, s_fin = (
            sem(n) for n in ("cst_loaded", "rows_loaded", "wg_loaded", "pos_loaded", "a_dt_loaded",
                             "decays_loaded", "final_w_loaded"))
        s_out = sem("out_stored")
        hi_ready, lo_ready, proj_done = sem("w_hi_ready"), sem("w_lo_ready"), sem("unit_projected")
        memsets, cols_mm, cols_ready = sem("memsets"), sem("cols_turned"), sem("cols_ready")
        x_sq, x_ms, x_rstd, x_scaled = sem("x_squared"), sem("x_mean"), sem("x_rstd"), sem("x_scaled")
        xt_mm, xhi_ready, xlo_ready = sem("x_turned"), sem("x_hi_ready"), sem("x_lo_ready")
        wg_hi_ready, wg_lo_ready, gates_mm = sem("wg_hi"), sem("wg_lo"), sem("gates_projected")
        gates_copied = sem("gates_copied")
        p_dve, p_act, p_mm, p_ready = sem("par_dve"), sem("par_act"), sem("cumsum_mm"), sem("par_ready")
        ug_ready, g_mm, dif_ready, dif_exp, decay_ready = (
            sem(n) for n in ("ug_ready", "decay_mm", "decay_log_ready", "decay_exp", "decay_ready"))
        dt_added = sem("dt_added")
        angle_ready, rope_arg, cos_arg, rope_ready = (
            sem(n) for n in ("angle_ready", "rope_arg", "cos_arg", "rope_ready"))
        dve_link, pool_link = sem("dve_link"), sem("pool_link")
        dve_link_gdn, dve_link_ret = sem("dve_link_gdn"), sem("dve_link_ret")
        par_ready, conv_par_ready = sem("head_par_ready"), sem("conv_par_ready")
        tap_done, conv_done, silu_done, gate_done = (
            sem(n) for n in ("tap_done", "conv_done", "silu_done", "gate_done"))
        tr_in, qk_sq, v_ready, ss_ready, r_ready, k_tok_ready, q_kept = (
            sem(n) for n in ("qkv_turned", "qk_squared", "v_ready", "k_norm2_ready", "k_norm_ready",
                             "k_tok_ready", "q_kept"))
        kk_ready, kk_mm, low_ready = (sem(n) for n in ("k_scaled_ready", "kk_mm", "lower_ready"))
        qs_mm, o_part, o_summed = sem("q_state_mm"), sem("o_part"), sem("o_summed")
        y_ready, inv_first, t1_mm, t1_ready, lvl_mm, lvl_ready = (
            sem(n) for n in ("y_ready", "inv_first", "t1_mm", "t1_ready", "level_mm", "level_ready"))
        uw_mm, w_ready, u_ready = sem("uw_mm"), sem("w_ready"), sem("u_ready")
        ws_mm, vn_ready, ktv_mm, st_ready, o_mm = (
            sem(n) for n in ("ws_mm", "vnew_ready", "ktv_mm", "state_ready", "o_mm"))
        o_sq, o_ms, o_rstd, on_ready, otr_mm, mix_done = (
            sem(n) for n in ("o_squared", "o_mean", "o_rstd", "o_normed", "o_turned", "mix_done"))
        rot_read, rot_done, rs_mm, rs_ready, vf_done, rgate_done, rvt_mm, rvt_ready = (
            sem(n) for n in ("rot_read", "rot_done", "ret_scores_mm", "ret_scores_ready", "v_feat_done",
                             "ret_gate_done", "ret_v_turned", "ret_v_ready"))
        ro_mm, ro_sqd, ro_ms, ro_rstd, ron_ready, rotr_mm, rmix_done = (
            sem(n) for n in ("ret_o_mm", "ret_o_squared", "ret_o_mean", "ret_o_rstd", "ret_o_normed",
                             "ret_o_turned", "ret_mix_done"))
        mhi_ready, mlo_ready, oproj_mm, h_ready, h_sq, h_ms, h_rstd, y_done = (
            sem(n) for n in ("mix_hi_ready", "mix_lo_ready", "out_projected", "h_ready", "h_squared",
                             "h_mean", "h_rstd", "y_done"))
        h_weighed, y_left_done = sem("h_weighed"), sem("y_left_done")

        magic = 1.5 * 2.0 ** 23
        c1, c2 = 6.28125, float(np.float32(2 * math.pi - 6.28125))
        c3 = float(np.float32(2 * math.pi - 6.28125 - c2))

        block = ctx.enter_context(nc.Block())

        @block.sync
        def _(sp):
            for t in range(NT):
                sp.dma_start(x_tok[:, t, :], x_rows[:, t, :]).then_inc(s_x[t], 16)

            def load_in(slot, col, wait):
                if wait is not None:
                    sp.wait_ge(lo_ready, wait)
                sp.dma_start(w_raw[:, slot, :].rearrange("p (k c) -> p k c", k=KT),
                             w_in_k[:, :, bass.ds(col, P)]).then_inc(s_w[slot], 16)

            for s in range(4):
                if s == 2:
                    sp.wait_ge(xt_mm, KT)
                    for r in range(RH):
                        sp.dma_start(mix[:, GH + 2 * r, :], decays[r, :, :]).then_inc(s_dec, 16)
                load_in(s % 2, GDN_COL + GROUP * s, None if s < 2 else 4 * s - 4)
            with sp.Fori(1, GH) as h:
                for s in range(4):
                    load_in(s % 2, GDN_COL + GROUP * s + h * P, 16 * h + 4 * s - 4)
            with sp.Fori(0, RH) as r:
                for i in range(8):
                    load_in(i % 2, GROUP * (i // 2) + P * (i % 2) + r * (2 * P),
                            32 * r + 4 * N_GDN_UNITS + 4 * i - 4)

            def load_out(n, kg, after=None):
                first = GH + 4 * kg if kg < 2 else 4 * (kg - 2)
                col = n * SEQ if after is None else after * SEQ + SEQ
                sp.wait_ge(lo_ready, 16 * n + 4 * OUT_U + 4 * kg - 4)
                sp.dma_start(w_raw[:, kg % 2, :].rearrange("p (k c) -> p k c", k=4),
                             w_out_k[:, first:first + 4, bass.ds(col, SEQ)]).then_inc(s_w[kg % 2], 16)

            for kg in range(4):
                load_out(0, kg)
            sp.wait_ge(rmix_done, 2 * RH + 1)
            for n in range(4):
                sp.dma_start(h_tok[:, :, n * SEQ:(n + 1) * SEQ],
                             x_rows[:, :, n * SEQ:(n + 1) * SEQ]).then_inc(s_xres[n], 16)
            sp.dma_start(fin_w, final_norm_w.partition_broadcast(P)).then_inc(s_fin, 16)
            with sp.Fori(0, 3) as before:
                for kg in range(4):
                    load_out(before + 1, kg, before)
            for t in range(NT):
                sp.wait_ge(y_done, t + 1)
                sp.wait_ge(y_left_done, t + 1)
                sp.dma_start(out_rows[:, t, :], h_tok[:, t, :]).then_inc(s_out, 16)
            sp.wait_ge(s_out, 16 * NT)

        @block.tensor
        def _(pe):
            mm = pe.matmul

            class Unit:

                def __init__(self, first, bank_free):
                    self.first, self.bank_free, self.m = first, bank_free, 0

                def fill(self, n):
                    for _ in range(n):
                        i, m = divmod(self.m, UNIT_MM)
                        kt, pas = divmod(m, 3)
                        slot = i % 2
                        if m == 0:
                            self.bank_free(i)
                        if m % 12 == 0:
                            pe.wait_ge(lo_ready, self.first * 4 + (4 * i + m // 12 + 1))
                        w = (w_hi, w_hi, w_lo)[pas][:, slot, kt * P:(kt + 1) * P]
                        a = (act_hi, act_lo, act_hi)[pas][:, kt, :]
                        op = mm(bank(slot), w, a, start=m == 0, stop=m == UNIT_MM - 1)
                        if m == UNIT_MM - 1:
                            op.then_inc(proj_done, 1)
                        self.m += 1

            pe.wait_ge(s_ident, 16)
            for t in range(NT):
                if t == NT - 1:
                    pe.wait_ge(s_rows, 48)
                    pe.transpose(bank(7)[:, 0:113], rows[0:113, :], ident[0:113, 0:113]).then_inc(cols_mm, 1)
                pe.wait_ge(x_scaled, t + 1)
                for kt in range(5):
                    op = pe.transpose(tiles(bank(2 + kt))[:, t, :], x_tok[:, t, kt * P:(kt + 1) * P], ident)
                    if t == NT - 1:
                        op.then_inc(xt_mm, 1)

            def turn_x(kt):
                pe.wait_ge(xlo_ready, kt - 4)
                for t in range(NT):
                    op = pe.transpose(tiles(bank(2 + kt % 5))[:, t, :], x_tok[:, t, kt * P:(kt + 1) * P],
                                      ident)
                op.then_inc(xt_mm, 1)

            head0 = Unit(0, lambda i: None)
            for kt in range(KT):
                if kt >= 1 and kt + 4 < KT:
                    turn_x(kt + 4)
                pe.wait_ge(xlo_ready, kt + 1)
                head0.fill(3)

            pe.wait_ge(wg_lo_ready, 1)
            for kt in range(KT):
                for pas in range(3):
                    op = mm(bank(2)[0:16, :], (wg_hi, wg_hi, wg_lo)[pas][:, kt, :],
                            (act_hi, act_lo, act_hi)[pas][:, kt, :],
                            start=kt == 0 and pas == 0, stop=kt == KT - 1 and pas == 2)
            op.then_inc(gates_mm, 1)

            def head0_bank(i):
                if i >= 2:
                    pe.wait_ge(conv_done, i - 1)

            head0.bank_free = head0_bank
            head0.fill(8)
            pe.wait_ge(gates_copied, 1)
            for t in range(NT):
                op = pe.transpose(bank(6)[:, 16 * t:16 * t + 16], gates_f[:, t * P:(t + 1) * P],
                                  ident[0:16, 0:16])
            op.then_inc(gates_mm, 1)
            head0.fill(22)
            pe.wait_ge(s_cst, 16)
            pe.wait_ge(p_dve, 1)
            g_all = g_log[:, :, :].rearrange("p h t -> p (h t)")
            mm(bank(3)[:, 0:GH * NT], causal, g_all, start=True, stop=True)
            mm(bank(3)[:, GH * NT:2 * GH * NT], ones[:, :], g_all, start=True, stop=True).then_inc(p_mm, 1)
            head0.fill(UNIT_MM - 30)
            for e in range(GH):
                pe.wait_ge(ug_ready, e + 1)
                if e >= 2:
                    pe.wait_ge(dif_ready, e - 1)
                mm(bank(4 + e % 2), ones[:, :], ys[e % 2], start=True, stop=True).then_inc(g_mm, 1)
                head0.fill(10)
            head0.fill(2 * UNIT_MM - 10 * GH)
            pe.wait_ge(dif_ready, GH)

            def gdn_head(h, unit, per):
                fill = unit.fill
                for s in range(3):
                    pe.wait_ge(silu_done, 3 * h + (s + 1))
                    for t in range(NT):
                        op = pe.transpose(tiles(bank(2 + s))[:, t, :], conv[:, s, t * P:(t + 1) * P], ident)
                    op.then_inc(tr_in, 1)
                    if s == 1:
                        fill(per)
                pe.wait_ge(mix_done, h + 1)
                for b, rhs in ((5, 1), (6, 0)):
                    for t in range(NT):
                        op = mm(tiles(bank(b))[:, t, :], tiles(conv[:, 1, :])[:, t, :],
                                tiles(conv[:, rhs, :])[:, t, :], start=True, stop=True)
                    op.then_inc(kk_mm, 1)
                fill(6 * per)
                for n in range(1, LEVELS):
                    pe.wait_ge(y_ready, 7 * h + (n + 1))
                    if n == 1:
                        pe.wait_ge(inv_first, h + 1)
                        pe.wait_ge(v_ready, h + 1)
                    else:
                        pe.wait_ge(lvl_ready, 7 * h + (n - 1 if n < 6 else 6))
                    for t in range(NT):
                        if n < 5:
                            op = mm(diag(bank(4))[:, t, :], tiles(ys[n % 2])[:, t, :], inv_d[:, t, :],
                                    start=True, stop=True)
                        else:
                            op = mm(tiles(bank(4))[:, t, :], tiles(ys[n % 2])[:, t, :], tiles(inv)[:, t, :],
                                    start=True, stop=True)
                    op.then_inc(t1_mm, 1)
                    fill(4 if n < 5 else 6)
                    pe.wait_ge(t1_ready, 6 * h + n)
                    if n == 6:
                        pe.wait_ge(lvl_ready, 7 * h + 6)
                    if n < 6:
                        for t in range(NT):
                            part = tiles if n == 5 else diag
                            op = mm(part(bank(5))[:, t, :], tiles(inv_t)[:, t, :], part(t1)[:, t, :],
                                    start=True, stop=True)
                        op.then_inc(lvl_mm, 1)
                    if n >= 5:
                        for t in range(NT):
                            op = mm(tiles(bank(6))[:, t, :], tiles(t1)[:, t, :], tiles(inv_t)[:, t, :],
                                    start=True, stop=True)
                        op.then_inc(lvl_mm, 1)
                    fill((0, 8, 8, 8, 10, 7, 6)[n])
                pe.wait_ge(lvl_ready, 7 * h + 7)
                pe.wait_ge(kk_ready, 2 * h + 2)
                for t in range(NT):
                    op = mm(tiles(bank(2))[:, t, :], tiles(inv_t)[:, t, :], tiles(vtok)[:, t, :],
                            start=True, stop=True)
                op.then_inc(uw_mm, 1)
                for t in range(NT):
                    op = mm(tiles(bank(6))[:, t, :], tiles(kbg)[:, t, :], tiles(inv_t)[:, t, :],
                            start=True, stop=True)
                op.then_inc(uw_mm, 1)
                fill(per)
                for t in range(NT):
                    tt = slice(t * P, (t + 1) * P)
                    if t > 0:
                        pe.wait_ge(st_ready, 3 * h + t)
                        if t == 1:
                            pe.wait_ge(w_ready, h + 1)
                            pe.wait_ge(q_kept, h + 1)
                        mm(bank(4)[:, tt], w_t[:, tt], state[t - 1], start=True, stop=True).then_inc(ws_mm, 1)
                        mm(from_state(t), q_keep[:, tt], state[t - 1], start=True, stop=True).then_inc(qs_mm, 1)
                        fill(per)
                    pe.wait_ge(vn_ready, 4 * h + (t + 1))
                    if t < NT - 1:
                        mm(bank(5)[:, tt], ktail[:, tt], vnew[:, tt], start=True, stop=True).then_inc(ktv_mm, 1)
                    if t == 0:
                        pe.wait_ge(low_ready, 2 * h + 2)
                    mm(within(t), attn_t[:, tt], vnew[:, tt], start=True, stop=True).then_inc(o_mm, 1)
                    fill(per)

            def gdn_body(h, unit):
                gdn_head(h, unit, 6)
                unit.fill(18)
                pe.wait_ge(on_ready, h + 1)
                for t in range(NT):
                    op = pe.transpose(tiles(bank(6))[:, t, :], tiles(o_n)[:, t, :], ident)
                op.then_inc(otr_mm, 1)
                unit.fill(4 * UNIT_MM - unit.m)

            def gdn_bank(h):
                def free(i):
                    if i == 1:
                        pe.wait_ge(gate_done, h + 1)
                    else:
                        pe.wait_ge(conv_done, 3 * h + (3, 0, 4, 5)[i])
                return free

            def ret_bank(r):
                def free(i):
                    if i < 2:
                        if isinstance(r, int) and r == 0:
                            pe.wait_ge(*((conv_done, 3 * GH), (gate_done, GH))[i])
                        else:
                            pe.wait_ge(rgate_done, 2 * r + (i - 1))
                    elif i < 6:
                        pe.wait_ge(rot_read, 4 * r + (i - 1))
                    else:
                        pe.wait_ge(vf_done, 2 * r + (i - 5))
                return free

            with pe.Fori(0, GH - 1) as h:
                gdn_body(h, Unit(4 * h + 4, gdn_bank(h)))
            gdn_body(GH - 1, Unit(N_GDN_UNITS, ret_bank(0)))

            def ret_scores(r, unit):
                unit.fill(26)
                for j in range(NT):
                    if j == 0:
                        pe.wait_ge(rot_done, 4 * r + 4)
                        pe.wait_ge(rmix_done, 2 * r + 1)
                    n = SEQ - j * P
                    for d in range(2):
                        op = mm(bank(4 + j)[:, 0:n], k_rot[:, d, j * P:(j + 1) * P], q_rot[:, d, j * P:],
                                start=d == 0, stop=d == 1)
                    op.then_inc(rs_mm, 1)
                    unit.fill(24)
                for d in range(2):
                    pe.wait_ge(vf_done, 2 * r + (d + 1))
                    if d == 0:
                        pe.wait_ge(rs_ready, 4 * r + 2)
                    for j in range(NT):
                        op = pe.transpose(bank(4 + j // 2)[:, (j % 2) * RDK + d * P:(j % 2) * RDK + (d + 1) * P],
                                          v_feat[:, d, j * P:(j + 1) * P], ident)
                op.then_inc(rvt_mm, 1)
                unit.fill(8 * UNIT_MM - unit.m)

            def ret_out(r, fill, after=(6, 6, 6, 6)):
                pe.wait_ge(rs_ready, 4 * r + 4)
                pe.wait_ge(rvt_ready, 2 * r + 2)
                for i in range(NT):
                    for j in range(i + 1):
                        at = s_off[j] + (i - j) * P
                        op = mm(bank(6 + i // 2)[:, (i % 2) * RDK:(i % 2 + 1) * RDK], s_all[:, at:at + P],
                                rv_tok[:, j, :], start=j == 0, stop=j == i)
                    if i % 2:
                        op.then_inc(ro_mm, 1)
                    fill(after[i])
                fill(24)
                for d in range(2):
                    pe.wait_ge(ron_ready, 2 * r + 2)
                    for t in range(NT):
                        op = pe.transpose(tiles(bank(4 + d))[:, t, :], ro_n[:, t, d * P:(d + 1) * P], ident)
                    op.then_inc(rotr_mm, 1)

            pe.wait_ge(mix_done, GH + 1)
            with pe.Fori(0, RH - 1) as r:
                unit = Unit(8 * r + N_GDN_UNITS, ret_bank(r))
                unit.m = 4 * UNIT_MM
                ret_scores(r, unit)
                unit = Unit(8 * r + (N_GDN_UNITS + 8), ret_bank(r + 1))
                ret_out(r, unit.fill)
                unit.fill(4 * UNIT_MM - unit.m)
            last = RH - 1
            unit = Unit(8 * last + N_GDN_UNITS, ret_bank(last))
            unit.m = 4 * UNIT_MM
            ret_scores(last, unit)

            def out_mm(kg, kt, t, pas):
                a = (act_hi, act_lo, act_hi)[pas][:, 4 * kg + kt, t * P:(t + 1) * P]
                w = (w_hi, w_hi, w_lo)[pas][:, kg % 2, kt * SEQ:(kt + 1) * SEQ]
                return mm(bank(t), a, w, start=kg == 0 and kt == 0 and pas == 0,
                          stop=kg == 3 and kt == 3 and pas == 2)

            class Early:
                m = 0

                def fill(self, n):
                    for _ in range(n):
                        kg, m = divmod(self.m, UNIT_MM)
                        kt, rest = divmod(m, 12)
                        t, pas = divmod(rest, 3)
                        if self.m < 4 and self.m == 0:
                            pe.wait_ge(rgate_done, 2 * RH)
                        if rest == 0:
                            pe.wait_ge(lo_ready, 4 * OUT_U + 4 * kg + kt + 1)
                            pe.wait_ge(mlo_ready, 4 * kg + kt + 1)
                        op = out_mm(kg, kt, t, pas)
                        if m == UNIT_MM - 1:
                            op.then_inc(proj_done, 1)
                        self.m += 1

            early = Early()
            ret_out(last, early.fill, (0, 0, 6, 18))
            early.fill(3 * UNIT_MM - early.m)

            def last_group(n):
                pe.wait_ge(lo_ready, 16 * n + (4 * OUT_U + 16))
                for t in range(NT):
                    for kt in range(4):
                        for pas in range(3):
                            op = out_mm(3, kt, t, pas)
                    op.then_inc(oproj_mm, 1)

            pe.wait_ge(mlo_ready, 16)
            last_group(0)
            with pe.Fori(1, 4) as n:
                for kg in range(3):
                    for kt in range(4):
                        pe.wait_ge(lo_ready, 16 * n + (4 * OUT_U + 4 * kg + kt + 1))
                        for t in range(NT):
                            if kg == 0 and kt == 0:
                                pe.wait_ge(h_ready, 4 * n + (t - 3))
                            for pas in range(3):
                                op = out_mm(kg, kt, t, pas)
                    op.then_inc(proj_done, 1)
                last_group(n)

        @block.scalar
        def _(act):
            A = act.activation
            act.dma_start(cst[:, 0:P], consts[:, 0:P]).then_inc(s_ident, 16)
            act.dma_start(rows[0:96, :], conv_w.rearrange("t (c p) -> (t c) p", p=P)).then_inc(s_rows, 16)
            act.dma_start(rows[96:112, :], norm_w.rearrange("(k p) -> k p", p=P)).then_inc(s_rows, 16)
            act.dma_start(rows[112:113, :], gdn_norm_w.rearrange("(a p) -> a p", a=1)).then_inc(s_rows, 16)
            act.dma_start(a_row[:, :], a_log.partition_broadcast(P)).then_inc(s_arow, 16)
            act.dma_start(dt_row[:, :], dt_bias.partition_broadcast(P)).then_inc(s_arow, 16)
            wg_raw = work2[:, W_KBG, 0:KT * 16].rearrange("p (k c) -> p k c", k=KT)

            def tap3(s):
                A(conv[:, s, :], bank(s % 2), ACT.Copy, scale=conv_par[:, 3, s:s + 1]).then_inc(tap_done, 1)

            def silu(s):
                A(conv[:, s, :], conv[:, s, :], ACT.Silu).then_inc(silu_done, 1)

            for t in range(NT):
                act.wait_ge(s_x[t], 16)
                if t > 0:
                    act.wait_ge(x_sq, t)
                A(work2[:, 0:2, :].rearrange("p a c -> p (a c)"), x_tok[:, t, 0:D // 2], ACT.Square,
                  accum_out=stat[:, 0, t:t + 1]).then_inc(x_sq, 1)
                if t == 0:
                    act.dma_start(cst[:, P:], consts[:, P:]).then_inc(s_cst, 16)
                    act.dma_start(work2[:, W_GATE, :].bitcast(I32),
                                  positions.partition_broadcast(P)).then_inc(s_pos, 16)
                    act.dma_start(wg_raw, w_in_k[:, :, GATE_COL:GATE_COL + 16]).then_inc(s_wg, 16)

            def split_hi(u, pair, i, p):
                if p == 0:
                    act.wait_ge(s_w[i % 2], 16 * pair + 16 * (i // 2 + 1))
                    if not (isinstance(u, int) and u + i < 2):
                        act.wait_ge(proj_done, u + (i - 1))
                at = slice(p * PIECE, (p + 1) * PIECE)
                A(w_hi[:, i % 2, at], w_raw[:, i % 2, at], ACT.Copy).then_inc(hi_ready, 1)

            split_hi(0, 0, 0, 0)
            act.wait_ge(cols_mm, 1)
            A(cols[:, 0:113], bank(7)[:, 0:113], ACT.Copy).then_inc(cols_ready, 1)
            act.wait_ge(cols_ready, 1)
            for kt in range(KT):
                act.wait_ge(xt_mm, kt + 1)
                A(act_hi[:, kt, :], bank(2 + kt % 5), ACT.Copy,
                  scale=cols[:, 96 + kt:97 + kt]).then_inc(xhi_ready, 1)
                if kt < 3:
                    split_hi(0, 0, 0, kt + 1)
                if kt % 4 == 3:
                    split_hi(0, 0, 1, kt // 4)
            act.wait_ge(s_wg, 16)
            A(wg_hi[:, :, :], wg_raw, ACT.Copy).then_inc(wg_hi_ready, 1)
            for p in range(4):
                split_hi(0, 0, 2, p)
            act.wait_ge(conv_par_ready, 1)
            tap3(0)
            act.wait_ge(rope_arg, 1)
            A(rope_sin[:, :], rope_sin[:, :], ACT.Sin).then_inc(rope_ready, 1)
            act.wait_ge(cos_arg, 1)
            A(rope_cos[:, :], rope_cos[:, :], ACT.Sin).then_inc(rope_ready, 1)


            act.wait_ge(gates_mm, 1)
            A(gates_f, bank(2)[0:16, :], ACT.Copy).then_inc(gates_copied, 1)
            act.wait_ge(gates_mm, 2)
            gates = bank(6)[:, 0:16 * NT].rearrange("p (t c) -> p c t", c=16)
            sm = [small[:, i, :].rearrange("p (h t) -> p h t", h=GH) for i in range(6)]
            A(sm[0], gates[:, 0:8, :], ACT.Exp, scale=-1.0).then_inc(p_act, 1)
            act.wait_ge(dt_added, 1)
            A(sm[2], sm[1], ACT.Abs).then_inc(p_act, 1)
            act.wait_ge(p_act, 2)
            A(sm[2], sm[2], ACT.Exp, scale=-1.0).then_inc(p_act, 1)
            act.wait_ge(p_act, 3)
            A(sm[2], sm[2], ACT.Ln, bias=1.0).then_inc(p_act, 1)
            act.wait_ge(s_arow, 32)
            A(a_row[:, :], a_row[:, :], ACT.Exp).then_inc(p_act, 1)

            act.wait_ge(p_mm, 1)
            cum = bank(3)[:, 0:GH * NT].rearrange("p (h t) -> p h t", h=GH)
            tot = bank(3)[:, GH * NT:2 * GH * NT].rearrange("p (h t) -> p h t", h=GH)
            A(head_par[:, :, 8:12], cum, ACT.Exp).then_inc(p_act, 1)
            A(head_par[:, :, 16:20], tot, ACT.Exp).then_inc(p_act, 1)
            act.wait_ge(p_dve, 2)
            A(head_par[:, :, 12:16], sm[3], ACT.Exp).then_inc(p_ready, 1)

            for e in range(GH):
                split_hi(0, 0, 3 + e // 4, e % 4)
                if e in (1, 5):
                    s = 1 + e // 4
                    act.wait_ge(proj_done, s + 1)
                    tap3(s)
                act.wait_ge(dif_ready, e + 1)
                A(wk(W_X + e % 2), wk(W_X + e % 2), ACT.Exp).then_inc(dif_exp, 1)
            for s in range(3):
                act.wait_ge(conv_done, s + 1)
                silu(s)

            def gdn_body(h, unit0, pair, following):
                hi = lambda k: split_hi(unit0, pair, 1 + k // 4, k % 4)
                act.wait_ge(proj_done, 4 * h + 4)
                act.wait_ge(mix_done, h + 1)
                A(gate, bank(1), ACT.Silu).then_inc(gate_done, 1)
                hi(0)
                for s in range(2):
                    act.wait_ge(tr_in, 3 * h + (s + 1))
                    A(ys[s], bank(2 + s), ACT.Square).then_inc(qk_sq, 1)
                A(ktok, bank(3), ACT.Copy).then_inc(k_tok_ready, 1)
                A(q_keep, conv[:, 0, :], ACT.Copy).then_inc(q_kept, 1)
                hi(1)
                hi(2)
                hi(3)
                for n in range(1, LEVELS):
                    act.wait_ge(t1_mm, 6 * h + n)
                    width = SEQ if n >= 5 else NT * BLK
                    A(t1[:, 0:width], bank(4)[:, 0:width], ACT.Copy).then_inc(t1_ready, 1)
                    hi(3 + n)
                    if following == "gdn":
                        if n == 1:
                            act.wait_ge(proj_done, unit0 + 1)
                            act.wait_ge(conv_par_ready, h + 2)
                            act.wait_ge(q_kept, h + 1)
                            tap3(0)
                        if n == 3:
                            act.wait_ge(conv_done, 3 * h + 4)
                            silu(0)
                        if n == 5:
                            act.wait_ge(proj_done, unit0 + 2)
                            tap3(1)
                act.wait_ge(uw_mm, 2 * h + 2)
                A(w_t, bank(6), ACT.Copy).then_inc(w_ready, 1)
                hi(10)
                if following == "gdn":
                    act.wait_ge(conv_done, 3 * h + 5)
                    silu(1)
                hi(11)
                if following == "gdn":
                    act.wait_ge(proj_done, unit0 + 3)
                    tap3(2)
                hi(12)
                hi(13)
                hi(14)
                act.wait_ge(o_summed, 4 * h + 4)
                A(ys[0], o_raw, ACT.Square).then_inc(o_sq, 1)
                hi(15)
                if following == "gdn":
                    act.wait_ge(conv_done, 3 * h + 6)
                    silu(2)

            with act.Fori(0, GH - 1) as h:
                gdn_body(h, 4 * h + 4, 2 * h + 2, "gdn")
            gdn_body(GH - 1, N_GDN_UNITS, N_GDN_UNITS // 2, "ret")

            def ret_a(r, unit0, pair, n_pieces=16):
                hi = lambda k: split_hi(unit0, pair, 5 + k // 4, k % 4)
                for k in range(n_pieces):
                    hi(k)
                    if k == 5 or k == 9:
                        d = (k - 5) // 4
                        act.wait_ge(proj_done, unit0 + (5 + d))

                        A(v_feat[:, d, :], bank(d), ACT.Copy).then_inc(vf_done, 1)
                act.wait_ge(proj_done, unit0 + 7)
                A(rgate[:, 0, :], bank(0), ACT.Silu).then_inc(rgate_done, 1)
                act.wait_ge(rvt_mm, r + 1)
                for b in range(2):
                    A(work2[:, 2 + b, :], bank(4 + b), ACT.Copy).then_inc(rvt_ready, 1)
                act.wait_ge(proj_done, unit0 + 8)
                A(rgate[:, 1, :], bank(1), ACT.Silu).then_inc(rgate_done, 1)

            def ret_b(r, hi):
                for b in range(2):
                    act.wait_ge(ro_mm, 2 * r + (b + 1))
                    A(ro_sq[:, b, :], bank(6 + b), ACT.Square).then_inc(ro_sqd, 1)
                    hi(b)

            act.wait_ge(mix_done, GH + 1)
            with act.Fori(0, RH - 1) as r:
                ret_a(r, 8 * r + N_GDN_UNITS, 4 * r + N_GDN_UNITS // 2)
                hi = lambda k: split_hi(8 * r + (N_GDN_UNITS + 8), 4 * r + (N_GDN_UNITS // 2 + 4),
                                        1 + k // 4, k % 4)
                ret_b(r, hi)
                for k in range(2, 16):
                    hi(k)
            last = RH - 1
            ret_a(last, 8 * last + N_GDN_UNITS, 4 * last + N_GDN_UNITS // 2)

            def mix_hi(s):
                if s >= GH:
                    act.wait_ge(rmix_done, s - GH + 2)
                A(act_hi[:, s, :], mix[:, s, :], ACT.Copy).then_inc(mhi_ready, 1)

            for s in range(6):
                mix_hi(s)
            hi = lambda k: split_hi(OUT_U, OUT_U // 2, 1 + k // 4, k % 4)
            ret_b(last, hi)
            for s in range(6, 14):
                mix_hi(s)
                hi(s - 4)
            hi(10)
            hi(11)
            mix_hi(14)
            mix_hi(15)
            for k in range(12, 16):
                hi(k)

            def square_h(n, t):
                act.wait_ge(h_ready, 4 * n + (t + 1))
                if not (isinstance(n, int) and n + t == 0):
                    act.wait_ge(h_sq, 4 * n + t)
                A(work1[:, 4, :], h_tok[:, t, bass.ds(n * SEQ, SEQ)], ACT.Square,
                  accum_out=small[:, 0, bass.ds(4 * t + n, 1)]).then_inc(h_sq, 1)

            for t in range(NT):
                square_h(0, t)
            def hi_out(n, k):
                i, p = 1 + k // 4, k % 4
                if p == 0:
                    act.wait_ge(s_w[i % 2], 32 * n + (8 * OUT_U + 16 * (i // 2) + 16))
                    if i == 1:
                        act.wait_ge(oproj_mm, 4 * n)
                    else:
                        act.wait_ge(proj_done, 3 * n + (OUT_U + i - 1))
                at = slice(p * PIECE, (p + 1) * PIECE)
                A(w_hi[:, i % 2, at], w_raw[:, i % 2, at], ACT.Copy).then_inc(hi_ready, 1)

            with act.Fori(1, 3) as n:
                for k in range(16):
                    hi_out(n, k)
                for t in range(NT):
                    square_h(n, t)
            for k in range(12):
                hi_out(3, k)
            for t in range(NT):
                square_h(3, t)
                act.wait_ge(h_rstd, t + 1)
                A(h_tok[:, t, 0:2 * SEQ], h_tok[:, t, 0:2 * SEQ], ACT.Copy,
                  scale=stat[:, 2, t:t + 1]).then_inc(y_left_done, 1)

        @block.vector
        def _(dve):
            TT, TS, STT = dve.tensor_tensor, dve.tensor_scalar, dve.scalar_tensor_tensor
            link = Links(dve, dve_link)
            dve.memset(ones[:, :], 1.0).then_inc(memsets, 1)
            dve.memset(half[:, 0:8], -0.5).then_inc(memsets, 1)
            dve.memset(half[:, 8:16], 0.5).then_inc(memsets, 1)
            dve.memset(stat[:, 0, 14:15], 0.0).then_inc(mix_done, 1)
            dve.memset(stat[:, 0, 15:16], 0.0).then_inc(rmix_done, 1)

            def scale_x(t):
                dve.wait_ge(x_rstd, t + 1)
                TS(x_tok[:, t, :], x_tok[:, t, :], stat[:, 3, t:t + 1], math.sqrt(D), ALU.mult,
                   ALU.mult).then_inc(x_scaled, 1)

            for t in range(NT):
                dve.wait_ge(s_x[t], 16)
                link(dve.tensor_tensor_reduce(work2[:, 2:4, :].rearrange("p a c -> p (a c)"),
                                              x_tok[:, t, D // 2:], x_tok[:, t, D // 2:], 1.0, 0.0,
                                              ALU.mult, ALU.add, stat[:, 1, t:t + 1]))
                dve.wait_ge(x_sq, t + 1)
                TS(stat[:, 2, t:t + 1], stat[:, 0, t:t + 1], stat[:, 1, t:t + 1], D * EPS, ALU.add,
                   ALU.add).then_inc(x_ms, 1)
                if t > 0:
                    scale_x(t - 1)
            scale_x(NT - 1)

            def split_lo(u, i, p):
                dve.wait_ge(hi_ready, 4 * u + (4 * i + p + 1))
                at = slice(p * PIECE, (p + 1) * PIECE)
                TT(w_lo[:, i % 2, at], w_raw[:, i % 2, at], w_hi[:, i % 2, at].bitcast(F32),
                   ALU.subtract).then_inc(lo_ready, 1)

            split_lo(0, 0, 0)
            dve.wait_ge(cols_ready, 1)
            angle, turns, angle_cos = wk(W_QGTOK), wk(W_KT), rope_cos[:, :]
            cosine_steps = iter((
                lambda: TS(turns, angle, 1.0 / (2 * math.pi), 0.25, ALU.mult, ALU.add),
                lambda: TS(turns, turns, magic, None, ALU.add),
                lambda: TS(turns, turns, -magic, None, ALU.add),
                lambda: STT(angle_cos, turns, -c1, angle, ALU.mult, ALU.add),
                lambda: STT(angle_cos, turns, -c2, angle_cos, ALU.mult, ALU.add),
                lambda: STT(angle_cos, turns, -c3, angle_cos, ALU.mult, ALU.add),
                lambda: TS(angle_cos, angle_cos, 0.5 * math.pi, 3.1415925, ALU.add, ALU.min)))
            for kt in range(KT):
                dve.wait_ge(xhi_ready, kt + 1)
                STT(act_lo[:, kt, :], bank(2 + kt % 5), cols[:, 96 + kt:97 + kt],
                    act_hi[:, kt, :].bitcast(F32), ALU.mult, ALU.subtract).then_inc(xlo_ready, 1)
                if kt < 3:
                    split_lo(0, 0, kt + 1)
                if kt % 4 == 3:
                    split_lo(0, 1, kt // 4)
                elif kt in (6, 8, 10, 12, 14):
                    if kt == 6:
                        dve.wait_ge(angle_ready, 1)
                    link(next(cosine_steps)())

            def conv_weights(h):
                if not isinstance(h, int):
                    dve.wait_ge(conv_done, 3 * h)
                src = cols[:, 0:96].rearrange("p (t s c) -> p t s c", t=4, s=3)[:, :, :, bass.ds(h, 1)]
                dve.tensor_copy(conv_par[:, :, :].unsqueeze(3), src).then_inc(conv_par_ready, 1)

            def tap(s, j, link):
                back = 3 - j
                op = STT(conv[:, s, back:], bank(s % 2)[:, 0:SEQ - back], conv_par[:, j, s:s + 1],
                         conv[:, s, back:], ALU.mult, ALU.add)
                if j == 2:
                    op.then_inc(conv_done, 1)
                else:
                    link(op)

            wg_raw = work2[:, W_KBG, 0:KT * 16].rearrange("p (k c) -> p k c", k=KT)
            dve.wait_ge(wg_hi_ready, 1)
            TT(wg_lo[:, :, :], wg_raw, wg_hi[:, :, :].bitcast(F32), ALU.subtract).then_inc(wg_lo_ready, 1)
            for p in range(4):
                split_lo(0, 2, p)
            for step in cosine_steps:
                link(step())
            TS(angle_cos, angle_cos, -3.1415925, None, ALU.max).then_inc(cos_arg, 1)
            conv_weights(0)
            dve.wait_ge(tap_done, 1)
            for j in range(3):
                tap(0, j, link)



            sm = [small[:, i, :].rearrange("p (h t) -> p h t", h=GH) for i in range(6)]
            gates = bank(6)[:, 0:16 * NT].rearrange("p (t c) -> p c t", c=16)
            dve.wait_ge(s_arow, 32)
            dve.wait_ge(p_act, 1)
            TT(sm[1], gates[:, 8:16, :], over_free(dt_row[:, :], NT), ALU.add).then_inc(dt_added, 1)
            link(TS(sm[0], sm[0], 1.0, None, ALU.add))
            link(dve.reciprocal(head_par[:, :, 0:4], sm[0]))
            TS(head_par[:, :, 4:8], head_par[:, :, 0:4], -1.0, None, ALU.mult).then_inc(p_ready, 1)
            dve.wait_ge(p_act, 5)
            link(STT(sm[4], sm[1], 0.0, sm[2], ALU.max, ALU.add))
            STT(g_log[:, :, :], sm[4], -1.0, over_free(a_row[:, :], NT), ALU.mult, ALU.mult).then_inc(p_dve, 1)
            dve.wait_ge(p_mm, 1)
            cum = bank(3)[:, 0:GH * NT].rearrange("p (h t) -> p h t", h=GH)
            tot = bank(3)[:, GH * NT:2 * GH * NT].rearrange("p (h t) -> p h t", h=GH)
            dve.wait_ge(p_act, 7)
            link(dve.tensor_copy(g_cum[:, :, :], cum))
            link(TT(sm[5], tot, g_cum[:, :, :], ALU.subtract))
            TS(sm[3], sm[5], 0.0, None, ALU.min).then_inc(p_dve, 1)


            def decay_in(e):
                if e >= 2:
                    dve.wait_ge(g_mm, e - 1)
                TT(tiles(ys[e % 2]), over_tiles(causal), over_free(g_log[:, e, :]),
                   ALU.mult).then_inc(ug_ready, 1)

            decay_in(0)
            for e in range(GH):
                if e + 1 < GH:
                    decay_in(e + 1)
                dve.wait_ge(g_mm, e + 1)
                if e >= 2:
                    dve.wait_ge(decay_ready, e - 1)
                dif = wk(W_X + e % 2)
                link(TT(tiles(dif), tiles(bank(4 + e % 2)), over_free(g_cum[:, e, :]), ALU.subtract))
                TS(dif, dif, 0.0, None, ALU.min).then_inc(dif_ready, 1)
                split_lo(0, 3 + e // 4, e % 4)
                if e in (1, 5):
                    s = 1 + e // 4
                    dve.wait_ge(tap_done, s + 1)
                    for j in range(3):
                        tap(s, j, link)

            dve.wait_ge(p_ready, 2)
            dve.wait_ge(rope_ready, 2)

            def rot(r, i, first_wait):
                dst = (q_rot, k_rot)[i // 2]
                if i == 0:
                    first_wait()
                dve.wait_ge(proj_done, 8 * r + (N_GDN_UNITS + 1 + i))
                if i % 2 == 0:
                    a, b = dst[:, 0, :], dst[:, 1, :]
                else:
                    if i == 3:
                        dve.wait_ge(rot_done, 4 * r + 2)
                    elif not isinstance(r, int):
                        dve.wait_ge(rot_done, 4 * r)
                    a, b = rot_tmp[:, 1, :], rot_tmp[:, 0, :]
                TT(a, bank(i % 2), rope_cos[:, :], ALU.mult)
                TT(b, bank(i % 2), rope_sin[:, :], ALU.mult).then_inc(rot_read, 1)

            def gdn_body(h, unit0, following):
                glink = Links(dve, dve_link_gdn, DVE_GDN_LINKS * h)
                lo = lambda k: split_lo(unit0, 1 + k // 4, k % 4)
                dve.wait_ge(mix_done, h + 1)
                dve.tensor_copy(par[:, :].unsqueeze(1), head_par[:, bass.ds(h, 1), :]).then_inc(par_ready, 1)
                if following == "gdn":
                    conv_weights(h + 1)
                eg = par[:, 8:12]
                lo(0)
                for s in (1, 0):
                    dve.wait_ge(qk_sq, 2 * h + 2) if s == 1 else None
                    glink(dve.tensor_reduce(stat[:, 0, 4 * s:4 * s + 4], tiles(ys[s]), AX.X, ALU.add))
                TS(k_norm2, stat[:, 0, 4:8], P * EPS, None, ALU.add).then_inc(ss_ready, 1)
                TS(q_eps, stat[:, 0, 0:4], P * EPS, EPS * P, ALU.add, ALU.mult)
                dve.wait_ge(ss_ready, h + 1)
                glink(dve.reciprocal(stat[:, 3, 0:4], k_norm2))
                dve.wait_ge(par_ready, h + 1)
                glink(TT(beta_both.rearrange("p (a t) -> p a t", a=2),
                         par[:, 0:8].rearrange("p (a t) -> p a t", a=2),
                         stat[:, 3, 0:4].unsqueeze(1).to_broadcast([P, 2, NT]), ALU.mult))
                lo(1)
                decay = mix[:, bass.ds(h, 1), :].rearrange("p a (t c) -> p (a t) c", t=NT)
                dve.wait_ge(decay_ready, GH)
                dve.wait_ge(kk_mm, 2 * h + 1)
                for t in range(NT):
                    op = STT(tiles(lower_t)[:, t, :], tiles(bank(5))[:, t, :], beta_k[:, t:t + 1],
                             decay[:, t, :], ALU.mult, ALU.mult)
                    op.then_inc(low_ready, 1) if t == NT - 1 else None
                dve.wait_ge(kk_mm, 2 * h + 2)
                TT(tiles(attn_t), tiles(bank(6)), decay, ALU.mult).then_inc(low_ready, 1)
                dve.wait_ge(r_ready, h + 1)
                dve.wait_ge(tr_in, 3 * h + 3)
                TT(tiles(vtok), tiles(bank(4)), over_free(k_norm), ALU.mult).then_inc(v_ready, 1)
                lo(2)
                dve.wait_ge(y_ready, 7 * h + 1)
                glink(TT(tiles(inv_t), tiles(ys[0]), over_tiles(ident), ALU.add))
                for q in range(P // BLK):
                    op = dve.transpose(inv_d[q * BLK:(q + 1) * BLK, :, :], on_diag(inv_t, q))
                op.then_inc(inv_first, 1)
                lo(3)
                for n in range(1, 7):
                    dve.wait_ge(lvl_mm, 7 * h + n) if n < 6 else None
                    if n < 5:
                        glink(TT(inv_d, inv_d, diag(bank(5)), ALU.add))
                        if n == 4:
                            TT(inv.rearrange("p (t b c) -> p t b c", t=NT, c=BLK),
                               inv_d.unsqueeze(2).to_broadcast([P, NT, P // BLK, BLK]),
                               diag_mask.rearrange("p (b c) -> p b c", c=BLK).unsqueeze(1).to_broadcast(
                                   [P, NT, P // BLK, BLK]), ALU.mult)
                        for q in range(P // BLK):
                            op = dve.transpose(on_diag(inv_t, q), inv_d[q * BLK:(q + 1) * BLK, :, :])
                        op.then_inc(lvl_ready, 1)
                    else:
                        if n == 5:
                            TT(inv, inv, bank(5), ALU.add).then_inc(lvl_ready, 1)
                        dve.wait_ge(lvl_mm, 7 * h + (n + 1))
                        TT(inv_t, inv_t, bank(6), ALU.add).then_inc(lvl_ready, 1)
                    lo(3 + n)
                    if following == "gdn":
                        if n in (1, 2, 3):
                            if n == 1:
                                dve.wait_ge(tap_done, 3 * h + 4)
                            tap(0, n - 1, glink)
                        if n == 6:
                            dve.wait_ge(tap_done, 3 * h + 5)
                            for j in range(3):
                                tap(1, j, glink)
                    else:
                        if n == 2:
                            rot(0, 0, lambda: dve.wait_ge(tr_in, 3 * GH))
                        if n == 6:
                            rot(0, 1, None)
                dve.wait_ge(uw_mm, 2 * h + 1)
                TT(tiles(vnew), tiles(bank(2)), over_free(beta_k), ALU.mult).then_inc(vn_ready, 1)
                lo(10)

                def sum_o(t):
                    dve.wait_ge(o_mm, 4 * h + (t + 1))
                    dst = o_raw[:, t * P:(t + 1) * P]
                    if t == 0:
                        dve.tensor_copy(dst, within(t)).then_inc(o_summed, 1)
                    else:
                        dve.wait_ge(o_part, 3 * h + t)
                        TT(dst, dst, within(t), ALU.add).then_inc(o_summed, 1)

                for t in range(NT):
                    tt = slice(t * P, (t + 1) * P)
                    if t > 0:
                        dve.wait_ge(ws_mm, 3 * h + t)
                        STT(vnew[:, tt], bank(4)[:, tt], nbeta_k[:, t:t + 1], vnew[:, tt], ALU.mult,
                            ALU.add).then_inc(vn_ready, 1)
                        dve.wait_ge(qs_mm, 3 * h + t)
                        TS(o_raw[:, tt], from_state(t), eg[:, t:t + 1], None, ALU.mult).then_inc(o_part, 1)
                        sum_o(t - 1)
                    if t < NT - 1:
                        dve.wait_ge(ktv_mm, 3 * h + (t + 1))
                        if t == 0:
                            dve.tensor_copy(state[0], bank(5)[:, tt]).then_inc(st_ready, 1)
                        else:
                            dve.wait_ge(st_ready, 3 * h + t)
                            STT(state[t], state[t - 1], par[:, 16 + t:17 + t], bank(5)[:, tt], ALU.mult,
                                ALU.add).then_inc(st_ready, 1)
                    if t == 0:
                        lo(11)
                    if t >= 2 and following == "gdn":
                        if t == 2:
                            dve.wait_ge(tap_done, 3 * h + 6)
                        tap(2, t - 2, glink)
                    if t == 3 and following == "ret":
                        rot(0, 2, None)
                    if t == 3:
                        sum_o(3)
                        lo(12)
                dve.wait_ge(o_sq, h + 1)
                glink(dve.tensor_reduce(stat[:, 0, 8:12], tiles(ys[0]), AX.X, ALU.add))
                STT(stat[:, 1, 8:12], stat[:, 0, 8:12], 1.0 / P, q_eps, ALU.mult, ALU.add).then_inc(o_ms, 1)
                if following == "gdn":
                    tap(2, 2, glink)
                lo(13)
                lo(14)
                lo(15)
                dve.wait_ge(o_rstd, h + 1)
                TT(tiles(o_n), tiles(o_raw), over_free(stat[:, 2, 8:12]), ALU.mult).then_inc(on_ready, 1)
                dve.wait_ge(otr_mm, h + 1)
                STT(mix[:, bass.ds(h, 1), :].rearrange("p a c -> p (a c)"), bank(6), cols[:, 112:113], gate,
                    ALU.mult, ALU.mult).then_inc(mix_done, 1)
                return glink.n

            with dve.Fori(0, GH - 1) as h:
                used = gdn_body(h, 4 * h + 4, "gdn")
            assert used == DVE_GDN_LINKS, used
            gdn_body(GH - 1, N_GDN_UNITS, "ret")

            def ret_a(r, unit0):
                lo = lambda k: split_lo(unit0, 5 + k // 4, k % 4)
                rot(r, 3, None)
                for k in range(16):
                    lo(k)
                    if k in (1, 3, 5, 7):
                        j = k // 2
                        n = SEQ - j * P
                        dve.wait_ge(rs_mm, 4 * r + (j + 1))
                        if j == 0:
                            dve.wait_ge(s_dec, 16 * RH)
                        table = mix[:, bass.ds(2 * r + GH, 1), 0:n].rearrange("p a c -> p (a c)")
                        TT(s_all[:, s_off[j]:s_off[j] + n], bank(4 + j)[:, 0:n], table,
                           ALU.mult).then_inc(rs_ready, 1)

            def ret_b(r, lo, following):
                rlink = Links(dve, dve_link_ret, DVE_RET_LINKS * r)
                sq = ro_sq.rearrange("p a c -> p (a c)").rearrange("p (j d) -> p j d", j=NT)
                for b in range(2):
                    dve.wait_ge(ro_sqd, 2 * r + (b + 1))
                    rlink(dve.tensor_reduce(stat[:, 0, 2 * b:2 * b + 2], sq[:, 2 * b:2 * b + 2, :], AX.X,
                                            ALU.add))
                    lo(b)
                TS(stat[:, 1, 0:4], stat[:, 0, 0:4], 1.0 / RDK, EPS, ALU.mult, ALU.add).then_inc(ro_ms, 1)
                lo(2)
                dve.wait_ge(ro_rstd, r + 1)
                for b in range(2):
                    TT(ro_n[:, 2 * b:2 * b + 2, :], bank(6 + b).rearrange("p (j d) -> p j d", j=2),
                       over_free(stat[:, 2, 2 * b:2 * b + 2], RDK), ALU.mult).then_inc(ron_ready, 1)
                lo(3)
                for d in range(2):
                    dve.wait_ge(rotr_mm, 2 * r + (d + 1))
                    dve.wait_ge(rgate_done, 2 * r + (d + 1))
                    TT(mix[:, bass.ds(2 * r + (GH + d), 1), :].rearrange("p a c -> p (a c)"), bank(4 + d),
                       rgate[:, d, :], ALU.mult).then_inc(rmix_done, 1)
                assert rlink.n == DVE_RET_LINKS

            with dve.Fori(0, RH - 1) as r:
                ret_a(r, 8 * r + N_GDN_UNITS)
                lo = lambda k: split_lo(8 * r + (N_GDN_UNITS + 8), 1 + k // 4, k % 4)
                ret_b(r, lo, "ret")
                for i in range(3):
                    for k in range(4):
                        lo(4 + 4 * i + k)
                    rot(r + 1, i, lambda: dve.wait_ge(rs_mm, 4 * r + 4))
            last = RH - 1
            ret_a(last, 8 * last + N_GDN_UNITS)

            def mix_lo(s):
                dve.wait_ge(mhi_ready, s + 1)
                if s == 0:
                    dve.wait_ge(proj_done, OUT_U)
                TT(act_lo[:, s, :], mix[:, s, :], act_hi[:, s, :].bitcast(F32),
                   ALU.subtract).then_inc(mlo_ready, 1)

            for s in range(6):
                mix_lo(s)
            lo = lambda k: split_lo(OUT_U, 1 + k // 4, k % 4)
            ret_b(last, lo, "out")
            for s in range(6, 14):
                mix_lo(s)
                if s < 14 and s - 2 < 12:
                    lo(s - 2)
            mix_lo(14)
            mix_lo(15)
            for k in range(12, 16):
                lo(k)

            def add_x(n, t):
                dve.wait_ge(oproj_mm, 4 * n + (t + 1))
                at = h_tok[:, t, bass.ds(n * SEQ, SEQ)]
                TT(at, at, bank(t), ALU.add).then_inc(h_ready, 1)

            def weigh_h(n):
                for t in range(NT):
                    dve.wait_ge(h_sq, 4 * n + (t + 1))
                    at = h_tok[:, t, bass.ds(n * SEQ, SEQ)]
                    TT(at, at, fin_w[:, bass.ds(n * SEQ, SEQ)], ALU.mult).then_inc(h_weighed, 1)

            dve.wait_ge(s_xres[0], 16)
            for t in range(NT):
                add_x(0, t)
            dve.wait_ge(s_fin, 16)
            weigh_h(0)
            for n in range(1, 4):
                dve.wait_ge(s_xres[n], 16)
            with dve.Fori(1, 3) as n:
                for k in range(16):
                    split_lo(4 * n + OUT_U, 1 + k // 4, k % 4)
                for t in range(NT):
                    add_x(n, t)
                weigh_h(n)
            for k in range(12):
                split_lo(OUT_U + 12, 1 + k // 4, k % 4)
            for t in range(NT):
                add_x(3, t)
                dve.wait_ge(h_sq, 12 + t + 1)
                link(dve.tensor_reduce(stat[:, 0, t:t + 1], small[:, 0, 4 * t:4 * t + 4], AX.X, ALU.add))
                TS(stat[:, 1, t:t + 1], stat[:, 0, t:t + 1], 1.0 / D, EPS, ALU.mult, ALU.add).then_inc(h_ms, 1)
                dve.wait_ge(h_rstd, t + 1)
                at = slice(3 * SEQ, 4 * SEQ)
                STT(h_tok[:, t, at], h_tok[:, t, at], stat[:, 2, t:t + 1], fin_w[:, at], ALU.mult, ALU.mult)
                at = slice(2 * SEQ, 3 * SEQ)
                dve.wait_ge(h_weighed, 3 * NT)
                TS(h_tok[:, t, at], h_tok[:, t, at], stat[:, 2, t:t + 1], None, ALU.mult).then_inc(y_done, 1)

        @block.gpsimd
        def _(pool):
            TT = pool.tensor_tensor
            for t in range(NT):
                pool.wait_ge(x_ms, t + 1)
                if t == 0:
                    pool.wait_ge(memsets, 3)
                TT(stat[:, 3, t:t + 1], stat[:, 2, t:t + 1], half[:, 0:1], ALU.pow).then_inc(x_rstd, 1)
            pool_then = Links(pool, pool_link)
            pos_f, turns, angle, whole = wk(W_KTOK), wk(W_QTOK), wk(W_QGTOK), wk(W_VTOK)
            TS = pool.tensor_scalar
            pool.wait_ge(s_cst, 16)
            pool.wait_ge(s_pos, 16)
            pool_then(pool.tensor_copy(pos_f, work2[:, W_GATE, :].bitcast(I32)))
            TS(angle, pos_f, inv_freq, None, ALU.mult).then_inc(angle_ready, 1)
            pool.wait_ge(angle_ready, 1)
            angle_sin = rope_sin[:, :]
            pool_then(TS(turns, angle, 1.0 / (2 * math.pi), None, ALU.mult))
            pool_then(TS(turns, turns, magic, None, ALU.add))
            pool_then(TS(turns, turns, -magic, None, ALU.add))
            for part, rest in ((c1, angle), (c2, angle_sin), (c3, angle_sin)):
                pool_then(TS(whole, turns, part, None, ALU.mult))
                pool_then(TT(angle_sin, rest, whole, ALU.subtract))
            TS(angle_sin, angle_sin, -3.1415925, 3.1415925, ALU.max, ALU.min).then_inc(rope_arg, 1)

            pool.wait_ge(xt_mm, KT)
            for e in range(GH):
                pool.wait_ge(dif_exp, e + 1)
                TT(tiles(mix[:, e, :]), tiles(wk(W_X + e % 2)), over_tiles(causal),
                   ALU.mult).then_inc(decay_ready, 1)

            def rot_sum(r, i):
                dst = (q_rot, k_rot)[i]
                pool.wait_ge(rot_read, 4 * r + (2 * i + 2))
                TT(dst[:, 0, :], dst[:, 0, :], rot_tmp[:, 0, :], ALU.subtract).then_inc(rot_done, 1)
                TT(dst[:, 1, :], dst[:, 1, :], rot_tmp[:, 1, :], ALU.add).then_inc(rot_done, 1)

            def gdn_body(h, following):
                pool.wait_ge(ss_ready, h + 1)
                TT(k_norm, k_norm2, half[:, 8:12], ALU.pow).then_inc(r_ready, 1)
                pool.wait_ge(k_tok_ready, h + 1)
                pool.wait_ge(par_ready, h + 1)
                pool.wait_ge(low_ready, 2 * h + 1)
                for n in range(2):
                    TT(tiles(ys[n]), tiles(lower_t), over_tiles(level_mask(n)), ALU.mult).then_inc(y_ready, 1)
                TT(tiles(kbg), tiles(ktok), over_free(par[:, 8:12]), ALU.mult).then_inc(kk_ready, 1)
                TT(tiles(ktail), tiles(ktok), over_free(par[:, 12:16]), ALU.mult).then_inc(kk_ready, 1)
                for n in range(2, LEVELS):
                    if n == 2:
                        pool.wait_ge(inv_first, h + 1)
                    else:
                        pool.wait_ge(t1_mm, 6 * h + (n - 2))
                    TT(tiles(ys[n % 2]), tiles(lower_t), over_tiles(level_mask(n)), ALU.mult).then_inc(y_ready, 1)
                if following == "ret":
                    rot_sum(0, 0)
                pool.wait_ge(o_ms, h + 1)
                TT(stat[:, 2, 8:12], stat[:, 1, 8:12], half[:, 0:4], ALU.pow).then_inc(o_rstd, 1)

            with pool.Fori(0, GH - 1) as h:
                gdn_body(h, "gdn")
            gdn_body(GH - 1, "ret")

            def ret_norm(r):
                pool.wait_ge(ro_ms, r + 1)
                TT(stat[:, 2, 0:4], stat[:, 1, 0:4], half[:, 0:4], ALU.pow).then_inc(ro_rstd, 1)

            with pool.Fori(0, RH - 1) as r:
                rot_sum(r, 1)
                ret_norm(r)
                rot_sum(r + 1, 0)
            rot_sum(RH - 1, 1)
            ret_norm(RH - 1)
            for t in range(NT):
                pool.wait_ge(h_ms, t + 1)
                TT(stat[:, 2, t:t + 1], stat[:, 1, t:t + 1], half[:, 0:1], ALU.pow).then_inc(h_rstd, 1)


def shape_constants():
    j, i = np.arange(P)[:, None], np.arange(P)[None, :]
    parts = [np.eye(P), (i >= j)]
    for n in range(LEVELS):
        parts.append(-1.0 * (((i >> n) & 1 == 1) & ((j >> n) == (i >> n) - 1)))
    parts.append(i // BLK == j // BLK)
    freq = 1.0 / (np.float32(10000.0) ** (np.arange(0, RDK, 2, dtype=np.float32) / np.float32(RDK)))
    parts.append(freq[:, None])
    consts = np.concatenate([p.astype(np.float32) for p in parts], axis=1)
    gamma = 1.0 - 2.0 ** (-5.0 - np.arange(RH))
    rel = np.arange(SEQ)[None, :] - np.arange(P)[:, None]
    decays = np.where(rel >= 0, gamma[:, None, None] ** np.maximum(rel, 0), 0.0) * RDK ** -0.5
    return consts, decays.astype(np.float32)


def kernel(**inputs):
    import concourse.bacc as bacc
    from concourse.bass_utils import run_bass_kernel_spmd

    consts, decays = shape_constants()
    given = {name: np.asarray(a) for name, a in inputs.items()}
    arrays = {
        "x": given["x"][0], "positions": given["positions"][0], "norm_w": given["norm_w"][0],
        "w_in": given["w_in"][0], "conv_w": given["conv_w"][0], "a_log": given["a_log"][0],
        "dt_bias": given["dt_bias"][0], "gdn_norm_w": given["gdn_norm_w"][0],
        "w_out": given["w_out"][0], "final_norm_w": given["final_norm_w"],
        "consts": consts, "decays": decays,
    }
    arrays = {f"in_{name}": np.ascontiguousarray(a) for name, a in arrays.items()}
    nc = bacc.Bacc("TRN2", target_bir_lowering=False, num_devices=1)
    aps = [nc.dram_tensor(name, a.shape, mybir.dt.from_np(a.dtype), kind="ExternalInput").ap()
           for name, a in arrays.items()]
    y = nc.dram_tensor("y", (SEQ, D), F32, kind="ExternalOutput").ap()
    build(nc, *aps, y)
    result = run_bass_kernel_spmd(nc, [arrays], core_ids=[0])
    return result.results[0]["y"].reshape(1, SEQ, D)
```

```python
import math
from contextlib import ExitStack

import numpy as np
import concourse.bass as bass
from concourse import mybir

F32 = mybir.dt.float32
F32R = mybir.dt.float32r
I32 = mybir.dt.int32
ALU = mybir.AluOpType
ACT = mybir.ActivationFunctionType
AX = mybir.AxisListType

P = 128
SEQ = 512
D = 2048
KT = D // P
NT = SEQ // P
GH, RH = 8, 4
RDK = 256
GROUP = 1024
GDN_COL = 4 * GROUP
GATE_COL = 8 * GROUP
EPS = 1e-6
PIECE = 512
UNIT_MM = 3 * KT
N_GDN_UNITS = 4 * GH
N_RET_UNITS = 8 * RH
OUT_U = N_GDN_UNITS + N_RET_UNITS
SMALL = 8
BLK = 32
MASKS = 4
NP = 20

(W_KTOK, W_LOWER, W_ATTN, W_VTOK, W_KKEEP, W_QKEEP, W_ORAW, W_Y0, W_Y1, W_X, W_XT, W_T1, W_GRAW,
 W_KTAIL, W_VN, W_S, W_GATE) = range(17)

DVE_GDN_LINKS = 18
DVE_RET_LINKS = 2


class Links:

    def __init__(self, eng, sem, base=0):
        self.eng, self.sem, self.base, self.n = eng, sem, base, 0

    def __call__(self, instruction):
        instruction.then_inc(self.sem, 1)
        self.n += 1
        self.eng.wait_ge(self.sem, self.base + self.n)


def build(nc, x, positions, norm_w, w_in, conv_w, a_log, dt_bias, gdn_norm_w, w_out, final_norm_w,
          consts, decays, out):
    with ExitStack() as ctx:
        def sb(name, shape, dt=F32):
            return ctx.enter_context(nc.sbuf_tensor(name, shape, dt))

        def sem(name):
            return ctx.enter_context(nc.semaphore(name))

        act_hi = sb("act_hi", [P, KT, SEQ], F32R)
        act_lo = sb("act_lo", [P, KT, SEQ], F32R)
        w_raw = sb("w_raw", [P, 2, KT * P])
        w_hi = sb("w_hi", [P, 2, KT * P], F32R)
        w_lo = sb("w_lo", [P, 2, KT * P], F32R)
        mix = sb("mix", [P, KT, SEQ])
        work1 = sb("work1", [P, 6, SEQ])
        work2 = sb("work2", [P, 17, SEQ])
        cst = sb("cst", [P, (3 + MASKS) * P + BLK + 1])
        blocks = sb("blocks", [P, NT, 3 * BLK])
        ones = sb("ones", [P, P])
        rope_cos = sb("rope_cos", [P, SEQ])
        rope_sin = sb("rope_sin", [P, SEQ])
        rows = sb("rows", [P, P])
        cols = sb("cols", [P, P])
        wg_hi = sb("wg_hi", [P, KT, 16], F32R)
        wg_lo = sb("wg_lo", [P, KT, 16], F32R)
        head_par = sb("head_par", [P, GH, NP])
        par = sb("par", [P, NP])
        conv_par = sb("conv_par", [P, 4, 3])
        g_log = sb("g_log", [P, GH, NT])
        g_cum = sb("g_cum", [P, GH, NT])
        small = sb("small", [P, 6, GH * NT])
        a_row = sb("a_row", [P, GH])
        dt_row = sb("dt_row", [P, GH])
        stat = sb("stat", [P, 4, 16])
        half = sb("half", [P, 16])
        ps = ctx.enter_context(nc.psum_tensor("ps", [P, 8, SEQ], F32))

        ident = cst[:, 0:P]
        causal = cst[:, P:2 * P]
        diag_mask = cst[:, (2 + MASKS) * P:(3 + MASKS) * P]
        ident_d = cst[:, (3 + MASKS) * P:(3 + MASKS) * P + BLK]
        inv_freq = cst[:, (3 + MASKS) * P + BLK:]

        def level_mask(n):
            return cst[:, (2 + n) * P:(3 + n) * P]

        def tiles(ap):
            return ap.rearrange("p (t c) -> p t c", t=NT)

        def bank(b):
            return ps[:, b, :]

        def over_free(col, n=P):
            return col.unsqueeze(2).to_broadcast([P, col.shape[1], n])

        def over_tiles(mat, n=NT):
            return mat.unsqueeze(1).to_broadcast([P, n, mat.shape[1]])

        wk = lambda i: work2[:, i, :]
        conv = work1
        q_eps, k_norm2, k_norm = stat[:, 1, 0:4], stat[:, 1, 4:8], stat[:, 2, 4:8]
        beta_both = stat[:, 3, 8:16]
        beta_k, nbeta_k = beta_both[:, 0:4], beta_both[:, 4:8]
        x_tok = mix[:, :, :].rearrange("p (t a) c -> p t (a c)", t=NT)
        ktok, vtok, q_keep = wk(W_KTOK), wk(W_VTOK), wk(W_QKEEP)
        lower_t, attn_t, k_keep = wk(W_LOWER), wk(W_ATTN), wk(W_KKEEP)
        ys = [wk(W_Y0), wk(W_Y1)]
        inv, inv_t, t1, o_n = wk(W_X), wk(W_XT), wk(W_T1), wk(W_T1)
        ktail, vnew = wk(W_KTAIL), wk(W_VN)
        all_d, inv_off_d = blocks[:, :, :], blocks[:, :, BLK:]
        pow_d, inv_d, off_d = (blocks[:, :, i * BLK:(i + 1) * BLK] for i in range(3))

        def on_diag(ap, q):
            return tiles(ap)[q * BLK:(q + 1) * BLK, :, q * BLK:(q + 1) * BLK]

        state = [wk(W_S)[:, i * P:(i + 1) * P] for i in range(3)]
        o_raw = wk(W_ORAW)
        gate = wk(W_GATE)

        def from_state(t):
            return bank(2 + t % 2)[:, t * P:(t + 1) * P]

        def within(t):
            return bank(7 - t % 2)[:, t * P:(t + 1) * P]
        gates_f = wk(W_KTAIL)[0:16, :]
        q_rot, k_rot, rot_tmp = work1[:, 0:2, :], work1[:, 2:4, :], work1[:, 4:6, :]
        v_feat = work2[:, 0:2, :]
        rv_tok = work2[:, 2:4, :].rearrange("p a c -> p (a c)").rearrange("p (j d) -> p j d", j=NT)
        rgate = work2[:, 4:6, :]
        s_off = [0, 512, 896, 1152]
        s_all = work2[:, 6:9, :].rearrange("p a c -> p (a c)")
        ro_n = work2[:, 9:11, :].rearrange("p a c -> p (a c)").rearrange("p (j d) -> p j d", j=NT)
        ro_sq = work2[:, 11:13, :]
        h_tok = work2[:, 0:16, :].rearrange("p a c -> p (a c)").rearrange("p (t n) -> p t n", t=NT)
        fin_w = work1[:, 0:4, :].rearrange("p a c -> p (a c)")

        w_in_k = w_in.rearrange("(k p) c -> p k c", p=P)
        w_out_k = w_out.rearrange("(k p) c -> p k c", p=P)
        x_rows = x.rearrange("(t p) c -> p t c", p=P)
        out_rows = out.rearrange("(t p) c -> p t c", p=P)

        s_x = [sem(f"x_loaded{t}") for t in range(NT)]
        s_xres = [sem(f"x_again_loaded{n}") for n in range(4)]
        s_w = [sem(f"w_loaded{i}") for i in range(2)]
        s_ident = sem("ident_loaded")
        s_cst, s_rows, s_wg, s_pos, s_arow, s_dec, s_fin = (
            sem(n) for n in ("cst_loaded", "rows_loaded", "wg_loaded", "pos_loaded", "a_dt_loaded",
                             "decays_loaded", "final_w_loaded"))
        s_out = sem("out_stored")
        hi_ready, lo_ready, proj_done = sem("w_hi_ready"), sem("w_lo_ready"), sem("unit_projected")
        memsets, cols_mm, cols_ready = sem("memsets"), sem("cols_turned"), sem("cols_ready")
        x_sq, x_ms, x_rstd, x_scaled = sem("x_squared"), sem("x_mean"), sem("x_rstd"), sem("x_scaled")
        xt_mm, xhi_ready, xlo_ready = sem("x_turned"), sem("x_hi_ready"), sem("x_lo_ready")
        wg_hi_ready, wg_lo_ready, gates_mm = sem("wg_hi"), sem("wg_lo"), sem("gates_projected")
        gates_copied = sem("gates_copied")
        p_dve, p_act, p_mm, p_ready = sem("par_dve"), sem("par_act"), sem("cumsum_mm"), sem("par_ready")
        ug_ready, g_mm, dif_ready, dif_exp, decay_ready = (
            sem(n) for n in ("ug_ready", "decay_mm", "decay_log_ready", "decay_exp", "decay_ready"))
        dt_added = sem("dt_added")
        angle_ready, rope_arg, cos_arg, rope_ready = (
            sem(n) for n in ("angle_ready", "rope_arg", "cos_arg", "rope_ready"))
        dve_link, pool_link = sem("dve_link"), sem("pool_link")
        dve_link_gdn, dve_link_ret = sem("dve_link_gdn"), sem("dve_link_ret")
        par_ready, conv_par_ready = sem("head_par_ready"), sem("conv_par_ready")
        tap_done, conv_done, silu_done, gate_done = (
            sem(n) for n in ("tap_done", "conv_done", "silu_done", "gate_done"))
        tr_in, qk_sq, v_ready, ss_ready, r_ready, k_tok_ready, kq_kept = (
            sem(n) for n in ("qkv_turned", "qk_squared", "v_ready", "k_norm2_ready", "k_norm_ready",
                             "k_tok_ready", "kq_kept"))
        ktail_ready, kk_mm, low_ready = (sem(n) for n in ("k_tail_ready", "kk_mm", "lower_ready"))
        qs_mm, o_part, o_summed = sem("q_state_mm"), sem("o_part"), sem("o_summed")
        y_ready, blk_ready, blk_mm, t1_mm, t1_ready, lvl_mm, lvl_ready = (
            sem(n) for n in ("y_ready", "block_ready", "block_mm", "t1_mm", "t1_ready", "level_mm",
                             "level_ready"))
        rest_ready, xr_mm = sem("v_less_state_ready"), sem("inverse_v_mm")
        ks_mm, vn_ready, ktv_mm, st_ready, o_mm = (
            sem(n) for n in ("k_state_mm", "vnew_ready", "ktv_mm", "state_ready", "o_mm"))
        o_sq, o_ms, o_rstd, on_ready, otr_mm, mix_done = (
            sem(n) for n in ("o_squared", "o_mean", "o_rstd", "o_normed", "o_turned", "mix_done"))
        rot_read, rot_done, rs_mm, rs_ready, vf_done, rgate_done, rvt_mm, rvt_ready = (
            sem(n) for n in ("rot_read", "rot_done", "ret_scores_mm", "ret_scores_ready", "v_feat_done",
                             "ret_gate_done", "ret_v_turned", "ret_v_ready"))
        ro_mm, ro_sqd, ro_ms, ro_rstd, ron_ready, rotr_mm, rmix_done = (
            sem(n) for n in ("ret_o_mm", "ret_o_squared", "ret_o_mean", "ret_o_rstd", "ret_o_normed",
                             "ret_o_turned", "ret_mix_done"))
        mhi_ready, mlo_ready, oproj_mm, h_ready, h_sq, h_ms, h_rstd, y_done = (
            sem(n) for n in ("mix_hi_ready", "mix_lo_ready", "out_projected", "h_ready", "h_squared",
                             "h_mean", "h_rstd", "y_done"))
        h_weighed, y_left_done = sem("h_weighed"), sem("y_left_done")

        magic = 1.5 * 2.0 ** 23
        c1, c2 = 6.28125, float(np.float32(2 * math.pi - 6.28125))
        c3 = float(np.float32(2 * math.pi - 6.28125 - c2))

        block = ctx.enter_context(nc.Block())

        @block.sync
        def _(sp):
            for t in range(NT):
                sp.dma_start(x_tok[:, t, :], x_rows[:, t, :]).then_inc(s_x[t], 16)

            def load_in(slot, col, wait):
                if wait is not None:
                    sp.wait_ge(lo_ready, wait)
                sp.dma_start(w_raw[:, slot, :].rearrange("p (k c) -> p k c", k=KT),
                             w_in_k[:, :, bass.ds(col, P)]).then_inc(s_w[slot], 16)

            for s in range(4):
                if s == 2:
                    sp.wait_ge(xt_mm, KT)
                    for r in range(RH):
                        sp.dma_start(mix[:, GH + 2 * r, :], decays[r, :, :]).then_inc(s_dec, 16)
                load_in(s % 2, GDN_COL + GROUP * s, None if s < 2 else 4 * s - 4)
            with sp.Fori(1, GH) as h:
                for s in range(4):
                    load_in(s % 2, GDN_COL + GROUP * s + h * P, 16 * h + 4 * s - 4)
            with sp.Fori(0, RH) as r:
                for i in range(8):
                    load_in(i % 2, GROUP * (i // 2) + P * (i % 2) + r * (2 * P),
                            32 * r + 4 * N_GDN_UNITS + 4 * i - 4)

            def load_out(n, kg, after=None):
                first = GH + 4 * kg if kg < 2 else 4 * (kg - 2)
                col = n * SEQ if after is None else after * SEQ + SEQ
                sp.wait_ge(lo_ready, 16 * n + 4 * OUT_U + 4 * kg - 4)
                sp.dma_start(w_raw[:, kg % 2, :].rearrange("p (k c) -> p k c", k=4),
                             w_out_k[:, first:first + 4, bass.ds(col, SEQ)]).then_inc(s_w[kg % 2], 16)

            for kg in range(4):
                load_out(0, kg)
            sp.wait_ge(rmix_done, 2 * RH + 1)
            for n in range(4):
                sp.dma_start(h_tok[:, :, n * SEQ:(n + 1) * SEQ],
                             x_rows[:, :, n * SEQ:(n + 1) * SEQ]).then_inc(s_xres[n], 16)
            sp.dma_start(fin_w, final_norm_w.partition_broadcast(P)).then_inc(s_fin, 16)
            with sp.Fori(0, 3) as before:
                for kg in range(4):
                    load_out(before + 1, kg, before)
            for t in range(NT):
                sp.wait_ge(y_done, t + 1)
                sp.wait_ge(y_left_done, t + 1)
                sp.dma_start(out_rows[:, t, :], h_tok[:, t, :]).then_inc(s_out, 16)
            sp.wait_ge(s_out, 16 * NT)

        @block.tensor
        def _(pe):
            mm = pe.matmul

            class Unit:

                def __init__(self, first, bank_free):
                    self.first, self.bank_free, self.m = first, bank_free, 0

                def fill(self, n):
                    for _ in range(n):
                        i, m = divmod(self.m, UNIT_MM)
                        kt, pas = divmod(m, 3)
                        slot = i % 2
                        if m == 0:
                            self.bank_free(i)
                        if m % 12 == 0:
                            pe.wait_ge(lo_ready, self.first * 4 + (4 * i + m // 12 + 1))
                        w = (w_hi, w_hi, w_lo)[pas][:, slot, kt * P:(kt + 1) * P]
                        a = (act_hi, act_lo, act_hi)[pas][:, kt, :]
                        op = mm(bank(slot), w, a, start=m == 0, stop=m == UNIT_MM - 1)
                        if m == UNIT_MM - 1:
                            op.then_inc(proj_done, 1)
                        self.m += 1

            pe.wait_ge(s_ident, 16)
            for t in range(NT):
                if t == NT - 1:
                    pe.wait_ge(s_rows, 48)
                    pe.transpose(bank(7)[:, 0:113], rows[0:113, :], ident[0:113, 0:113]).then_inc(cols_mm, 1)
                pe.wait_ge(x_scaled, t + 1)
                for kt in range(5):
                    op = pe.transpose(tiles(bank(2 + kt))[:, t, :], x_tok[:, t, kt * P:(kt + 1) * P], ident)
                    if t == NT - 1:
                        op.then_inc(xt_mm, 1)

            def turn_x(kt):
                pe.wait_ge(xlo_ready, kt - 4)
                for t in range(NT):
                    op = pe.transpose(tiles(bank(2 + kt % 5))[:, t, :], x_tok[:, t, kt * P:(kt + 1) * P],
                                      ident)
                op.then_inc(xt_mm, 1)

            head0 = Unit(0, lambda i: None)
            for kt in range(KT):
                if kt >= 1 and kt + 4 < KT:
                    turn_x(kt + 4)
                pe.wait_ge(xlo_ready, kt + 1)
                head0.fill(3)

            pe.wait_ge(wg_lo_ready, 1)
            for kt in range(KT):
                for pas in range(3):
                    op = mm(bank(2)[0:16, :], (wg_hi, wg_hi, wg_lo)[pas][:, kt, :],
                            (act_hi, act_lo, act_hi)[pas][:, kt, :],
                            start=kt == 0 and pas == 0, stop=kt == KT - 1 and pas == 2)
            op.then_inc(gates_mm, 1)

            def head0_bank(i):
                if i >= 2:
                    pe.wait_ge(conv_done, i - 1)

            head0.bank_free = head0_bank
            head0.fill(8)
            pe.wait_ge(gates_copied, 1)
            for t in range(NT):
                op = pe.transpose(bank(6)[:, 16 * t:16 * t + 16], gates_f[:, t * P:(t + 1) * P],
                                  ident[0:16, 0:16])
            op.then_inc(gates_mm, 1)
            head0.fill(22)
            pe.wait_ge(s_cst, 16)
            pe.wait_ge(p_dve, 1)
            g_all = g_log[:, :, :].rearrange("p h t -> p (h t)")
            mm(bank(3)[:, 0:GH * NT], causal, g_all, start=True, stop=True)
            mm(bank(3)[:, GH * NT:2 * GH * NT], ones[:, :], g_all, start=True, stop=True).then_inc(p_mm, 1)
            head0.fill(UNIT_MM - 30)
            for e in range(GH):
                pe.wait_ge(ug_ready, e + 1)
                if e >= 2:
                    pe.wait_ge(dif_ready, e - 1)
                mm(bank(4 + e % 2), ones[:, :], ys[e % 2], start=True, stop=True).then_inc(g_mm, 1)
                head0.fill(10)
            head0.fill(2 * UNIT_MM - 10 * GH)
            pe.wait_ge(dif_ready, GH)

            def gdn_head(h, unit, per):
                fill = unit.fill
                for s in range(3):
                    pe.wait_ge(silu_done, 3 * h + (s + 1))
                    for t in range(NT):
                        op = pe.transpose(tiles(bank(2 + s))[:, t, :], conv[:, s, t * P:(t + 1) * P], ident)
                    op.then_inc(tr_in, 1)
                    if s == 1:
                        fill(per)
                pe.wait_ge(mix_done, h + 1)
                for b, rhs in ((5, 1), (6, 0)):
                    for t in range(NT):
                        op = mm(tiles(bank(b))[:, t, :], tiles(conv[:, 1, :])[:, t, :],
                                tiles(conv[:, rhs, :])[:, t, :], start=True, stop=True)
                    op.then_inc(kk_mm, 1)
                fill(7 * per)
                pe.wait_ge(y_ready, 4 * h + 1)
                pe.wait_ge(v_ready, h + 1)
                for m, factor in enumerate((all_d, all_d, inv_off_d, inv_off_d, inv_d)):
                    pe.wait_ge(blk_ready, 5 * h + (m + 1))
                    dst = bank(4 + m % 2)[:, 0:NT * factor.shape[2]].rearrange("p (t c) -> p t c", t=NT)
                    for t in range(NT):
                        op = mm(dst[:, t, :], tiles(ys[0])[:, t, :], factor[:, t, :], start=True, stop=True)
                    op.then_inc(blk_mm, 1)
                    fill((9, 10, 10, 8, 10)[m])
                for n in range(2):
                    pe.wait_ge(y_ready, 4 * h + (n + 3))
                    pe.wait_ge(lvl_ready, 4 * h + (1, 3)[n])
                    for t in range(NT):
                        op = mm(tiles(bank(4))[:, t, :], tiles(ys[1 - n])[:, t, :], tiles(inv)[:, t, :],
                                start=True, stop=True)
                    op.then_inc(t1_mm, 1)
                    fill(6)
                    pe.wait_ge(t1_ready, 2 * h + (n + 1))
                    if n == 0:
                        for t in range(NT):
                            op = mm(tiles(bank(5))[:, t, :], tiles(inv_t)[:, t, :], tiles(t1)[:, t, :],
                                    start=True, stop=True)
                        op.then_inc(lvl_mm, 1)
                    for t in range(NT):
                        op = mm(tiles(bank(6))[:, t, :], tiles(t1)[:, t, :], tiles(inv_t)[:, t, :],
                                start=True, stop=True)
                    op.then_inc(lvl_mm, 1)
                    fill((7, 6)[n])
                pe.wait_ge(lvl_ready, 4 * h + 4)
                for t in range(NT):
                    tt = slice(t * P, (t + 1) * P)
                    if t > 0:
                        pe.wait_ge(st_ready, 3 * h + t)
                        if t == 1:
                            pe.wait_ge(kq_kept, 2 * h + 2)
                        op = mm(bank(4)[:, tt], k_keep[:, tt], state[t - 1], start=True, stop=True)
                        op.then_inc(ks_mm, 1)
                        mm(from_state(t), q_keep[:, tt], state[t - 1], start=True, stop=True).then_inc(qs_mm, 1)
                        fill(4)
                        pe.wait_ge(rest_ready, 3 * h + t)
                    mm(bank(4)[:, tt], inv_t[:, tt], vtok[:, tt], start=True, stop=True).then_inc(xr_mm, 1)
                    fill(4)
                    pe.wait_ge(vn_ready, 4 * h + (t + 1))
                    if t == 0:
                        pe.wait_ge(ktail_ready, h + 1)
                    if t < NT - 1:
                        mm(bank(5)[:, tt], ktail[:, tt], vnew[:, tt], start=True, stop=True).then_inc(ktv_mm, 1)
                    if t == 0:
                        pe.wait_ge(low_ready, 2 * h + 2)
                    mm(within(t), attn_t[:, tt], vnew[:, tt], start=True, stop=True).then_inc(o_mm, 1)
                    fill(per)

            def gdn_body(h, unit):
                gdn_head(h, unit, 6)
                unit.fill(18)
                pe.wait_ge(on_ready, h + 1)
                for t in range(NT):
                    op = pe.transpose(tiles(bank(6))[:, t, :], tiles(o_n)[:, t, :], ident)
                op.then_inc(otr_mm, 1)
                unit.fill(4 * UNIT_MM - unit.m)

            def gdn_bank(h):
                def free(i):
                    if i == 1:
                        pe.wait_ge(gate_done, h + 1)
                    else:
                        pe.wait_ge(conv_done, 3 * h + (3, 0, 4, 5)[i])
                return free

            def ret_bank(r):
                def free(i):
                    if i < 2:
                        if isinstance(r, int) and r == 0:
                            pe.wait_ge(*((conv_done, 3 * GH), (gate_done, GH))[i])
                        else:
                            pe.wait_ge(rgate_done, 2 * r + (i - 1))
                    elif i < 6:
                        pe.wait_ge(rot_read, 4 * r + (i - 1))
                    else:
                        pe.wait_ge(vf_done, 2 * r + (i - 5))
                return free

            with pe.Fori(0, GH - 1) as h:
                gdn_body(h, Unit(4 * h + 4, gdn_bank(h)))
            gdn_body(GH - 1, Unit(N_GDN_UNITS, ret_bank(0)))

            def ret_scores(r, unit):
                unit.fill(26)
                for j in range(NT):
                    if j == 0:
                        pe.wait_ge(rot_done, 4 * r + 4)
                        pe.wait_ge(rmix_done, 2 * r + 1)
                    n = SEQ - j * P
                    for d in range(2):
                        op = mm(bank(4 + j)[:, 0:n], k_rot[:, d, j * P:(j + 1) * P], q_rot[:, d, j * P:],
                                start=d == 0, stop=d == 1)
                    op.then_inc(rs_mm, 1)
                    unit.fill(24)
                for d in range(2):
                    pe.wait_ge(vf_done, 2 * r + (d + 1))
                    if d == 0:
                        pe.wait_ge(rs_ready, 4 * r + 2)
                    for j in range(NT):
                        col = (j % 2) * RDK + d * P
                        op = pe.transpose(bank(4 + j // 2)[:, col:col + P],
                                          v_feat[:, d, j * P:(j + 1) * P], ident)
                op.then_inc(rvt_mm, 1)
                unit.fill(8 * UNIT_MM - unit.m)

            def ret_out(r, fill, after=(6, 6, 6, 6)):
                pe.wait_ge(rs_ready, 4 * r + 4)
                pe.wait_ge(rvt_ready, 2 * r + 2)
                for i in range(NT):
                    for j in range(i + 1):
                        at = s_off[j] + (i - j) * P
                        op = mm(bank(6 + i // 2)[:, (i % 2) * RDK:(i % 2 + 1) * RDK], s_all[:, at:at + P],
                                rv_tok[:, j, :], start=j == 0, stop=j == i)
                    if i % 2:
                        op.then_inc(ro_mm, 1)
                    fill(after[i])
                fill(24)
                for d in range(2):
                    pe.wait_ge(ron_ready, 2 * r + 2)
                    for t in range(NT):
                        op = pe.transpose(tiles(bank(4 + d))[:, t, :], ro_n[:, t, d * P:(d + 1) * P], ident)
                    op.then_inc(rotr_mm, 1)

            pe.wait_ge(mix_done, GH + 1)
            with pe.Fori(0, RH - 1) as r:
                unit = Unit(8 * r + N_GDN_UNITS, ret_bank(r))
                unit.m = 4 * UNIT_MM
                ret_scores(r, unit)
                unit = Unit(8 * r + (N_GDN_UNITS + 8), ret_bank(r + 1))
                ret_out(r, unit.fill)
                unit.fill(4 * UNIT_MM - unit.m)
            last = RH - 1
            unit = Unit(8 * last + N_GDN_UNITS, ret_bank(last))
            unit.m = 4 * UNIT_MM
            ret_scores(last, unit)

            def out_mm(kg, kt, t, pas):
                a = (act_hi, act_lo, act_hi)[pas][:, 4 * kg + kt, t * P:(t + 1) * P]
                w = (w_hi, w_hi, w_lo)[pas][:, kg % 2, kt * SEQ:(kt + 1) * SEQ]
                return mm(bank(t), a, w, start=kg == 0 and kt == 0 and pas == 0,
                          stop=kg == 3 and kt == 3 and pas == 2)

            class Early:
                m = 0

                def fill(self, n):
                    for _ in range(n):
                        kg, m = divmod(self.m, UNIT_MM)
                        kt, rest = divmod(m, 12)
                        t, pas = divmod(rest, 3)
                        if self.m == 0:
                            pe.wait_ge(rgate_done, 2 * RH)
                        if rest == 0:
                            pe.wait_ge(lo_ready, 4 * OUT_U + 4 * kg + kt + 1)
                            pe.wait_ge(mlo_ready, 4 * kg + kt + 1)
                        op = out_mm(kg, kt, t, pas)
                        if m == UNIT_MM - 1:
                            op.then_inc(proj_done, 1)
                        self.m += 1

            early = Early()
            ret_out(last, early.fill, (0, 0, 6, 18))
            early.fill(3 * UNIT_MM - early.m)

            def last_group(n):
                pe.wait_ge(lo_ready, 16 * n + (4 * OUT_U + 16))
                for t in range(NT):
                    for kt in range(4):
                        for pas in range(3):
                            op = out_mm(3, kt, t, pas)
                    op.then_inc(oproj_mm, 1)

            pe.wait_ge(mlo_ready, 16)
            last_group(0)
            with pe.Fori(1, 4) as n:
                for kg in range(3):
                    for kt in range(4):
                        pe.wait_ge(lo_ready, 16 * n + (4 * OUT_U + 4 * kg + kt + 1))
                        for t in range(NT):
                            if kg == 0 and kt == 0:
                                pe.wait_ge(h_ready, 4 * n + (t - 3))
                            for pas in range(3):
                                op = out_mm(kg, kt, t, pas)
                    op.then_inc(proj_done, 1)
                last_group(n)

        @block.scalar
        def _(act):
            A = act.activation
            act.dma_start(cst[:, 0:P], consts[:, 0:P]).then_inc(s_ident, 16)
            act.dma_start(rows[0:96, :], conv_w.rearrange("t (c p) -> (t c) p", p=P)).then_inc(s_rows, 16)
            act.dma_start(rows[96:112, :], norm_w.rearrange("(k p) -> k p", p=P)).then_inc(s_rows, 16)
            act.dma_start(rows[112:113, :], gdn_norm_w.rearrange("(a p) -> a p", a=1)).then_inc(s_rows, 16)
            act.dma_start(a_row[:, :], a_log.partition_broadcast(P)).then_inc(s_arow, 16)
            act.dma_start(dt_row[:, :], dt_bias.partition_broadcast(P)).then_inc(s_arow, 16)
            wg_raw = work2[:, W_GRAW, 0:KT * 16].rearrange("p (k c) -> p k c", k=KT)

            def tap3(s):
                A(conv[:, s, :], bank(s % 2), ACT.Copy, scale=conv_par[:, 3, s:s + 1]).then_inc(tap_done, 1)

            def silu(s):
                A(conv[:, s, :], conv[:, s, :], ACT.Silu).then_inc(silu_done, 1)

            for t in range(NT):
                act.wait_ge(s_x[t], 16)
                if t > 0:
                    act.wait_ge(x_sq, t)
                A(work2[:, 0:2, :].rearrange("p a c -> p (a c)"), x_tok[:, t, 0:D // 2], ACT.Square,
                  accum_out=stat[:, 0, t:t + 1]).then_inc(x_sq, 1)
                if t == 0:
                    act.dma_start(cst[:, P:], consts[:, P:]).then_inc(s_cst, 16)
                    act.dma_start(work2[:, W_GATE, :].bitcast(I32),
                                  positions.partition_broadcast(P)).then_inc(s_pos, 16)
                    act.dma_start(wg_raw, w_in_k[:, :, GATE_COL:GATE_COL + 16]).then_inc(s_wg, 16)

            def split_hi(u, pair, i, p):
                if p == 0:
                    act.wait_ge(s_w[i % 2], 16 * pair + 16 * (i // 2 + 1))
                    if not (isinstance(u, int) and u + i < 2):
                        act.wait_ge(proj_done, u + (i - 1))
                at = slice(p * PIECE, (p + 1) * PIECE)
                A(w_hi[:, i % 2, at], w_raw[:, i % 2, at], ACT.Copy).then_inc(hi_ready, 1)

            split_hi(0, 0, 0, 0)
            act.wait_ge(cols_mm, 1)
            A(cols[:, 0:113], bank(7)[:, 0:113], ACT.Copy).then_inc(cols_ready, 1)
            act.wait_ge(cols_ready, 1)
            for kt in range(KT):
                act.wait_ge(xt_mm, kt + 1)
                A(act_hi[:, kt, :], bank(2 + kt % 5), ACT.Copy,
                  scale=cols[:, 96 + kt:97 + kt]).then_inc(xhi_ready, 1)
                if kt < 3:
                    split_hi(0, 0, 0, kt + 1)
                if kt % 4 == 3:
                    split_hi(0, 0, 1, kt // 4)
            act.wait_ge(s_wg, 16)
            A(wg_hi[:, :, :], wg_raw, ACT.Copy).then_inc(wg_hi_ready, 1)
            for p in range(4):
                split_hi(0, 0, 2, p)
            act.wait_ge(conv_par_ready, 1)
            tap3(0)
            act.wait_ge(rope_arg, 1)
            A(rope_sin[:, :], rope_sin[:, :], ACT.Sin).then_inc(rope_ready, 1)
            act.wait_ge(cos_arg, 1)
            A(rope_cos[:, :], rope_cos[:, :], ACT.Sin).then_inc(rope_ready, 1)


            act.wait_ge(gates_mm, 1)
            A(gates_f, bank(2)[0:16, :], ACT.Copy).then_inc(gates_copied, 1)
            act.wait_ge(gates_mm, 2)
            gates = bank(6)[:, 0:16 * NT].rearrange("p (t c) -> p c t", c=16)
            sm = [small[:, i, :].rearrange("p (h t) -> p h t", h=GH) for i in range(6)]
            A(sm[0], gates[:, 0:8, :], ACT.Exp, scale=-1.0).then_inc(p_act, 1)
            act.wait_ge(dt_added, 1)
            A(sm[2], sm[1], ACT.Abs).then_inc(p_act, 1)
            act.wait_ge(p_act, 2)
            A(sm[2], sm[2], ACT.Exp, scale=-1.0).then_inc(p_act, 1)
            act.wait_ge(p_act, 3)
            A(sm[2], sm[2], ACT.Ln, bias=1.0).then_inc(p_act, 1)
            act.wait_ge(s_arow, 32)
            A(a_row[:, :], a_row[:, :], ACT.Exp).then_inc(p_act, 1)

            act.wait_ge(p_mm, 1)
            cum = bank(3)[:, 0:GH * NT].rearrange("p (h t) -> p h t", h=GH)
            tot = bank(3)[:, GH * NT:2 * GH * NT].rearrange("p (h t) -> p h t", h=GH)
            A(head_par[:, :, 8:12], cum, ACT.Exp).then_inc(p_act, 1)
            A(head_par[:, :, 16:20], tot, ACT.Exp).then_inc(p_act, 1)
            act.wait_ge(p_dve, 2)
            A(head_par[:, :, 12:16], sm[3], ACT.Exp).then_inc(p_ready, 1)

            for e in range(GH):
                split_hi(0, 0, 3 + e // 4, e % 4)
                if e in (1, 5):
                    s = 1 + e // 4
                    act.wait_ge(proj_done, s + 1)
                    tap3(s)
                act.wait_ge(dif_ready, e + 1)
                A(wk(W_X + e % 2), wk(W_X + e % 2), ACT.Exp).then_inc(dif_exp, 1)
            for s in range(3):
                act.wait_ge(conv_done, s + 1)
                silu(s)

            def gdn_body(h, unit0, pair, following):
                hi = lambda k: split_hi(unit0, pair, 1 + k // 4, k % 4)
                act.wait_ge(proj_done, 4 * h + 4)
                act.wait_ge(mix_done, h + 1)
                A(gate, bank(1), ACT.Silu).then_inc(gate_done, 1)
                hi(0)
                for s in range(2):
                    act.wait_ge(tr_in, 3 * h + (s + 1))
                    A(ys[s], bank(2 + s), ACT.Square).then_inc(qk_sq, 1)
                A(ktok, bank(3), ACT.Copy).then_inc(k_tok_ready, 1)
                A(q_keep, conv[:, 0, :], ACT.Copy).then_inc(kq_kept, 1)
                A(k_keep, conv[:, 1, :], ACT.Copy).then_inc(kq_kept, 1)
                hi(1)
                hi(2)
                hi(3)
                hi(4)
                if following == "gdn":
                    act.wait_ge(conv_par_ready, h + 2)
                    act.wait_ge(kq_kept, 2 * h + 2)
                    tap3(0)
                hi(5)
                hi(6)
                hi(7)
                if following == "gdn":
                    act.wait_ge(conv_done, 3 * h + 4)
                    silu(0)
                for n in range(2):
                    act.wait_ge(t1_mm, 2 * h + (n + 1))
                    A(t1, bank(4), ACT.Copy).then_inc(t1_ready, 1)
                    hi(8 + n)
                    if following == "gdn" and n == 0:
                        act.wait_ge(proj_done, unit0 + 2)
                        tap3(1)
                hi(10)
                hi(11)
                if following == "gdn":
                    act.wait_ge(conv_done, 3 * h + 5)
                    silu(1)
                    act.wait_ge(proj_done, unit0 + 3)
                    tap3(2)
                hi(12)
                hi(13)
                hi(14)
                act.wait_ge(o_summed, 4 * h + 4)
                A(ys[0], o_raw, ACT.Square).then_inc(o_sq, 1)
                hi(15)
                if following == "gdn":
                    act.wait_ge(conv_done, 3 * h + 6)
                    silu(2)

            with act.Fori(0, GH - 1) as h:
                gdn_body(h, 4 * h + 4, 2 * h + 2, "gdn")
            gdn_body(GH - 1, N_GDN_UNITS, N_GDN_UNITS // 2, "ret")

            def ret_a(r, unit0, pair, n_pieces=16):
                hi = lambda k: split_hi(unit0, pair, 5 + k // 4, k % 4)
                for k in range(n_pieces):
                    hi(k)
                    if k == 5 or k == 9:
                        d = (k - 5) // 4
                        act.wait_ge(proj_done, unit0 + (5 + d))

                        A(v_feat[:, d, :], bank(d), ACT.Copy).then_inc(vf_done, 1)
                act.wait_ge(proj_done, unit0 + 7)
                A(rgate[:, 0, :], bank(0), ACT.Silu).then_inc(rgate_done, 1)
                act.wait_ge(rvt_mm, r + 1)
                for b in range(2):
                    A(work2[:, 2 + b, :], bank(4 + b), ACT.Copy).then_inc(rvt_ready, 1)
                act.wait_ge(proj_done, unit0 + 8)
                A(rgate[:, 1, :], bank(1), ACT.Silu).then_inc(rgate_done, 1)

            def ret_b(r, hi):
                for b in range(2):
                    act.wait_ge(ro_mm, 2 * r + (b + 1))
                    A(ro_sq[:, b, :], bank(6 + b), ACT.Square).then_inc(ro_sqd, 1)
                    hi(b)

            act.wait_ge(mix_done, GH + 1)
            with act.Fori(0, RH - 1) as r:
                ret_a(r, 8 * r + N_GDN_UNITS, 4 * r + N_GDN_UNITS // 2)
                hi = lambda k: split_hi(8 * r + (N_GDN_UNITS + 8), 4 * r + (N_GDN_UNITS // 2 + 4),
                                        1 + k // 4, k % 4)
                ret_b(r, hi)
                for k in range(2, 16):
                    hi(k)
            last = RH - 1
            ret_a(last, 8 * last + N_GDN_UNITS, 4 * last + N_GDN_UNITS // 2)

            def mix_hi(s):
                if s >= GH:
                    act.wait_ge(rmix_done, s - GH + 2)
                A(act_hi[:, s, :], mix[:, s, :], ACT.Copy).then_inc(mhi_ready, 1)

            for s in range(6):
                mix_hi(s)
            hi = lambda k: split_hi(OUT_U, OUT_U // 2, 1 + k // 4, k % 4)
            ret_b(last, hi)
            for s in range(6, 14):
                mix_hi(s)
                hi(s - 4)
            hi(10)
            hi(11)
            mix_hi(14)
            mix_hi(15)
            for k in range(12, 16):
                hi(k)

            def square_h(n, t):
                act.wait_ge(h_ready, 4 * n + (t + 1))
                if not (isinstance(n, int) and n + t == 0):
                    act.wait_ge(h_sq, 4 * n + t)
                A(work1[:, 4, :], h_tok[:, t, bass.ds(n * SEQ, SEQ)], ACT.Square,
                  accum_out=small[:, 0, bass.ds(4 * t + n, 1)]).then_inc(h_sq, 1)

            for t in range(NT):
                square_h(0, t)
            def hi_out(n, k):
                i, p = 1 + k // 4, k % 4
                if p == 0:
                    act.wait_ge(s_w[i % 2], 32 * n + (8 * OUT_U + 16 * (i // 2) + 16))
                    if i == 1:
                        act.wait_ge(oproj_mm, 4 * n)
                    else:
                        act.wait_ge(proj_done, 3 * n + (OUT_U + i - 1))
                at = slice(p * PIECE, (p + 1) * PIECE)
                A(w_hi[:, i % 2, at], w_raw[:, i % 2, at], ACT.Copy).then_inc(hi_ready, 1)

            with act.Fori(1, 3) as n:
                for k in range(16):
                    hi_out(n, k)
                for t in range(NT):
                    square_h(n, t)
            for k in range(12):
                hi_out(3, k)
            for t in range(NT):
                square_h(3, t)
                act.wait_ge(h_rstd, t + 1)
                A(h_tok[:, t, 0:2 * SEQ], h_tok[:, t, 0:2 * SEQ], ACT.Copy,
                  scale=stat[:, 2, t:t + 1]).then_inc(y_left_done, 1)

        @block.vector
        def _(dve):
            TT, TS, STT = dve.tensor_tensor, dve.tensor_scalar, dve.scalar_tensor_tensor
            link = Links(dve, dve_link)
            dve.memset(ones[:, :], 1.0).then_inc(memsets, 1)
            dve.memset(half[:, 0:8], -0.5).then_inc(memsets, 1)
            dve.memset(half[:, 8:16], 0.5).then_inc(memsets, 1)
            dve.memset(stat[:, 0, 14:15], 0.0).then_inc(mix_done, 1)
            dve.memset(stat[:, 0, 15:16], 0.0).then_inc(rmix_done, 1)

            def scale_x(t):
                dve.wait_ge(x_rstd, t + 1)
                TS(x_tok[:, t, :], x_tok[:, t, :], stat[:, 3, t:t + 1], math.sqrt(D), ALU.mult,
                   ALU.mult).then_inc(x_scaled, 1)

            for t in range(NT):
                dve.wait_ge(s_x[t], 16)
                link(dve.tensor_tensor_reduce(work2[:, 2:4, :].rearrange("p a c -> p (a c)"),
                                              x_tok[:, t, D // 2:], x_tok[:, t, D // 2:], 1.0, 0.0,
                                              ALU.mult, ALU.add, stat[:, 1, t:t + 1]))
                dve.wait_ge(x_sq, t + 1)
                TS(stat[:, 2, t:t + 1], stat[:, 0, t:t + 1], stat[:, 1, t:t + 1], D * EPS, ALU.add,
                   ALU.add).then_inc(x_ms, 1)
                if t > 0:
                    scale_x(t - 1)
            scale_x(NT - 1)

            def split_lo(u, i, p):
                dve.wait_ge(hi_ready, 4 * u + (4 * i + p + 1))
                at = slice(p * PIECE, (p + 1) * PIECE)
                TT(w_lo[:, i % 2, at], w_raw[:, i % 2, at], w_hi[:, i % 2, at].bitcast(F32),
                   ALU.subtract).then_inc(lo_ready, 1)

            split_lo(0, 0, 0)
            dve.wait_ge(cols_ready, 1)
            angle, turns, angle_cos = wk(W_ATTN), wk(W_KKEEP), rope_cos[:, :]
            cosine_steps = iter((
                lambda: TS(turns, angle, 1.0 / (2 * math.pi), 0.25, ALU.mult, ALU.add),
                lambda: TS(turns, turns, magic, None, ALU.add),
                lambda: TS(turns, turns, -magic, None, ALU.add),
                lambda: STT(angle_cos, turns, -c1, angle, ALU.mult, ALU.add),
                lambda: STT(angle_cos, turns, -c2, angle_cos, ALU.mult, ALU.add),
                lambda: STT(angle_cos, turns, -c3, angle_cos, ALU.mult, ALU.add),
                lambda: TS(angle_cos, angle_cos, 0.5 * math.pi, 3.1415925, ALU.add, ALU.min)))
            for kt in range(KT):
                dve.wait_ge(xhi_ready, kt + 1)
                STT(act_lo[:, kt, :], bank(2 + kt % 5), cols[:, 96 + kt:97 + kt],
                    act_hi[:, kt, :].bitcast(F32), ALU.mult, ALU.subtract).then_inc(xlo_ready, 1)
                if kt < 3:
                    split_lo(0, 0, kt + 1)
                if kt % 4 == 3:
                    split_lo(0, 1, kt // 4)
                elif kt in (6, 8, 10, 12, 14):
                    if kt == 6:
                        dve.wait_ge(angle_ready, 1)
                    link(next(cosine_steps)())

            def conv_weights(h):
                if not isinstance(h, int):
                    dve.wait_ge(conv_done, 3 * h)
                src = cols[:, 0:96].rearrange("p (t s c) -> p t s c", t=4, s=3)[:, :, :, bass.ds(h, 1)]
                dve.tensor_copy(conv_par[:, :, :].unsqueeze(3), src).then_inc(conv_par_ready, 1)

            def tap(s, j, link):
                back = 3 - j
                op = STT(conv[:, s, back:], bank(s % 2)[:, 0:SEQ - back], conv_par[:, j, s:s + 1],
                         conv[:, s, back:], ALU.mult, ALU.add)
                if j == 2:
                    op.then_inc(conv_done, 1)
                else:
                    link(op)

            wg_raw = work2[:, W_GRAW, 0:KT * 16].rearrange("p (k c) -> p k c", k=KT)
            dve.wait_ge(wg_hi_ready, 1)
            TT(wg_lo[:, :, :], wg_raw, wg_hi[:, :, :].bitcast(F32), ALU.subtract).then_inc(wg_lo_ready, 1)
            for p in range(4):
                split_lo(0, 2, p)
            for step in cosine_steps:
                link(step())
            TS(angle_cos, angle_cos, -3.1415925, None, ALU.max).then_inc(cos_arg, 1)
            conv_weights(0)
            dve.wait_ge(tap_done, 1)
            for j in range(3):
                tap(0, j, link)



            sm = [small[:, i, :].rearrange("p (h t) -> p h t", h=GH) for i in range(6)]
            gates = bank(6)[:, 0:16 * NT].rearrange("p (t c) -> p c t", c=16)
            dve.wait_ge(s_arow, 32)
            dve.wait_ge(p_act, 1)
            TT(sm[1], gates[:, 8:16, :], over_free(dt_row[:, :], NT), ALU.add).then_inc(dt_added, 1)
            link(TS(sm[0], sm[0], 1.0, None, ALU.add))
            link(dve.reciprocal(head_par[:, :, 0:4], sm[0]))
            TS(head_par[:, :, 4:8], head_par[:, :, 0:4], -1.0, None, ALU.mult).then_inc(p_ready, 1)
            dve.wait_ge(p_act, 5)
            link(STT(sm[4], sm[1], 0.0, sm[2], ALU.max, ALU.add))
            STT(g_log[:, :, :], sm[4], -1.0, over_free(a_row[:, :], NT), ALU.mult, ALU.mult).then_inc(p_dve, 1)
            dve.wait_ge(p_mm, 1)
            cum = bank(3)[:, 0:GH * NT].rearrange("p (h t) -> p h t", h=GH)
            tot = bank(3)[:, GH * NT:2 * GH * NT].rearrange("p (h t) -> p h t", h=GH)
            dve.wait_ge(p_act, 7)
            link(dve.tensor_copy(g_cum[:, :, :], cum))
            link(TT(sm[5], tot, g_cum[:, :, :], ALU.subtract))
            TS(sm[3], sm[5], 0.0, None, ALU.min).then_inc(p_dve, 1)


            def decay_in(e):
                if e >= 2:
                    dve.wait_ge(g_mm, e - 1)
                TT(tiles(ys[e % 2]), over_tiles(causal), over_free(g_log[:, e, :]),
                   ALU.mult).then_inc(ug_ready, 1)

            decay_in(0)
            for e in range(GH):
                if e + 1 < GH:
                    decay_in(e + 1)
                dve.wait_ge(g_mm, e + 1)
                if e >= 2:
                    dve.wait_ge(decay_ready, e - 1)
                dif = wk(W_X + e % 2)
                link(TT(tiles(dif), tiles(bank(4 + e % 2)), over_free(g_cum[:, e, :]), ALU.subtract))
                TS(dif, dif, 0.0, None, ALU.min).then_inc(dif_ready, 1)
                split_lo(0, 3 + e // 4, e % 4)
                if e in (1, 5):
                    s = 1 + e // 4
                    dve.wait_ge(tap_done, s + 1)
                    for j in range(3):
                        tap(s, j, link)

            dve.wait_ge(p_ready, 2)
            dve.wait_ge(rope_ready, 2)

            def rot(r, i, first_wait):
                dst = (q_rot, k_rot)[i // 2]
                if i == 0:
                    first_wait()
                dve.wait_ge(proj_done, 8 * r + (N_GDN_UNITS + 1 + i))
                if i % 2 == 0:
                    a, b = dst[:, 0, :], dst[:, 1, :]
                else:
                    if i == 3:
                        dve.wait_ge(rot_done, 4 * r + 2)
                    elif not isinstance(r, int):
                        dve.wait_ge(rot_done, 4 * r)
                    a, b = rot_tmp[:, 1, :], rot_tmp[:, 0, :]
                TT(a, bank(i % 2), rope_cos[:, :], ALU.mult)
                TT(b, bank(i % 2), rope_sin[:, :], ALU.mult).then_inc(rot_read, 1)

            def gdn_body(h, unit0, following):
                glink = Links(dve, dve_link_gdn, DVE_GDN_LINKS * h)
                lo = lambda k: split_lo(unit0, 1 + k // 4, k % 4)
                dve.wait_ge(mix_done, h + 1)
                dve.tensor_copy(par[:, :].unsqueeze(1), head_par[:, bass.ds(h, 1), :]).then_inc(par_ready, 1)
                if following == "gdn":
                    conv_weights(h + 1)
                eg = par[:, 8:12]
                lo(0)
                for s in (1, 0):
                    dve.wait_ge(qk_sq, 2 * h + 2) if s == 1 else None
                    glink(dve.tensor_reduce(stat[:, 0, 4 * s:4 * s + 4], tiles(ys[s]), AX.X, ALU.add))
                TS(k_norm2, stat[:, 0, 4:8], P * EPS, None, ALU.add).then_inc(ss_ready, 1)
                TS(q_eps, stat[:, 0, 0:4], P * EPS, EPS * P, ALU.add, ALU.mult)
                dve.wait_ge(ss_ready, h + 1)
                glink(dve.reciprocal(stat[:, 3, 0:4], k_norm2))
                dve.wait_ge(par_ready, h + 1)
                glink(TT(beta_both.rearrange("p (a t) -> p a t", a=2),
                         par[:, 0:8].rearrange("p (a t) -> p a t", a=2),
                         stat[:, 3, 0:4].unsqueeze(1).to_broadcast([P, 2, NT]), ALU.mult))
                lo(1)
                decay = mix[:, bass.ds(h, 1), :].rearrange("p a (t c) -> p (a t) c", t=NT)
                dve.wait_ge(decay_ready, GH)
                dve.wait_ge(kk_mm, 2 * h + 1)
                for t in range(NT):
                    op = STT(tiles(lower_t)[:, t, :], tiles(bank(5))[:, t, :], beta_k[:, t:t + 1],
                             decay[:, t, :], ALU.mult, ALU.mult)
                    op.then_inc(low_ready, 1) if t == NT - 1 else None
                dve.wait_ge(kk_mm, 2 * h + 2)
                TT(tiles(attn_t), tiles(bank(6)), decay, ALU.mult).then_inc(low_ready, 1)
                dve.wait_ge(r_ready, h + 1)
                dve.wait_ge(tr_in, 3 * h + 3)
                TT(tiles(vtok), tiles(bank(4)), over_free(k_norm), ALU.mult).then_inc(v_ready, 1)
                lo(2)
                def turn(dst, src, src_is_full=False):
                    for q in range(P // BLK):
                        part = slice(q * BLK, (q + 1) * BLK)
                        if src_is_full:
                            op = dve.transpose(dst[part, :, :], on_diag(src, q))
                        else:
                            op = dve.transpose(on_diag(dst, q), src[part, :, :])
                    return op

                def product(m, first, last):
                    n = NT * BLK * (3, 3, 2, 2, 1)[m]
                    dst = bank(4 + m % 2)[:, 0:n].rearrange("p (t c) -> p t c", t=NT)
                    return dst[:, :, first * BLK:(last + 1) * BLK]

                dve.wait_ge(y_ready, 4 * h + 1)
                glink(turn(pow_d, ys[0], True))
                TT(inv_d, pow_d, ident_d.unsqueeze(1).to_broadcast([P, NT, BLK]), ALU.add)
                dve.wait_ge(y_ready, 4 * h + 2)
                turn(off_d, ys[1], True).then_inc(blk_ready, 1)
                lo(3)
                for m in range(5):
                    dve.wait_ge(blk_mm, 5 * h + (m + 1))
                    if m == 0:
                        TT(off_d, off_d, product(m, 2, 2), ALU.add)
                    elif m == 1:
                        TT(inv_off_d, inv_off_d, product(m, 1, 2), ALU.add)
                    elif m == 2:
                        op = TT(inv_off_d, inv_off_d, product(m, 0, 1), ALU.add)
                    else:
                        op = TT(inv_d, inv_d, product(m, 0, 0), ALU.add)
                    if m in (0, 1, 3):
                        op = dve.tensor_copy(pow_d, product(m, m // 3, m // 3))
                    glink(op)
                    if m < 4:
                        turn(ys[0], off_d if m == 2 else pow_d).then_inc(blk_ready, 1)
                        lo(4 + m)
                    if following == "gdn" and 1 <= m <= 3:
                        dve.wait_ge(tap_done, 3 * h + 4) if m == 1 else None
                        tap(0, m - 1, glink)
                    if following == "ret" and m == 1:
                        rot(0, 0, lambda: dve.wait_ge(kq_kept, 2 * GH))
                glink(TT(inv.rearrange("p (t b c) -> p t b c", t=NT, c=BLK),
                         inv_d.unsqueeze(2).to_broadcast([P, NT, P // BLK, BLK]),
                         diag_mask.rearrange("p (b c) -> p b c", c=BLK).unsqueeze(1).to_broadcast(
                             [P, NT, P // BLK, BLK]), ALU.mult))
                dve.transpose(inv_t, inv).then_inc(lvl_ready, 1)
                for n in range(2):
                    dve.wait_ge(lvl_mm, 3 * h + (2 * n + 1))
                    if n == 0:
                        TT(inv, inv, bank(5), ALU.add).then_inc(lvl_ready, 1)
                        dve.wait_ge(lvl_mm, 3 * h + 2)
                    TT(inv_t, inv_t, bank(6), ALU.add).then_inc(lvl_ready, 1)
                    lo(8 + n)

                def sum_o(t):
                    dve.wait_ge(o_mm, 4 * h + (t + 1))
                    dst = o_raw[:, t * P:(t + 1) * P]
                    if t == 0:
                        dve.tensor_copy(dst, within(t)).then_inc(o_summed, 1)
                    else:
                        dve.wait_ge(o_part, 3 * h + t)
                        TT(dst, dst, within(t), ALU.add).then_inc(o_summed, 1)

                for t in range(NT):
                    tt = slice(t * P, (t + 1) * P)
                    if t > 0:
                        dve.wait_ge(ks_mm, 3 * h + t)
                        STT(vtok[:, tt], bank(4)[:, tt], eg[:, t:t + 1], vtok[:, tt], ALU.mult,
                            ALU.subtract).then_inc(rest_ready, 1)
                    dve.wait_ge(xr_mm, 4 * h + (t + 1))
                    TS(vnew[:, tt], bank(4)[:, tt], (nbeta_k if t else beta_k)[:, t:t + 1], None,
                       ALU.mult).then_inc(vn_ready, 1)
                    if t > 0:
                        dve.wait_ge(qs_mm, 3 * h + t)
                        TS(o_raw[:, tt], from_state(t), eg[:, t:t + 1], None, ALU.mult).then_inc(o_part, 1)
                        sum_o(t - 1)
                    if t == 0 and following == "gdn":
                        dve.wait_ge(tap_done, 3 * h + 5)
                        tap(1, 0, glink)
                    if t < NT - 1:
                        dve.wait_ge(ktv_mm, 3 * h + (t + 1))
                        if t == 0:
                            dve.tensor_copy(state[0], bank(5)[:, tt]).then_inc(st_ready, 1)
                        else:
                            dve.wait_ge(st_ready, 3 * h + t)
                            STT(state[t], state[t - 1], par[:, 16 + t:17 + t], bank(5)[:, tt], ALU.mult,
                                ALU.add).then_inc(st_ready, 1)
                    if t < 2 and following == "gdn":
                        tap(1, t + 1, glink)
                    if t == 0 and following == "ret":
                        rot(0, 1, None)
                    if t == 0:
                        lo(10)
                    if t == 1:
                        lo(11)
                    if t >= 2 and following == "gdn":
                        if t == 2:
                            dve.wait_ge(tap_done, 3 * h + 6)
                        tap(2, t - 2, glink)
                    if t == 3 and following == "ret":
                        rot(0, 2, None)
                    if t == 3:
                        sum_o(3)
                        lo(12)
                dve.wait_ge(o_sq, h + 1)
                glink(dve.tensor_reduce(stat[:, 0, 8:12], tiles(ys[0]), AX.X, ALU.add))
                STT(stat[:, 1, 8:12], stat[:, 0, 8:12], 1.0 / P, q_eps, ALU.mult, ALU.add).then_inc(o_ms, 1)
                if following == "gdn":
                    tap(2, 2, glink)
                lo(13)
                dve.wait_ge(o_rstd, h + 1)
                TT(tiles(o_n), tiles(o_raw), over_free(stat[:, 2, 8:12]), ALU.mult).then_inc(on_ready, 1)
                lo(14)
                lo(15)
                dve.wait_ge(otr_mm, h + 1)
                STT(mix[:, bass.ds(h, 1), :].rearrange("p a c -> p (a c)"), bank(6), cols[:, 112:113], gate,
                    ALU.mult, ALU.mult).then_inc(mix_done, 1)
                return glink.n

            with dve.Fori(0, GH - 1) as h:
                used = gdn_body(h, 4 * h + 4, "gdn")
            assert used == DVE_GDN_LINKS, used
            gdn_body(GH - 1, N_GDN_UNITS, "ret")

            def ret_a(r, unit0):
                lo = lambda k: split_lo(unit0, 5 + k // 4, k % 4)
                rot(r, 3, None)
                for k in range(16):
                    lo(k)
                    if k in (1, 3, 5, 7):
                        j = k // 2
                        n = SEQ - j * P
                        dve.wait_ge(rs_mm, 4 * r + (j + 1))
                        if j == 0:
                            dve.wait_ge(s_dec, 16 * RH)
                        table = mix[:, bass.ds(2 * r + GH, 1), 0:n].rearrange("p a c -> p (a c)")
                        TT(s_all[:, s_off[j]:s_off[j] + n], bank(4 + j)[:, 0:n], table,
                           ALU.mult).then_inc(rs_ready, 1)

            def ret_b(r, lo):
                rlink = Links(dve, dve_link_ret, DVE_RET_LINKS * r)
                sq = ro_sq.rearrange("p a c -> p (a c)").rearrange("p (j d) -> p j d", j=NT)
                for b in range(2):
                    dve.wait_ge(ro_sqd, 2 * r + (b + 1))
                    rlink(dve.tensor_reduce(stat[:, 0, 2 * b:2 * b + 2], sq[:, 2 * b:2 * b + 2, :], AX.X,
                                            ALU.add))
                    lo(b)
                TS(stat[:, 1, 0:4], stat[:, 0, 0:4], 1.0 / RDK, EPS, ALU.mult, ALU.add).then_inc(ro_ms, 1)
                lo(2)
                dve.wait_ge(ro_rstd, r + 1)
                for b in range(2):
                    TT(ro_n[:, 2 * b:2 * b + 2, :], bank(6 + b).rearrange("p (j d) -> p j d", j=2),
                       over_free(stat[:, 2, 2 * b:2 * b + 2], RDK), ALU.mult).then_inc(ron_ready, 1)
                lo(3)
                for d in range(2):
                    dve.wait_ge(rotr_mm, 2 * r + (d + 1))
                    dve.wait_ge(rgate_done, 2 * r + (d + 1))
                    TT(mix[:, bass.ds(2 * r + (GH + d), 1), :].rearrange("p a c -> p (a c)"), bank(4 + d),
                       rgate[:, d, :], ALU.mult).then_inc(rmix_done, 1)
                assert rlink.n == DVE_RET_LINKS

            with dve.Fori(0, RH - 1) as r:
                ret_a(r, 8 * r + N_GDN_UNITS)
                lo = lambda k: split_lo(8 * r + (N_GDN_UNITS + 8), 1 + k // 4, k % 4)
                ret_b(r, lo)
                for i in range(3):
                    for k in range(4):
                        lo(4 + 4 * i + k)
                    rot(r + 1, i, lambda: dve.wait_ge(rs_mm, 4 * r + 4))
            last = RH - 1
            ret_a(last, 8 * last + N_GDN_UNITS)

            def mix_lo(s):
                dve.wait_ge(mhi_ready, s + 1)
                if s == 0:
                    dve.wait_ge(proj_done, OUT_U)
                TT(act_lo[:, s, :], mix[:, s, :], act_hi[:, s, :].bitcast(F32),
                   ALU.subtract).then_inc(mlo_ready, 1)

            for s in range(6):
                mix_lo(s)
            lo = lambda k: split_lo(OUT_U, 1 + k // 4, k % 4)
            ret_b(last, lo)
            for s in range(6, 14):
                mix_lo(s)
                lo(s - 2)
            mix_lo(14)
            mix_lo(15)
            for k in range(12, 16):
                lo(k)

            def add_x(n, t):
                dve.wait_ge(oproj_mm, 4 * n + (t + 1))
                at = h_tok[:, t, bass.ds(n * SEQ, SEQ)]
                TT(at, at, bank(t), ALU.add).then_inc(h_ready, 1)

            def weigh_h(n):
                for t in range(NT):
                    dve.wait_ge(h_sq, 4 * n + (t + 1))
                    at = h_tok[:, t, bass.ds(n * SEQ, SEQ)]
                    TT(at, at, fin_w[:, bass.ds(n * SEQ, SEQ)], ALU.mult).then_inc(h_weighed, 1)

            dve.wait_ge(s_xres[0], 16)
            for t in range(NT):
                add_x(0, t)
            dve.wait_ge(s_fin, 16)
            weigh_h(0)
            for n in range(1, 4):
                dve.wait_ge(s_xres[n], 16)
            with dve.Fori(1, 3) as n:
                for k in range(16):
                    split_lo(4 * n + OUT_U, 1 + k // 4, k % 4)
                for t in range(NT):
                    add_x(n, t)
                weigh_h(n)
            for k in range(12):
                split_lo(OUT_U + 12, 1 + k // 4, k % 4)
            for t in range(NT):
                add_x(3, t)
                dve.wait_ge(h_sq, 12 + t + 1)
                link(dve.tensor_reduce(stat[:, 0, t:t + 1], small[:, 0, 4 * t:4 * t + 4], AX.X, ALU.add))
                TS(stat[:, 1, t:t + 1], stat[:, 0, t:t + 1], 1.0 / D, EPS, ALU.mult, ALU.add).then_inc(h_ms, 1)
                dve.wait_ge(h_rstd, t + 1)
                at = slice(3 * SEQ, 4 * SEQ)
                STT(h_tok[:, t, at], h_tok[:, t, at], stat[:, 2, t:t + 1], fin_w[:, at], ALU.mult, ALU.mult)
                at = slice(2 * SEQ, 3 * SEQ)
                dve.wait_ge(h_weighed, 3 * NT)
                TS(h_tok[:, t, at], h_tok[:, t, at], stat[:, 2, t:t + 1], None, ALU.mult).then_inc(y_done, 1)

        @block.gpsimd
        def _(pool):
            TT = pool.tensor_tensor
            for t in range(NT):
                pool.wait_ge(x_ms, t + 1)
                if t == 0:
                    pool.wait_ge(memsets, 3)
                TT(stat[:, 3, t:t + 1], stat[:, 2, t:t + 1], half[:, 0:1], ALU.pow).then_inc(x_rstd, 1)
            pool_then = Links(pool, pool_link)
            pos_f, turns, angle, whole = wk(W_KTOK), wk(W_LOWER), wk(W_ATTN), wk(W_VTOK)
            TS = pool.tensor_scalar
            pool.wait_ge(s_cst, 16)
            pool.wait_ge(s_pos, 16)
            pool_then(pool.tensor_copy(pos_f, work2[:, W_GATE, :].bitcast(I32)))
            TS(angle, pos_f, inv_freq, None, ALU.mult).then_inc(angle_ready, 1)
            pool.wait_ge(angle_ready, 1)
            angle_sin = rope_sin[:, :]
            pool_then(TS(turns, angle, 1.0 / (2 * math.pi), None, ALU.mult))
            pool_then(TS(turns, turns, magic, None, ALU.add))
            pool_then(TS(turns, turns, -magic, None, ALU.add))
            for part, rest in ((c1, angle), (c2, angle_sin), (c3, angle_sin)):
                pool_then(TS(whole, turns, part, None, ALU.mult))
                pool_then(TT(angle_sin, rest, whole, ALU.subtract))
            TS(angle_sin, angle_sin, -3.1415925, 3.1415925, ALU.max, ALU.min).then_inc(rope_arg, 1)

            pool.wait_ge(xt_mm, KT)
            for e in range(GH):
                pool.wait_ge(dif_exp, e + 1)
                TT(tiles(mix[:, e, :]), tiles(wk(W_X + e % 2)), over_tiles(causal),
                   ALU.mult).then_inc(decay_ready, 1)

            def rot_sum(r, i):
                dst = (q_rot, k_rot)[i]
                pool.wait_ge(rot_read, 4 * r + (2 * i + 2))
                TT(dst[:, 0, :], dst[:, 0, :], rot_tmp[:, 0, :], ALU.subtract).then_inc(rot_done, 1)
                TT(dst[:, 1, :], dst[:, 1, :], rot_tmp[:, 1, :], ALU.add).then_inc(rot_done, 1)

            def gdn_body(h, following):
                pool.wait_ge(ss_ready, h + 1)
                TT(k_norm, k_norm2, half[:, 8:12], ALU.pow).then_inc(r_ready, 1)
                pool.wait_ge(k_tok_ready, h + 1)
                pool.wait_ge(par_ready, h + 1)
                pool.wait_ge(low_ready, 2 * h + 1)
                for n in range(2):
                    TT(tiles(ys[n]), tiles(lower_t), over_tiles(level_mask(n)), ALU.mult).then_inc(y_ready, 1)
                TT(tiles(ktail), tiles(ktok), over_free(par[:, 12:16]), ALU.mult).then_inc(ktail_ready, 1)
                for n in range(2):
                    if n == 0:
                        pool.wait_ge(blk_ready, 5 * h + 1)
                    else:
                        pool.wait_ge(blk_mm, 5 * h + 5)
                    TT(tiles(ys[1 - n]), tiles(lower_t), over_tiles(level_mask(2 + n)),
                       ALU.mult).then_inc(y_ready, 1)
                if following == "ret":
                    rot_sum(0, 0)
                pool.wait_ge(o_ms, h + 1)
                TT(stat[:, 2, 8:12], stat[:, 1, 8:12], half[:, 0:4], ALU.pow).then_inc(o_rstd, 1)

            with pool.Fori(0, GH - 1) as h:
                gdn_body(h, "gdn")
            gdn_body(GH - 1, "ret")

            def ret_norm(r):
                pool.wait_ge(ro_ms, r + 1)
                TT(stat[:, 2, 0:4], stat[:, 1, 0:4], half[:, 0:4], ALU.pow).then_inc(ro_rstd, 1)

            with pool.Fori(0, RH - 1) as r:
                rot_sum(r, 1)
                ret_norm(r)
                rot_sum(r + 1, 0)
            rot_sum(RH - 1, 1)
            ret_norm(RH - 1)
            for t in range(NT):
                pool.wait_ge(h_ms, t + 1)
                TT(stat[:, 2, t:t + 1], stat[:, 1, t:t + 1], half[:, 0:1], ALU.pow).then_inc(h_rstd, 1)


def shape_constants():
    j, i = np.arange(P)[:, None], np.arange(P)[None, :]
    parts = [np.eye(P), (i >= j)]
    bounds = (1, SMALL, BLK, 2 * BLK, P)
    for low, high in zip(bounds[:-1], bounds[1:]):
        parts.append(-1.0 * ((i // low > j // low) & (i // high == j // high)))
    parts.append(i // BLK == j // BLK)
    parts.append(np.arange(BLK)[None, :] == j % BLK)
    freq = 1.0 / (np.float32(10000.0) ** (np.arange(0, RDK, 2, dtype=np.float32) / np.float32(RDK)))
    parts.append(freq[:, None])
    consts = np.concatenate([p.astype(np.float32) for p in parts], axis=1)
    gamma = 1.0 - 2.0 ** (-5.0 - np.arange(RH))
    rel = np.arange(SEQ)[None, :] - np.arange(P)[:, None]
    decays = np.where(rel >= 0, gamma[:, None, None] ** np.maximum(rel, 0), 0.0) * RDK ** -0.5
    return consts, decays.astype(np.float32)


def kernel(**inputs):
    import concourse.bacc as bacc
    from concourse.bass_utils import run_bass_kernel_spmd

    consts, decays = shape_constants()
    given = {name: np.asarray(a) for name, a in inputs.items()}
    arrays = {
        "x": given["x"][0], "positions": given["positions"][0], "norm_w": given["norm_w"][0],
        "w_in": given["w_in"][0], "conv_w": given["conv_w"][0], "a_log": given["a_log"][0],
        "dt_bias": given["dt_bias"][0], "gdn_norm_w": given["gdn_norm_w"][0],
        "w_out": given["w_out"][0], "final_norm_w": given["final_norm_w"],
        "consts": consts, "decays": decays,
    }
    arrays = {f"in_{name}": np.ascontiguousarray(a) for name, a in arrays.items()}
    nc = bacc.Bacc("TRN2", target_bir_lowering=False, num_devices=1)
    aps = [nc.dram_tensor(name, a.shape, mybir.dt.from_np(a.dtype), kind="ExternalInput").ap()
           for name, a in arrays.items()]
    y = nc.dram_tensor("y", (SEQ, D), F32, kind="ExternalOutput").ap()
    build(nc, *aps, y)
    result = run_bass_kernel_spmd(nc, [arrays], core_ids=[0])
    return result.results[0]["y"].reshape(1, SEQ, D)
```
